# Optimizing a Trainium2 kernel written in Bass

```python
import math
import jax
import jax.numpy as jnp
from jax import lax
import numpy as np

D_MODEL = 1024
BATCH = 1
SEQ = 256
DEPTH = 2

GRID_W = 64
CTX_LEN = 256
N_MIXERS = 3
N_LAYERS_A = (DEPTH + 2) // N_MIXERS
N_LAYERS_B = (DEPTH + 1) // N_MIXERS
N_LAYERS_C = DEPTH // N_MIXERS
N_MOD = 6
HEAD_DIM = 64
N_HEADS = D_MODEL // (2 * HEAD_DIM)
V_HEAD_DIM = 2 * HEAD_DIM
Q_BLOCK = 128
ROPE_THETA = 10000.0
D_FF = 4 * D_MODEL
HYENA_EMB_DIM = 33
HYENA_FILTER_ORDER = 64
HYENA_SHORT_WIDTH = 3
HYENA_DECAY_TARGET = 1e-2
HYENA_FAST_DECAY_PCT = 0.3
HYENA_SLOW_DECAY_PCT = 1.5
CONV_WIDTH = 31
NORM_EPS = 1e-6
LN_EPS = 1e-5


def rms_norm(x, g, eps=NORM_EPS):
    xf = x.astype(jnp.float32)
    y = xf * lax.rsqrt(jnp.mean(xf * xf, axis=-1, keepdims=True) + eps)
    return (y * g.astype(jnp.float32)).astype(x.dtype)

def layer_norm(x, g, b, eps=LN_EPS):
    xf = x.astype(jnp.float32)
    mu = jnp.mean(xf, axis=-1, keepdims=True)
    var = jnp.mean(jnp.square(xf - mu), axis=-1, keepdims=True)
    y = (xf - mu) * lax.rsqrt(var + eps)
    return (y * g.astype(jnp.float32) + b.astype(jnp.float32)).astype(x.dtype)

def modulate(x, shift, scale):
    return x * (1.0 + scale) + shift

def depthwise_conv(x, w, b):
    y = lax.conv_general_dilated(
        x, w[:, None, :].astype(x.dtype), window_strides=(1,), padding="SAME",
        dimension_numbers=("NWC", "WIO", "NWC"), feature_group_count=x.shape[-1])
    return y + b

def grid_positions(n_tokens):
    rows = n_tokens // GRID_W
    row_ids = jnp.repeat(jnp.arange(rows, dtype=jnp.float32), GRID_W)
    col_ids = jnp.tile(jnp.arange(GRID_W, dtype=jnp.float32), rows)
    return row_ids, col_ids

def rope_1d(x, pos):
    half = x.shape[-1] // 2
    inv_freq = ROPE_THETA ** (-jnp.arange(half, dtype=jnp.float32) / half)
    ang = pos[:, None] * inv_freq[None, :]
    cos = jnp.cos(ang)[None, :, None, :]
    sin = jnp.sin(ang)[None, :, None, :]
    x1 = x[..., :half].astype(jnp.float32)
    x2 = x[..., half:].astype(jnp.float32)
    return jnp.concatenate([x1 * cos - x2 * sin, x2 * cos + x1 * sin], axis=-1).astype(x.dtype)

def rope_2d(x, rows, cols):
    rd = x.shape[-1] // 2
    return jnp.concatenate([rope_1d(x[..., :rd], rows), rope_1d(x[..., rd:], cols)], axis=-1)

def diff_attend(q, k, v, lam):
    s = jnp.einsum("bqhpd,bkhpd->bhpqk", q, k).astype(jnp.float32) * (HEAD_DIM ** -0.5)
    p = jax.nn.softmax(s, axis=-1)
    a = p[:, :, 0] - lam * p[:, :, 1]
    return jnp.einsum("bhqk,bkhe->bqhe", a.astype(v.dtype), v)

def differential_attention(u_lat, u_ctx, w_qkv, w_out, lam_vec, subln_g, lam_init, with_ctx):
    bsz, n_lat, _ = u_lat.shape

    def project(u):
        n = u.shape[1]
        q, k, v = jnp.split(u @ w_qkv, 3, axis=-1)
        return (q.reshape(bsz, n, N_HEADS, 2, HEAD_DIM),
                k.reshape(bsz, n, N_HEADS, 2, HEAD_DIM),
                v.reshape(bsz, n, N_HEADS, V_HEAD_DIM))

    q_l, k_l, v_l = project(u_lat)
    q_c, k_c, v_c = project(u_ctx)
    rows, cols = grid_positions(n_lat)
    q_l = rope_2d(q_l.reshape(bsz, n_lat, 2 * N_HEADS, HEAD_DIM), rows, cols).reshape(q_l.shape)
    k_l = rope_2d(k_l.reshape(bsz, n_lat, 2 * N_HEADS, HEAD_DIM), rows, cols).reshape(k_l.shape)
    lf = lam_vec.astype(jnp.float32)
    lam = jnp.exp(jnp.sum(lf[0] * lf[1])) - jnp.exp(jnp.sum(lf[2] * lf[3])) + lam_init
    k_all = jnp.concatenate([k_c, k_l], axis=1)
    v_all = jnp.concatenate([v_c, v_l], axis=1)
    n_blk = n_lat // Q_BLOCK
    q_blocks = jnp.moveaxis(q_l.reshape(bsz, n_blk, Q_BLOCK, N_HEADS, 2, HEAD_DIM), 1, 0)
    o_l = lax.map(lambda qb: diff_attend(qb, k_all, v_all, lam), q_blocks)
    o_l = jnp.moveaxis(o_l, 0, 1).reshape(bsz, n_lat, N_HEADS, V_HEAD_DIM)

    def merge_heads(o):
        o = rms_norm(o, subln_g) * (1.0 - lam_init)
        return o.reshape(bsz, o.shape[1], D_MODEL) @ w_out

    y_l = merge_heads(o_l)
    y_c = merge_heads(diff_attend(q_c, k_c, v_c, lam)) if with_ctx else None
    return y_l, y_c

def hyena_filters(n, w1, b1, w2, b2, freq, w_out):
    bands = (HYENA_EMB_DIM - 1) // 2
    t = jnp.linspace(0.0, 1.0, n, dtype=jnp.float32)[:, None]
    w = 2.0 * math.pi * jnp.arange(n, dtype=jnp.float32)[:, None] / n
    f = jnp.linspace(1e-4, bands - 1, bands, dtype=jnp.float32)[None, :]
    z = jnp.concatenate([t, jnp.cos(f * w), -jnp.sin(f * w)], axis=-1)
    hdn = jnp.sin(freq * (z @ w1 + b1))
    for j in range(w2.shape[0]):
        hdn = jnp.sin(freq * (hdn @ w2[j] + b2[j]))
    h = (hdn @ w_out).reshape(n, 2, D_MODEL)
    deltas = jnp.abs(jnp.linspace(math.log(HYENA_DECAY_TARGET) / HYENA_SLOW_DECAY_PCT,
                                  math.log(HYENA_DECAY_TARGET) / HYENA_FAST_DECAY_PCT,
                                  D_MODEL, dtype=jnp.float32))
    h = h * jnp.exp(-t * deltas[None, :])[:, None, :]
    return h[:, 0], h[:, 1]

def two_sided_fft_conv(v, h_fwd, h_bwd):
    n = v.shape[1]
    kern = jnp.concatenate([h_fwd, jnp.zeros((1, h_fwd.shape[1]), h_fwd.dtype), h_bwd[:0:-1]], axis=0)
    vf = jnp.fft.rfft(v.astype(jnp.float32), n=2 * n, axis=1)
    kf = jnp.fft.rfft(kern.astype(jnp.float32), n=2 * n, axis=0)
    y = jnp.fft.irfft(vf * kf[None], n=2 * n, axis=1)[:, :n]
    return y.astype(v.dtype)

def hyena_mixer(u, w_in, b_in, w_short, b_short, fw1, fb1, fw2, fb2, ffreq, fw_out, d_bias, w_out, b_out):
    z = depthwise_conv(u @ w_in + b_in, w_short, b_short)
    x0, x1, v = jnp.split(z, 3, axis=-1)
    h_fwd, h_bwd = hyena_filters(u.shape[1], fw1, fb1, fw2, fb2, ffreq, fw_out)
    v = v * x1
    v = two_sided_fft_conv(v, h_fwd, h_bwd) + v * d_bias
    return (v * x0) @ w_out + b_out

def conformer_conv(u, w_pw1, b_pw1, w_dw, b_dw, ln_g, ln_b, w_pw2, b_pw2):
    a, g = jnp.split(u @ w_pw1 + b_pw1, 2, axis=-1)
    z = depthwise_conv(a * jax.nn.sigmoid(g), w_dw, b_dw)
    z = jax.nn.silu(layer_norm(z, ln_g, ln_b))
    return z @ w_pw2 + b_pw2

def squared_relu_mlp(u, w_in, w_out):
    return jnp.square(jax.nn.relu(u @ w_in)) @ w_out

def first_inputs(seed: int = 0) -> dict:
    key = jax.random.key(seed)
    ks = iter(jax.random.split(key, 48))
    D = D_MODEL

    def nrm(shape, scale):
        return scale * jax.random.normal(next(ks), shape, jnp.float32)

    return {
        "x": nrm((BATCH, SEQ, D), 1.0),
        "c": nrm((BATCH, D), 1.0),
        "ctx": nrm((BATCH, CTX_LEN, D), 1.0),
        "c_ctx": nrm((D,), 1.0),
        "w_mod": nrm((DEPTH, D, N_MOD * D), 0.5 * D ** -0.5),
        "b_mod": nrm((DEPTH, N_MOD * D), 0.02),
        "norm_mix_pre": 1.0 + nrm((DEPTH, D), 0.05),
        "norm_mix_post": 1.0 + nrm((DEPTH, D), 0.05),
        "norm_mlp_pre": 1.0 + nrm((DEPTH, D), 0.05),
        "norm_mlp_post": 1.0 + nrm((DEPTH, D), 0.05),
        "w_mlp_in": nrm((DEPTH, D, D_FF), D ** -0.5),
        "w_mlp_out": nrm((DEPTH, D_FF, D), D_FF ** -0.5),
        "attn_w_qkv": nrm((N_LAYERS_A, D, 3 * D), D ** -0.5),
        "attn_w_out": nrm((N_LAYERS_A, D, D), D ** -0.5),
        "attn_lambda": nrm((N_LAYERS_A, 4, HEAD_DIM), 0.1),
        "attn_subln": 1.0 + nrm((N_LAYERS_A, V_HEAD_DIM), 0.05),
        "hy_w_in": nrm((N_LAYERS_B, D, 3 * D), D ** -0.5),
        "hy_b_in": nrm((N_LAYERS_B, 3 * D), 0.02),
        "hy_w_short": nrm((N_LAYERS_B, HYENA_SHORT_WIDTH, 3 * D), HYENA_SHORT_WIDTH ** -0.5),
        "hy_b_short": nrm((N_LAYERS_B, 3 * D), 0.02),
        "hy_filt_w1": nrm((N_LAYERS_B, HYENA_EMB_DIM, HYENA_FILTER_ORDER), HYENA_EMB_DIM ** -0.5),
        "hy_filt_b1": nrm((N_LAYERS_B, HYENA_FILTER_ORDER), 0.1),
        "hy_filt_w2": nrm((N_LAYERS_B, 2, HYENA_FILTER_ORDER, HYENA_FILTER_ORDER), HYENA_FILTER_ORDER ** -0.5),
        "hy_filt_b2": nrm((N_LAYERS_B, 2, HYENA_FILTER_ORDER), 0.1),
        "hy_filt_freq": 1.0 + nrm((N_LAYERS_B, HYENA_FILTER_ORDER), 0.05),
        "hy_filt_w_out": nrm((N_LAYERS_B, HYENA_FILTER_ORDER, 2 * D), HYENA_FILTER_ORDER ** -0.5),
        "hy_bias": nrm((N_LAYERS_B, D), 1.0),
        "hy_w_out": nrm((N_LAYERS_B, D, D), D ** -0.5),
        "hy_b_out": nrm((N_LAYERS_B, D), 0.02),
        "cv_w_pw1": nrm((N_LAYERS_C, D, 2 * D), D ** -0.5),
        "cv_b_pw1": nrm((N_LAYERS_C, 2 * D), 0.02),
        "cv_w_dw": nrm((N_LAYERS_C, CONV_WIDTH, D), CONV_WIDTH ** -0.5),
        "cv_b_dw": nrm((N_LAYERS_C, D), 0.02),
        "cv_ln_g": 1.0 + nrm((N_LAYERS_C, D), 0.05),
        "cv_ln_b": nrm((N_LAYERS_C, D), 0.02),
        "cv_w_pw2": nrm((N_LAYERS_C, D, D), D ** -0.5),
        "cv_b_pw2": nrm((N_LAYERS_C, D), 0.02),
    }

def first_block(x, c, ctx, c_ctx, w_mod, b_mod, norm_mix_pre, norm_mix_post, norm_mlp_pre, norm_mlp_post,
              w_mlp_in, w_mlp_out, attn_w_qkv, attn_w_out, attn_lambda, attn_subln,
              hy_w_in, hy_b_in, hy_w_short, hy_b_short, hy_filt_w1, hy_filt_b1, hy_filt_w2, hy_filt_b2,
              hy_filt_freq, hy_filt_w_out, hy_bias, hy_w_out, hy_b_out,
              cv_w_pw1, cv_b_pw1, cv_w_dw, cv_b_dw, cv_ln_g, cv_ln_b, cv_w_pw2, cv_b_pw2):
    h_lat, h_ctx = x, ctx
    silu_c = jax.nn.silu(c)
    silu_cc = jax.nn.silu(c_ctx)
    for i in range(DEPTH):
        last = i == DEPTH - 1
        kind, j = i % N_MIXERS, i // N_MIXERS
        need_ctx_out = not last
        need_ctx_in = need_ctx_out or kind == 0
        mod_l = jnp.split((silu_c @ w_mod[i] + b_mod[i])[:, None, :], N_MOD, axis=-1)
        mod_c = jnp.split(silu_cc @ w_mod[i] + b_mod[i], N_MOD, axis=-1)
        u_l = modulate(rms_norm(h_lat, norm_mix_pre[i]), mod_l[0], mod_l[1])
        u_c = modulate(rms_norm(h_ctx, norm_mix_pre[i]), mod_c[0], mod_c[1]) if need_ctx_in else None
        if kind == 0:
            y_l, y_c = differential_attention(u_l, u_c, attn_w_qkv[j], attn_w_out[j], attn_lambda[j],
                                              attn_subln[j], 0.8 - 0.6 * math.exp(-0.3 * i), need_ctx_out)
        elif kind == 1:
            hp = (hy_w_in[j], hy_b_in[j], hy_w_short[j], hy_b_short[j], hy_filt_w1[j], hy_filt_b1[j],
                  hy_filt_w2[j], hy_filt_b2[j], hy_filt_freq[j], hy_filt_w_out[j], hy_bias[j],
                  hy_w_out[j], hy_b_out[j])
            y_l = hyena_mixer(u_l, *hp)
            y_c = hyena_mixer(u_c, *hp) if need_ctx_out else None
        else:
            cp = (cv_w_pw1[j], cv_b_pw1[j], cv_w_dw[j], cv_b_dw[j], cv_ln_g[j], cv_ln_b[j],
                  cv_w_pw2[j], cv_b_pw2[j])
            y_l = conformer_conv(u_l, *cp)
            y_c = conformer_conv(u_c, *cp) if need_ctx_out else None
        h_lat = h_lat + mod_l[2] * rms_norm(y_l, norm_mix_post[i])
        v_l = modulate(rms_norm(h_lat, norm_mlp_pre[i]), mod_l[3], mod_l[4])
        h_lat = h_lat + mod_l[5] * rms_norm(squared_relu_mlp(v_l, w_mlp_in[i], w_mlp_out[i]), norm_mlp_post[i])
        if need_ctx_out:
            h_ctx = h_ctx + mod_c[2] * rms_norm(y_c, norm_mix_post[i])
            v_c = modulate(rms_norm(h_ctx, norm_mlp_pre[i]), mod_c[3], mod_c[4])
            h_ctx = h_ctx + mod_c[5] * rms_norm(squared_relu_mlp(v_c, w_mlp_in[i], w_mlp_out[i]), norm_mlp_post[i])
    return h_lat


DEPTH_2 = 1

MIX = D_MODEL // 2
GM_CHUNK = 128
GM_GROUPS = 4
GM_GW = MIX // GM_GROUPS
CONV_WIDTH_2 = 4
LRU_BLOCKS = 8
LRU_BW = MIX // LRU_BLOCKS
LRU_C = 8.0
N_HEADS_2 = 8
HEAD_DIM_2 = MIX // N_HEADS_2
N_KV = 2
HPG = N_HEADS_2 // N_KV
CMP_LEN = 32
CMP_STRIDE = 16
SLC_LEN = 64
SLC_TOPN = 8
WIN = 512
NSA_Q = N_HEADS_2 * HEAD_DIM_2
NSA_KV = N_KV * HEAD_DIM_2
POOL_WINDOWS = (2, 4, 8, 16)
POOL_GROUPS = len(POOL_WINDOWS)
POOL_GW = MIX // POOL_GROUPS
N_BRANCH = 4
N_GROUPS = 4
EXPERTS_PER_GROUP = 4
N_EXPERTS = N_GROUPS * EXPERTS_PER_GROUP
EXPERT_TOPK = 2
D_EXPERT = D_MODEL // 2

EPS = 1e-6
NEG_INF = -1e30
FORCE_SCORE = 1e6

IN_SPLITS = (MIX, MIX, MIX, MIX, NSA_Q, 6 * NSA_KV, 3 * N_HEADS_2, MIX, N_BRANCH * D_MODEL)
N_IN = sum(IN_SPLITS)


def rms_norm_2(x, g):
    xf = x.astype(jnp.float32)
    y = xf * lax.rsqrt(jnp.mean(xf * xf, axis=-1, keepdims=True) + EPS)
    return (y * g.astype(jnp.float32)).astype(x.dtype)

def gmlp_mixer(u, v, v_norm_g, ws, bs):
    B, S, _ = u.shape
    nc = S // GM_CHUNK
    u = jax.nn.gelu(u)
    v = rms_norm_2(jax.nn.gelu(v), v_norm_g).reshape(B, nc, GM_CHUNK, GM_GROUPS, GM_GW)
    causal = jnp.tril(jnp.ones((GM_CHUNK, GM_CHUNK), dtype=bool))
    w = jnp.where(causal[None], ws, 0.0)
    mixed = jnp.einsum('gts,bnsgc->bntgc', w, v) + bs.T[:, :, None]
    return u * mixed.reshape(B, S, MIX)

def rglru_mixer(gate_in, x_in, conv_w, conv_b, wa, ba, wx, bx, lam):
    B, S, C = x_in.shape
    f32 = jnp.float32
    xp = jnp.pad(x_in, ((0, 0), (CONV_WIDTH_2 - 1, 0), (0, 0)))
    xc = conv_b + sum(xp[:, k:k + S] * conv_w[k] for k in range(CONV_WIDTH_2))
    xb = xc.reshape(B, S, LRU_BLOCKS, LRU_BW)
    r = jax.nn.sigmoid(jnp.einsum('bshi,hij->bshj', xb, wa).reshape(B, S, C) + ba)
    i = jax.nn.sigmoid(jnp.einsum('bshi,hij->bshj', xb, wx).reshape(B, S, C) + bx)
    log_a = -LRU_C * r.astype(f32) * jax.nn.softplus(-lam.astype(f32))
    a = jnp.exp(log_a)
    b = jnp.sqrt(-jnp.expm1(2.0 * log_a)) * (i * xc).astype(f32)

    def combine(c1, c2):
        a1, b1 = c1
        a2, b2 = c2
        return a1 * a2, a2 * b1 + b2

    _, h = lax.associative_scan(combine, (a, b), axis=1)
    return jax.nn.gelu(gate_in) * h.astype(x_in.dtype)

def _gather_blocks(blocks, idx):
    return blocks[idx].reshape(idx.shape[0], -1, blocks.shape[-1])

_gather_bg = jax.vmap(jax.vmap(_gather_blocks))

def nsa_mixer(q, kv, gate_logits, cmp_pe, cmp_w1, cmp_w2):
    B, S, _ = q.shape
    f32 = jnp.float32
    scale = HEAD_DIM_2 ** -0.5
    t_pos = jnp.arange(S)
    qh = q.reshape(B, S, N_KV, HPG, HEAD_DIM_2).transpose(0, 2, 3, 1, 4)
    kv = kv.reshape(B, S, 6, N_KV, HEAD_DIM_2).transpose(2, 0, 3, 1, 4)

    n_sub = CMP_LEN // CMP_STRIDE
    n_chunk = S // CMP_STRIDE
    n_cmp = n_chunk - n_sub + 1
    chunks = kv[0:2].reshape(2, B, N_KV, n_chunk, CMP_STRIDE, HEAD_DIM_2)
    blocks = jnp.concatenate([chunks[:, :, :, j:j + n_cmp] for j in range(n_sub)], axis=4)
    blocks = blocks + cmp_pe[:, None, None, None]
    flat = blocks.reshape(2, B, N_KV, n_cmp, CMP_LEN * HEAD_DIM_2)
    hid = jax.nn.gelu(jnp.einsum('cbgnf,cgfe->cbgne', flat, cmp_w1))
    kvc = jnp.einsum('cbgne,cged->cbgnd', hid, cmp_w2)
    k_c, v_c = kvc[0], kvc[1]
    cmp_end = jnp.arange(n_cmp) * CMP_STRIDE + (CMP_LEN - 1)
    cmp_mask = cmp_end[None, :] <= t_pos[:, None]
    s_c = jnp.einsum('bgjsd,bgnd->bgjsn', qh, k_c).astype(f32) * scale
    p_c = jax.nn.softmax(jnp.where(cmp_mask, s_c, NEG_INF), axis=-1)
    p_c = jnp.where(jnp.any(cmp_mask, axis=-1)[:, None], p_c, 0.0)
    o_cmp = jnp.einsum('bgjsn,bgnd->bgjsd', p_c.astype(q.dtype), v_c)

    n_slc = S // SLC_LEN
    topn = min(SLC_TOPN, n_slc)
    c_start = np.arange(n_cmp) * CMP_STRIDE
    s_start = np.arange(n_slc) * SLC_LEN
    overlap = ((c_start[:, None] <= s_start[None, :] + SLC_LEN - 1)
               & (c_start[:, None] + CMP_LEN - 1 >= s_start[None, :])).astype(np.float32)
    imp = jnp.einsum('bgjsn,nm->bgsm', p_c, jnp.asarray(overlap))
    blk = jnp.arange(n_slc)
    cur = t_pos // SLC_LEN
    causal_blk = blk[None, :] * SLC_LEN <= t_pos[:, None]
    forced = (blk[None, :] == 0) | (blk[None, :] == cur[:, None]) | (blk[None, :] == cur[:, None] - 1)
    score = jnp.where(forced, FORCE_SCORE, jnp.where(causal_blk, imp, -1.0))
    top_val, top_idx = lax.top_k(score, topn)
    top_ok = top_val >= 0.0

    nq = S // Q_BLOCK
    ks_blk = kv[2].reshape(B, N_KV, n_slc, SLC_LEN, HEAD_DIM_2)
    vs_blk = kv[3].reshape(B, N_KV, n_slc, SLC_LEN, HEAD_DIM_2)

    def slc_block(args):
        q_b, idx_b, ok_b, t_b = args
        k_sel = _gather_bg(ks_blk, idx_b)
        v_sel = _gather_bg(vs_blk, idx_b)
        k_pos = idx_b[..., None] * SLC_LEN + jnp.arange(SLC_LEN)
        ok = (ok_b[..., None] & (k_pos <= t_b[:, None, None])).reshape(B, N_KV, Q_BLOCK, -1)
        s = jnp.einsum('bgjqd,bgqkd->bgjqk', q_b, k_sel).astype(f32) * scale
        p = jax.nn.softmax(jnp.where(ok[:, :, None], s, NEG_INF), axis=-1)
        return jnp.einsum('bgjqk,bgqkd->bgjqd', p.astype(q_b.dtype), v_sel)

    q_blocks = qh.reshape(B, N_KV, HPG, nq, Q_BLOCK, HEAD_DIM_2).transpose(3, 0, 1, 2, 4, 5)
    idx_blocks = top_idx.reshape(B, N_KV, nq, Q_BLOCK, topn).transpose(2, 0, 1, 3, 4)
    ok_blocks = top_ok.reshape(B, N_KV, nq, Q_BLOCK, topn).transpose(2, 0, 1, 3, 4)
    o_slc = lax.map(slc_block, (q_blocks, idx_blocks, ok_blocks, t_pos.reshape(nq, Q_BLOCK)))
    o_slc = o_slc.transpose(1, 2, 3, 0, 4, 5).reshape(B, N_KV, HPG, S, HEAD_DIM_2)

    n_pad = WIN // Q_BLOCK
    band_len = Q_BLOCK * (n_pad + 1)
    kw = jnp.pad(kv[4], ((0, 0), (0, 0), (WIN, 0), (0, 0))).reshape(B, N_KV, nq + n_pad, Q_BLOCK, HEAD_DIM_2)
    vw = jnp.pad(kv[5], ((0, 0), (0, 0), (WIN, 0), (0, 0))).reshape(B, N_KV, nq + n_pad, Q_BLOCK, HEAD_DIM_2)
    band_k = jnp.concatenate([kw[:, :, j:j + nq] for j in range(n_pad + 1)], axis=3)
    band_v = jnp.concatenate([vw[:, :, j:j + nq] for j in range(n_pad + 1)], axis=3)
    qb = qh.reshape(B, N_KV, HPG, nq, Q_BLOCK, HEAD_DIM_2)
    s_w = jnp.einsum('bgjiqd,bgikd->bgjiqk', qb, band_k).astype(f32) * scale
    q_idx = jnp.arange(Q_BLOCK)
    k_idx = jnp.arange(band_len)
    delta = WIN + q_idx[:, None] - k_idx[None, :]
    k_abs = (jnp.arange(nq)[:, None] - n_pad) * Q_BLOCK + k_idx[None, :]
    win_mask = ((delta >= 0) & (delta < WIN))[None] & (k_abs >= 0)[:, None, :]
    p_w = jax.nn.softmax(jnp.where(win_mask, s_w, NEG_INF), axis=-1)
    o_win = jnp.einsum('bgjiqk,bgikd->bgjiqd', p_w.astype(q.dtype), band_v).reshape(B, N_KV, HPG, S, HEAD_DIM_2)

    g = jax.nn.sigmoid(gate_logits.reshape(B, S, N_KV, HPG, 3).transpose(4, 0, 2, 3, 1))[..., None]
    o = g[0] * o_cmp + g[1] * o_slc + g[2] * o_win
    return o.transpose(0, 3, 1, 2, 4).reshape(B, S, NSA_Q)

def pool_mixer(xd, pool_w, pool_scale):
    B, S, C = xd.shape
    f32 = jnp.float32
    xf = xd.astype(f32)
    csum = jnp.pad(lax.cumsum(xf, axis=1), ((0, 0), (1, 0), (0, 0)))
    t = jnp.arange(S)
    outs = []
    for gi, w in enumerate(POOL_WINDOWS):
        c = csum[:, :, gi * POOL_GW:(gi + 1) * POOL_GW]
        lower = jnp.pad(c[:, :S + 1 - w], ((0, 0), (w - 1, 0), (0, 0)))
        cnt = jnp.minimum(t + 1, w).astype(f32)[None, :, None]
        outs.append((c[:, 1:] - lower) / cnt - xf[:, :, gi * POOL_GW:(gi + 1) * POOL_GW])
    pooled = jnp.stack(outs, axis=2).astype(xd.dtype)
    mixed = jnp.einsum('bsgi,gij->bsgj', pooled, pool_w).reshape(B, S, C)
    return mixed * pool_scale

def hybrid_mixer(h, w_in, gm_norm_g, gm_ws, gm_b, conv_w, conv_b, lru_wa, lru_ba, lru_wx,
                 lru_bx, lru_lambda, cmp_pe, cmp_w1, cmp_w2, pool_w, pool_scale, w_branch, w_out):
    B, S, _ = h.shape
    proj = h @ w_in
    cuts = np.cumsum(IN_SPLITS)[:-1].tolist()
    u, v, gate_b, rec_b, q, kv, nsa_g, xd, mg = jnp.split(proj, cuts, axis=-1)
    y_a = gmlp_mixer(u, v, gm_norm_g, gm_ws, gm_b)
    y_b = rglru_mixer(gate_b, rec_b, conv_w, conv_b, lru_wa, lru_ba, lru_wx, lru_bx, lru_lambda)
    y_c = nsa_mixer(q, kv, nsa_g, cmp_pe, cmp_w1, cmp_w2)
    y_d = pool_mixer(xd, pool_w, pool_scale)
    ys = jnp.stack([y_a, y_b, y_c, y_d])
    branch = jnp.einsum('nbsc,ncd->bsnd', ys, w_branch)
    gates = jax.nn.sigmoid(mg.reshape(B, S, N_BRANCH, D_MODEL))
    merged = jnp.sum(gates * branch, axis=2)
    return merged @ w_out

def hier_moe(h, wr_g, br_g, wr_e, br_e, w_gate, w_up, w_down):
    B, S, D = h.shape
    f32 = jnp.float32
    t = h.reshape(-1, D)
    T = t.shape[0]
    grp_p = jax.nn.softmax((t @ wr_g + br_g).astype(f32), axis=-1)
    grp_w, grp_idx = lax.top_k(grp_p, 1)
    exp_logits = (t @ wr_e + br_e).astype(f32).reshape(T, N_GROUPS, EXPERTS_PER_GROUP)
    in_grp = jnp.einsum('tge,tg->te', exp_logits, jax.nn.one_hot(grp_idx[:, 0], N_GROUPS, dtype=f32))
    top_l, top_e = lax.top_k(in_grp, EXPERT_TOPK)
    top_w = jax.nn.softmax(top_l, axis=-1) * grp_w
    expert_id = grp_idx * EXPERTS_PER_GROUP + top_e
    combine = jnp.sum(jax.nn.one_hot(expert_id, N_EXPERTS, dtype=f32) * top_w[..., None], axis=1)
    hid = jax.nn.silu(jnp.einsum('td,edf->etf', t, w_gate)) * jnp.einsum('td,edf->etf', t, w_up)
    hid = hid * combine.T[:, :, None].astype(hid.dtype)
    out = jnp.einsum('etf,efd->td', hid, w_down)
    return out.reshape(B, S, D)

def second_inputs(seed: int = 0) -> dict:
    key = jax.random.key(seed)
    ks = iter(jax.random.split(key, 40))
    f32 = jnp.float32
    L = DEPTH_2

    def nrm(shape, scale):
        return jax.random.normal(next(ks), shape, f32) * scale

    def gain(shape):
        return 1.0 + 0.02 * jax.random.normal(next(ks), shape, f32)

    a_c = jax.random.uniform(next(ks), (L, MIX), f32, minval=0.9, maxval=0.999)
    a0 = a_c ** (1.0 / LRU_C)
    lru_lambda = jnp.log(a0) - jnp.log1p(-a0)
    return {
        'x': nrm((BATCH, SEQ, D_MODEL), 1.0),
        'norm1_g': gain((L, D_MODEL)),
        'w_in': nrm((L, D_MODEL, N_IN), D_MODEL ** -0.5),
        'gm_norm_g': gain((L, MIX)),
        'gm_ws': nrm((L, GM_GROUPS, GM_CHUNK, GM_CHUNK), GM_CHUNK ** -0.5),
        'gm_b': gain((L, GM_GROUPS, GM_CHUNK)),
        'conv_w': nrm((L, CONV_WIDTH_2, MIX), CONV_WIDTH_2 ** -0.5),
        'conv_b': nrm((L, MIX), 0.02),
        'lru_wa': nrm((L, LRU_BLOCKS, LRU_BW, LRU_BW), LRU_BW ** -0.5),
        'lru_ba': nrm((L, MIX), 0.02),
        'lru_wx': nrm((L, LRU_BLOCKS, LRU_BW, LRU_BW), LRU_BW ** -0.5),
        'lru_bx': nrm((L, MIX), 0.02),
        'lru_lambda': lru_lambda,
        'cmp_pe': nrm((L, 2, CMP_LEN, HEAD_DIM_2), 0.02),
        'cmp_w1': nrm((L, 2, N_KV, CMP_LEN * HEAD_DIM_2, HEAD_DIM_2), (CMP_LEN * HEAD_DIM_2) ** -0.5),
        'cmp_w2': nrm((L, 2, N_KV, HEAD_DIM_2, HEAD_DIM_2), HEAD_DIM_2 ** -0.5),
        'pool_w': nrm((L, POOL_GROUPS, POOL_GW, POOL_GW), POOL_GW ** -0.5),
        'pool_scale': gain((L, MIX)),
        'w_branch': nrm((L, N_BRANCH, MIX, D_MODEL), MIX ** -0.5),
        'w_out': nrm((L, D_MODEL, D_MODEL), D_MODEL ** -0.5),
        'norm2_g': gain((L, D_MODEL)),
        'router_w_group': nrm((L, D_MODEL, N_GROUPS), D_MODEL ** -0.5),
        'router_b_group': nrm((L, N_GROUPS), 0.01),
        'router_w_expert': nrm((L, D_MODEL, N_EXPERTS), D_MODEL ** -0.5),
        'router_b_expert': nrm((L, N_EXPERTS), 0.01),
        'moe_w_gate': nrm((L, N_EXPERTS, D_MODEL, D_EXPERT), D_MODEL ** -0.5),
        'moe_w_up': nrm((L, N_EXPERTS, D_MODEL, D_EXPERT), D_MODEL ** -0.5),
        'moe_w_down': nrm((L, N_EXPERTS, D_EXPERT, D_MODEL), D_EXPERT ** -0.5),
        'final_norm_g': gain((D_MODEL,)),
    }

def second_block(x, norm1_g, w_in, gm_norm_g, gm_ws, gm_b, conv_w, conv_b, lru_wa, lru_ba, lru_wx,
              lru_bx, lru_lambda, cmp_pe, cmp_w1, cmp_w2, pool_w, pool_scale, w_branch, w_out,
              norm2_g, router_w_group, router_b_group, router_w_expert, router_b_expert,
              moe_w_gate, moe_w_up, moe_w_down, final_norm_g):
    h = x
    for l in range(DEPTH_2):
        h = h + hybrid_mixer(rms_norm_2(h, norm1_g[l]), w_in[l], gm_norm_g[l], gm_ws[l], gm_b[l],
                             conv_w[l], conv_b[l], lru_wa[l], lru_ba[l], lru_wx[l], lru_bx[l],
                             lru_lambda[l], cmp_pe[l], cmp_w1[l], cmp_w2[l], pool_w[l],
                             pool_scale[l], w_branch[l], w_out[l])
        h = h + hier_moe(rms_norm_2(h, norm2_g[l]), router_w_group[l], router_b_group[l],
                         router_w_expert[l], router_b_expert[l], moe_w_gate[l], moe_w_up[l],
                         moe_w_down[l])
    return rms_norm_2(h, final_norm_g)


def setup_inputs(seed=0):
    out = dict(first_inputs(seed))
    for name, value in second_inputs(seed + 1).items():
        if name != "x":
            out[name + "_2"] = value
    return out


def reference(
    x, c, ctx, c_ctx, w_mod, b_mod, norm_mix_pre, norm_mix_post, norm_mlp_pre, norm_mlp_post,
    w_mlp_in, w_mlp_out, attn_w_qkv, attn_w_out, attn_lambda, attn_subln, hy_w_in, hy_b_in,
    hy_w_short, hy_b_short, hy_filt_w1, hy_filt_b1, hy_filt_w2, hy_filt_b2, hy_filt_freq,
    hy_filt_w_out, hy_bias, hy_w_out, hy_b_out, cv_w_pw1, cv_b_pw1, cv_w_dw, cv_b_dw, cv_ln_g,
    cv_ln_b, cv_w_pw2, cv_b_pw2, norm1_g_2, w_in_2, gm_norm_g_2, gm_ws_2, gm_b_2, conv_w_2,
    conv_b_2, lru_wa_2, lru_ba_2, lru_wx_2, lru_bx_2, lru_lambda_2, cmp_pe_2, cmp_w1_2,
    cmp_w2_2, pool_w_2, pool_scale_2, w_branch_2, w_out_2, norm2_g_2, router_w_group_2,
    router_b_group_2, router_w_expert_2, router_b_expert_2, moe_w_gate_2, moe_w_up_2,
    moe_w_down_2, final_norm_g_2,
):
    x = first_block(
        x, c, ctx, c_ctx, w_mod, b_mod, norm_mix_pre, norm_mix_post, norm_mlp_pre,
        norm_mlp_post, w_mlp_in, w_mlp_out, attn_w_qkv, attn_w_out, attn_lambda, attn_subln,
        hy_w_in, hy_b_in, hy_w_short, hy_b_short, hy_filt_w1, hy_filt_b1, hy_filt_w2,
        hy_filt_b2, hy_filt_freq, hy_filt_w_out, hy_bias, hy_w_out, hy_b_out, cv_w_pw1,
        cv_b_pw1, cv_w_dw, cv_b_dw, cv_ln_g, cv_ln_b, cv_w_pw2, cv_b_pw2,
    )
    return second_block(
        x, norm1_g_2, w_in_2, gm_norm_g_2, gm_ws_2, gm_b_2, conv_w_2, conv_b_2, lru_wa_2,
        lru_ba_2, lru_wx_2, lru_bx_2, lru_lambda_2, cmp_pe_2, cmp_w1_2, cmp_w2_2, pool_w_2,
        pool_scale_2, w_branch_2, w_out_2, norm2_g_2, router_w_group_2, router_b_group_2,
        router_w_expert_2, router_b_expert_2, moe_w_gate_2, moe_w_up_2, moe_w_down_2,
        final_norm_g_2,
    )


_drawn_inputs = setup_inputs


def setup_inputs(seed=0):
    import zlib

    import numpy as np

    out = dict(_drawn_inputs(seed))
    spreads = {}
    factors = {'hy_b_short': 2.827,
     'hy_b_out': 29.431,
     'gm_norm_g_2': 32.541,
     'gm_b_2': 27.744,
     'lru_ba_2': 64.0,
     'lru_bx_2': 51.35,
     'cmp_pe_2': 59.614,
     'pool_scale_2': 22.033,
     'router_b_group_2': 56.104,
     'router_b_expert_2': 42.949,
     'final_norm_g_2': 8.366,
     'attn_subln': 3.244,
     'hy_b_in': 4.776,
     'conv_b_2': 6.045,
     'lru_wa_2': 3.603,
     'norm2_g_2': 8.0}
    for name, (base, spread) in spreads.items():
        noise = np.random.default_rng([zlib.crc32(name.encode()), seed]).standard_normal(out[name].shape)
        drawn = base * np.exp(spread * noise) if base else spread * noise
        out[name] = jnp.asarray(drawn.astype(out[name].dtype))
    for name, factor in factors.items():
        out[name] = (out[name] * factor).astype(out[name].dtype)
    return out
```

```python
from contextlib import ExitStack
import math

import numpy as np

import concourse.bass as bass
from concourse import mybir

F32 = mybir.dt.float32
F32R = mybir.dt.float32r
ACT = mybir.ActivationFunctionType
ALU = mybir.AluOpType
AX = mybir.AxisListType.X

P = 128
D = 1024
KT = D // P
T = 256
TT = T // P
DFF = 4096
HEADS = 8
RING = 3
CW = 2048
EXPERTS = 16
DE = 512
MIX = 512
MT = MIX // P
NCMP = 15
CMP_STRIDE, CMP_LEN = 16, 32
HD = 64
LAM_INIT = 0.8 - 0.6 * math.exp(0.0)
SCALE = HD ** -0.5
EPS = 1e-6
MASKED = -1e30
BRANCH_ORDER = (0, 3, 1, 2)
POOL_WINDOWS = (2, 4, 8, 16)

U0, V0, GATE0, REC0, Q0, KV0, NSAG0, XD0, MG0 = 0, 512, 1024, 1536, 2048, 2560, 3328, 3352, 3864


def weight_stream():
    def cols(a, n):
        return tuple(range(a, a + n))

    def mat(name, lead, c0):
        return (name, lead, 0, D, cols(c0, 256))

    def down(name, lead, c0):
        return (name, lead, 0, MIX, cols(c0, 512))

    def mlp(layer):
        return [mat("w_mlp_in", (layer,), 256 * j) for j in range(16)] + \
            [("w_mlp_out", (layer,), D * g, D, cols(256 * m, 256)) for m in range(4) for g in range(4)]

    out = [mat("attn_w_qkv", (0,), c0 + 256 * j) for c0 in (D, 0, 2 * D) for j in range(4)]
    out += [mat("attn_w_out", (0,), 256 * j) for j in range(4)]
    out += mlp(0)
    out += [mat("hy_w_in", (0,), c0 + 256 * j) for c0 in (2 * D, D, 0) for j in range(4)]
    out += [mat("hy_w_out", (0,), 256 * j) for j in range(4)]
    out += mlp(1)
    kv = lambda n: cols(KV0 + 128 * n, 128)
    qcol = lambda j: cols(Q0 + 64 * j, 64) + cols(Q0 + 256 + 64 * j, 64)
    for c in [kv(0) + kv(1), kv(2) + kv(4), qcol(0) + qcol(1), qcol(2) + qcol(3), kv(3) + kv(5), cols(NSAG0, 24)]:
        out.append(("w_in_2", (0,), 0, D, c))
    for c0 in (REC0, REC0 + 256, GATE0, GATE0 + 256, XD0, XD0 + 256, V0, V0 + 256, U0, U0 + 256):
        out.append(mat("w_in_2", (0,), c0))
    for n in BRANCH_ORDER:
        out += [mat("w_in_2", (0,), MG0 + D * n + 256 * j) for j in range(4)]
        out += [down("w_branch_2", (0, n), 512 * j) for j in range(2)]
    out += [mat("w_out_2", (0,), 256 * j) for j in range(4)]
    gate = lambda e: [mat("moe_w_gate_2", (0, e), 256 * j) for j in range(2)]
    upx = lambda e: [mat("moe_w_up_2", (0, e), 256 * j) for j in range(2)]
    dnx = lambda e: [down("moe_w_down_2", (0, e), 512 * j) for j in range(2)]
    out += gate(0) + upx(0)
    for e in range(1, EXPERTS):
        out += gate(e) + dnx(e - 1) + upx(e)
    out += dnx(EXPERTS - 1)
    return out


N_CHUNKS = 236
N_MODS = 96
I_QKV, I_AO, I_MLP0, I_HY, I_HO, I_MLP1, I_PROJ, I_BR, I_WO, I_MOE = 0, 12, 16, 48, 60, 64, 96, 112, 136, 140


def param_columns():
    names = [("b_mod", 96), ("mix_pre", 16), ("mix_post", 16), ("mlp_pre", 16), ("mlp_post", 16),
             ("subln", 1), ("hy_b_in", 24), ("hy_w_short", 72), ("hy_b_short", 24), ("hy_bias", 8),
             ("hy_b_out", 8), ("norm1", 8), ("gm_norm", 4), ("conv_w", 16), ("conv_b", 4), ("ba", 4),
             ("bx", 4), ("lam", 4), ("pool_scale", 4), ("norm2", 8), ("final", 8)]
    out, at = {}, 0
    for n, k in names:
        out[n] = (at, k)
        at += k
    return out, at


PCOL, NPAR = param_columns()

CONST = {}
_at = 0
for _n, _k in (("ones", 128), ("ident", 128), ("rot", 128), ("cos", 256), ("sin", 256), ("notfirst", 1), ("eps", 1)):
    CONST[_n] = (_at, _k)
    _at += _k
NCONST = _at
CONST_B = {}
_at = 0
for _n, _k in (("causal", 128), ("tril", 128), ("cmask", 30), ("cvalid", 2), ("recip", 1024)):
    CONST_B[_n] = (_at, _k)
    _at += _k
NCONST_B = _at


def shape_constants():
    f = np.float32
    p = np.arange(P)
    t = np.arange(T)
    c = np.zeros((P, NCONST), f)

    def put(table, where, name, v):
        a, k = where[name]
        table[:, a:a + k] = v

    put(c, CONST, "ones", 1.0)
    put(c, CONST, "ident", np.eye(P))
    rot = np.zeros((P, P))
    first = (p % 32) < 16
    rot[p[first] + 16, p[first]] = -1.0
    rot[p[~first] - 16, p[~first]] = 1.0
    put(c, CONST, "rot", rot)
    inv = (f(10000.0) ** (-(np.arange(16, dtype=f)) / f(16))).astype(f)
    pos = np.where((p % 64)[:, None] < 32, (t // 64)[None, :], (t % 64)[None, :]).astype(f)
    ang = pos * inv[p % 16][:, None]
    put(c, CONST, "cos", np.cos(ang, dtype=f))
    put(c, CONST, "sin", np.sin(ang, dtype=f))
    put(c, CONST, "notfirst", (p > 0).astype(f)[:, None])
    put(c, CONST, "eps", EPS)
    b = np.zeros((P, NCONST_B), f)
    put(b, CONST_B, "causal", np.where(p[None, :] <= p[:, None], 0.0, MASKED))
    put(b, CONST_B, "tril", (p[:, None] <= p[None, :]).astype(f))
    cm = np.zeros((P, 2, NCMP))
    for qt in range(2):
        cm[:, qt] = np.where((16 * np.arange(NCMP) + 31)[None, :] <= (qt * P + p)[:, None], 0.0, MASKED)
    put(b, CONST_B, "cmask", cm.reshape(P, -1))
    put(b, CONST_B, "cvalid", np.stack([p >= 31, p >= 0], 1).astype(f))
    rec = np.stack([1.0 / np.minimum(t + 1, w) for w in POOL_WINDOWS]).astype(f)
    put(b, CONST_B, "recip", np.broadcast_to(rec.reshape(1, -1), (P, 1024)))
    tl = np.linspace(0.0, 1.0, T, dtype=f)[:, None]
    w = f(2.0 * math.pi) * np.arange(T, dtype=f)[:, None] / f(T)
    fr = np.linspace(1e-4, 15, 16, dtype=f)[None, :]
    z = np.concatenate([tl, np.cos(fr * w), -np.sin(fr * w)], axis=1).astype(f)
    deltas = np.abs(np.linspace(math.log(1e-2) / 1.5, math.log(1e-2) / 0.3, D, dtype=f))
    decay = np.exp(-tl * deltas[None, :]).astype(f)
    k = np.arange(T)
    th = 2.0 * np.pi * (k + 0.5)[None, :] * t[:, None] / (2 * T)
    fwd = np.concatenate([np.cos(th), np.sin(th)], axis=1)
    inv_ = np.concatenate([np.cos(th).T, np.sin(th).T], axis=0) / T
    return {
        "const": c, "const_b": b, "zfeat": np.ascontiguousarray(z.T),
        "decay": np.ascontiguousarray(decay.reshape(TT, P, D).transpose(1, 0, 2)),
        "dft": np.ascontiguousarray(fwd.reshape(TT, P, 2 * T).transpose(1, 0, 2).astype(f)),
        "idft": np.ascontiguousarray(inv_.reshape(4, P, T).transpose(1, 0, 2).astype(f)),
    }


def program(nc, A, out, upto="all"):
    stages = ["attn", "mlp0", "hyena", "mlp1", "mixer", "all"]
    ends = {"attn": I_MLP0, "mlp0": I_HY, "hyena": I_MLP1, "mlp1": I_PROJ, "mixer": I_MOE, "all": N_CHUNKS}
    n_chunks = ends[upto] + (upto == "all")
    n_mods = {"attn": 80, "mlp0": 88}.get(upto, N_MODS)

    def on(stage):
        return stages.index(stage) <= stages.index(upto)

    stack = ExitStack()
    sems = {}

    def s(name):
        if name not in sems:
            sems[name] = stack.enter_context(nc.semaphore(name))
        return sems[name]

    def up(value, n=None, step=0):
        return value if n is None else n * step + value

    normed_inputs = ["x", "ctx", "mlp0_in", "hy_in", "hy", "mlp1_in", "mix_in", "merged", "moe_in"]
    turns_of = {
        "squares": [("x", 2), ("ctx", 2), ("post0", 4), ("mlp0_in", 2), ("mlp0", 4), ("hy_in", 2), ("post1", 4), ("mlp1_in", 2),
                    ("mlp1", 4), ("mix_in", 2), ("moe_in", 2), ("final", 2)],
        "normed": [(t, 2) for t in normed_inputs + ["final"]],
        "hi": [(t, 2) for t in normed_inputs], "lo": [(t, 2) for t in normed_inputs],
        "h": [(t, 2) for t in ("post0", "mlp0", "post1", "mlp1", "mixed", "moe")],
    }
    turns_of["sumsq"] = turns_of["std"] = [(t, 1) for t, _ in turns_of["squares"]]

    def nth(tag, step, count):
        before = 0
        for t, n in turns_of[step]:
            if t == tag:
                return s(step), before + count
            before += n
        raise KeyError((tag, step))

    def mlp_nth(tag, step, count):
        per_layer = {"free": 19, "rfree": 19, "hid_hi": 16, "hidden": 16, "yfree": 6}[step]
        return s("mlp_" + step), count + (per_layer if tag == "mlp1" else 0)

    class Chain:

        def __init__(self, eng, name):
            self.eng, self.sem, self.count, self.n, self.step = eng, s(name), 0, None, 0

        def tick(self, ins):
            self.count += 1
            ins.then_inc(self.sem, 1)
            return up(self.count, self.n, self.step)

        def __call__(self, ins):
            self.eng.wait_ge(self.sem, self.tick(ins))

        def enter(self, n, step):
            self.start, self.n, self.step = self.count, n, step

        def leave(self, turns):
            assert self.count == self.start + self.step, (self.count - self.start, self.step)
            self.count, self.n, self.step = self.start + self.step * turns, None, 0

    with stack:
        def alloc(where, name, shape, dt=F32):
            return where.enter_context(nc.sbuf_tensor(name, [P, *shape], dt))

        raw = alloc(stack, "raw", [RING, CW])
        mraw = alloc(stack, "mraw", [2, KT * P])
        whi = alloc(stack, "whi", [RING, CW], F32R)
        wlo = alloc(stack, "wlo", [RING, CW], F32R)
        h = alloc(stack, "h", [KT, T])
        uhi = alloc(stack, "uhi", [KT, T], F32R)
        ulo = alloc(stack, "ulo", [KT, T], F32R)
        y = alloc(stack, "y", [KT, T])
        sq = alloc(stack, "sq", [KT, T])
        std = alloc(stack, "std", [T])
        rstd = alloc(stack, "rstd", [T])
        par = alloc(stack, "par", [NPAR])
        con = alloc(stack, "con", [NCONST])
        modv = alloc(stack, "modv", [96, 2])
        coef = alloc(stack, "coef", [10, KT])
        small = alloc(stack, "small", [64])
        cvec = alloc(stack, "cvec", [KT, 2])
        csil = alloc(stack, "csil", [KT, 2])
        hdn = alloc(stack, "hdn", [T])
        ps = stack.enter_context(nc.psum_tensor("ps", [P, 8, 512], F32))

        with ExitStack() as st:
            qbuf = alloc(st, "qbuf", [HEADS, T])
            kbuf = alloc(st, "kbuf", [HEADS, 2 * T])
            vbuf = alloc(st, "vbuf", [4, D])
            with ExitStack() as st2:
                ctx = alloc(st2, "ctx", [KT, T])
                ctx_hi = alloc(st2, "ctx_hi", [KT, T], F32R)
                ctx_lo = alloc(st2, "ctx_lo", [KT, T], F32R)
            obuf = alloc(st, "obuf", [HEADS, T])
            ebuf = alloc(st, "ebuf", [2, 2, 512])
            atb = alloc(st, "atb", [2, 4, T])
        with ExitStack() as st:
            hid_hi = alloc(st, "hid_hi", [DFF // P, T], F32R)
            hid_lo = alloc(st, "hid_lo", [DFF // P, T], F32R)
        with ExitStack() as st:
            hv = alloc(st, "hv", [KT, T])
            hx0 = alloc(st, "hx0", [KT, T])
            hx1 = alloc(st, "hx1", [2, T])
            zpad = alloc(st, "zpad", [2, 2, T + 2])
            vtok = alloc(st, "vtok", [TT, D])
            dft = alloc(st, "dft", [TT, 2 * T])
            idft = alloc(st, "idft", [4, T])
            spec = alloc(st, "spec", [4, D])
            with ExitStack() as st2:
                fwo = alloc(st2, "fwo", [2 * D])
                taps = alloc(st2, "taps", [TT, 512])
            yspec = alloc(st, "yspec", [4, 512])
            prod = alloc(st, "prod", [2, 2, 512])
        with ExitStack() as st:
            gm = alloc(st, "gm", [2, MT, T])
            gate = alloc(st, "gate", [MT, T])
            rec = alloc(st, "rec", [MT, T + 3])
            qn = alloc(st, "qn", [MT, T])
            ksw = alloc(st, "ksw", [2, T])
            vsw = alloc(st, "vsw", [TT, 256])
            xd = alloc(st, "xd", [MT, T + 16])
            yhi = alloc(st, "yhi", [4 * MT, T], F32R)
            with ExitStack() as st2:
                ylo = alloc(st2, "ylo", [4 * MT, T], F32R)
            w1c = alloc(st, "w1c", [2, CMP_LEN * HD])
            w2c = alloc(st, "w2c", [2, HD])
            conb = alloc(st, "conb", [NCONST_B])
            gmw = alloc(st, "gmw", [MT, P])
            gmb = alloc(st, "gmb", [MT, P])
            lruw = alloc(st, "lruw", [2, MT, P])
            poolw = alloc(st, "poolw", [MT, P])
            cpe = alloc(st, "cpe", [2, CMP_LEN])
            hidc = alloc(st, "hidc", [2, 16])
            kc = alloc(st, "kc", [16])
            vc = alloc(st, "vc", [P])
            gates = alloc(st, "gates", [TT, 24])
            lru = alloc(st, "lru", [12, MT])
            sm = alloc(st, "sm", [64])
        with ExitStack() as st:
            comb = alloc(st, "comb", [EXPERTS, T])
            sg = alloc(st, "sg", [DE // P, T])
            hmid = alloc(st, "hmid", [DE // P, T])
            ehi = alloc(st, "ehi", [DE // P, T], F32R)
            elo = alloc(st, "elo", [DE // P, T], F32R)
            wr = alloc(st, "wr", [KT, 20])
            wrhi = alloc(st, "wrhi", [KT, 20], F32R)
            wrlo = alloc(st, "wrlo", [KT, 20], F32R)
            rb = alloc(st, "rb", [20])
            order4 = alloc(st, "order4", [4])
            lg = alloc(st, "lg", [TT, 20])
            ro = alloc(st, "ro", [24, TT, 4])
            cb = alloc(st, "cb", [TT, EXPERTS])
            cbt = alloc(st, "cbt", [T])

        def pcol(name, a=0, k=None):
            c0, n = PCOL[name]
            return par[:, c0 + a:c0 + (a + k if k else n)]

        def ccol(name):
            c0, n = CONST[name]
            return con[:, c0:c0 + n]

        ones, ident, rot = ccol("ones"), ccol("ident"), ccol("rot")

        def over_tiles(x, n):
            return x.unsqueeze(1).to_broadcast([P, n, x.shape[1]])

        def over_cols(x, w):
            return x.unsqueeze(2).to_broadcast([P, x.shape[1], w])

        def f32(x):
            return x.bitcast(F32)

        def mod_scale(layer, part, who):
            return modv[:, layer * 48 + part * 8:layer * 48 + part * 8 + 8, who]

        lamv = sq[:, 7, :]
        zfeat, fw1, fw2 = y[:, 0, :], y[:, 1, 0:HD], y[:, 1, HD:3 * HD].rearrange("p (a d) -> p a d", a=2)
        farg, frnd, fpar = y[:, 2, :], y[:, 3, :], y[:, 5, 0:4]
        decay = y[:].rearrange("p (t a) c -> p t (a c)", t=TT)
        tapf, tapb = sq[:, 0:4, :].rearrange("p (t a) c -> p t (a c)", t=TT), sq[:, 4:8, :].rearrange("p (t a) c -> p t (a c)", t=TT)

        def bcol(name):
            c0, n = CONST_B[name]
            return conb[:, c0:c0 + n]

        ug, vg, gated = gm[:, 0], gm[:, 1].rearrange("p (t a) c -> p t (a c)", t=TT), gm[:].rearrange("p a m t -> p (a m) t")
        causal, tril = bcol("causal"), bcol("tril")
        blocks = sq[:, 0:4, :].rearrange("p a c -> p (a c)")[:, 0:2 * CMP_LEN * NCMP].rearrange("p (c l n) -> p c l n", c=2, l=CMP_LEN)
        cmp_t = sq[0:NCMP].rearrange("p a c -> p (a c)").rearrange("p (u q) -> p u q", u=16)
        cmp_p = sq[:, 0, 0:2 * HEADS * NCMP].rearrange("p (t h n) -> p t h n", t=TT, h=HEADS)
        nsa_e = y[:, 0:4, :].rearrange("p (a b) k -> p a b k", a=2)
        nsa_t = y[:, 4:8, :]
        slot_of = {n: MT * b for b, n in enumerate(BRANCH_ORDER)}

        block = stack.enter_context(nc.Block())

        @block.sync
        def _(sp):
            W = A["weights"]
            for i in range(RING):
                sp.dma_start(raw[:, i, :], W[i]).then_inc(s(f"raw_loaded{i}"), 16)
            turns, rest = divmod(n_chunks - RING, RING)
            with sp.Fori(0, turns) as n:
                for j in range(RING):
                    sp.wait_ge(s("lo_ready"), n * RING + (j + 1))
                    sp.dma_start(raw[:, j, :], W[bass.ds(n * RING + (RING + j), 1)].rearrange("a p c -> (a p) c"))\
                        .then_inc(s(f"raw_loaded{j}"), 16)
            for j in range(rest):
                i = RING * (turns + 1) + j
                sp.wait_ge(s("lo_ready"), i - RING + 1)
                sp.dma_start(raw[:, j, :], W[i]).then_inc(s(f"raw_loaded{j}"), 16)
            sp.wait_ge(s("result_ready"), 1)
            sp.dma_start(out, y[:]).then_inc(s("stored"), 16)
            sp.wait_ge(s("stored"), 16)

        @block.gpsimd
        def _(pool):
            M = A["mods"]
            for j in range(2):
                pool.dma_start(mraw[:, j, :], M[j]).then_inc(s(f"mraw_loaded{j}"), 16)
            with pool.Fori(0, n_mods // 2 - 1) as n:
                for j in range(2):
                    pool.wait_ge(s("mraw_used"), n * 2 + (j + 1))
                    pool.dma_start(mraw[:, j, :], M[bass.ds(n * 2 + (2 + j), 1)].rearrange("a p c -> (a p) c"))\
                        .then_inc(s(f"mraw_loaded{j}"), 16)

        @block.tensor
        def _(pe):
            mm = nc.tensor.matmul

            def three(o, w0, w1, x0, x1, first, last, **kw):
                mm(o, w0, x0, start=first, stop=False, **kw)
                mm(o, w1, x0, start=False, stop=False, **kw)
                return mm(o, w0, x1, start=False, stop=last, **kw)

            def three_rows(mm, o, a0, a1, w0, w1, first, last):
                mm(o, a0, w0, start=first, stop=False)
                mm(o, a0, w1, start=False, stop=False)
                return mm(o, a1, w0, start=False, stop=last)

            def weights_ready(i, n=None, step=0):
                pe.wait_ge(s("lo_ready"), up(i + 1, n, step))

            def used(ins):
                ins.then_inc(s("chunk_used"), 1)

            def tiles(i, bank_of, xs, kts=8, width=2, cols=T, k0=0, first=True, last=True, x_wait=None):
                sl = i % RING
                span = P * width
                for m in range(width):
                    for x_i, (x0, x1) in enumerate(xs):
                        o = bank_of(m, x_i)
                        for k in range(kts):
                            if x_wait and m == 0 and k % 4 == 0 and x_i == len(xs) - 1:
                                pe.wait_ge(*nth(x_wait, "lo", k // 4 + 1))
                            w = k * span + m * P
                            ins = three(o, whi[:, sl, w:w + P], wlo[:, sl, w:w + P], x0[:, k0 + k, :], x1[:, k0 + k, :],
                                        first and k == 0, last and k == kts - 1)
                return ins

            def by_token(i, out_of, xs, ncols=256):
                sl = i % RING
                tt = 0
                for x0, x1 in xs:
                    for t0 in range(TT):
                        o = out_of(tt)
                        tt += 1
                        for k in range(KT):
                            w0, w1 = (w[:, sl, k * 256:k * 256 + ncols] for w in (whi, wlo))
                            a0, a1 = (x[:, k, t0 * P:(t0 + 1) * P] for x in (x0, x1))
                            mm(o, a0, w0, start=k == 0, stop=False)
                            mm(o, a0, w1, start=False, stop=False)
                            ins = mm(o, a1, w0, start=False, stop=k == KT - 1)
                return ins

            def modulation(g):
                if g:
                    pe.wait_ge(s("mod_drained"), g)
                for j in range(4 * g, 4 * g + 4):
                    pe.wait_ge(s(f"mraw_loaded{j % 2}"), 16 * (j // 2 + 1))
                    for k in range(KT):
                        ins = mm(ps[:, 7, 2 * (j % 4):2 * (j % 4) + 2], mraw[:, j % 2, k * P:(k + 1) * P], csil[:, k, :],
                                 start=k == 0, stop=k == KT - 1)
                    ins.then_inc(s("mraw_used"), 1)

            def sum_squares(tag, bank, src=sq, counts=2):
                per = KT // counts
                for c in range(counts):
                    pe.wait_ge(*nth(tag, "squares", c + 1))
                    for k in range(c * per, (c + 1) * per):
                        ins = mm(ps[:, bank, 0:T], ones, src[:, k, :], start=k == 0, stop=k == KT - 1)
                ins.then_inc(s("sumsq"), 1)

            def filter_layer(j):
                if j == 0:
                    pe.wait_ge(s("filter_loaded"), 16 * 4)
                    w, x = fw1[0:33, :], zfeat[0:33, :]
                else:
                    pe.wait_ge(s("filter_sin"), j)
                    w, x = fw2[0:HD, j - 1, :], hdn[0:HD, :]
                mm(ps[0:HD, 6, 0:T], w, x, start=True, stop=True).then_inc(s("filter_layer"), 1)

            def filter_taps(half, t0):
                r = 2 * half + t0
                if r == 0:
                    pe.wait_ge(s("hyena_loaded"), 16 * 3)
                else:
                    pe.wait_ge(s("taps_ready"), r)
                if half and t0 == 0:
                    pe.wait_ge(s("spec_stored"), 2)
                for d in range(2):
                    ins = mm(ps[:, 6 + d, :], hdn[0:HD, t0 * P:(t0 + 1) * P],
                             fwo[0:HD, d * D + half * 512:d * D + half * 512 + 512], start=True, stop=True)
                ins.then_inc(s("filter_taps"), 1)

            def filter_spec(half, kind):
                pe.wait_ge(s("taps_ready"), 2 * half + 2)
                pe.wait_ge(s("hyena_loaded"), 16 * 3)
                if kind:
                    pe.wait_ge(s("spec_stored"), 2 * half + 1)
                for k in range(2):
                    for t0 in range(TT):
                        ins = mm(ps[:, 6 + k, :], dft[:, t0, (2 * kind + k) * P:(2 * kind + k + 1) * P],
                                 (tapf if kind else taps)[:, t0, :], start=t0 == 0, stop=t0 == 1)
                ins.then_inc(s("filter_spec"), 1)

            pe.wait_ge(s("c_silu"), 1)
            for g in range(4):
                modulation(g)

            sum_squares("x", 4)
            sum_squares("ctx", 5, src=y)
            lat, con_x = (uhi, ulo), (ctx_hi, ctx_lo)

            def rope(r):
                pe.wait_ge(s("qkv_drained"), r + 1)
                if r >= 2:
                    pe.wait_ge(s("rope_drained"), r - 1)
                src = kbuf[:, 2 * r:2 * r + 2, T:2 * T] if r < 4 else qbuf[:, 2 * (r - 4):2 * (r - 4) + 2, :]
                mm(ps[:, 4 + r % 2, :], rot, src, start=True, stop=True).then_inc(s("roped"), 1)

            pe.wait_ge(*nth("ctx", "lo", 2))
            pe.wait_ge(*nth("x", "std", 1))
            pe.wait_ge(*nth("ctx", "std", 1))
            for g in range(12):
                i = I_QKV + g
                b = 2 * (g % 2)
                if g >= 2:
                    pe.wait_ge(s("qkv_drained"), g - 1)
                weights_ready(i)
                if g < 4:
                    ins = tiles(i, lambda m, x_i: ps[:, b + m, x_i * T:(x_i + 1) * T], [con_x, lat],
                                x_wait="x" if g == 0 else None)
                elif g < 8:
                    ins = tiles(i, lambda m, _: ps[:, b, m * T:(m + 1) * T], [lat])
                else:
                    ins = by_token(i, lambda tt: ps[:, b + tt // 2, (tt % 2) * 256:(tt % 2) * 256 + 256], [con_x, lat])
                used(ins)
                if 1 <= g <= 8:
                    rope(g - 1)
                if g >= 9:
                    filter_layer(g - 9)

            def scores(u):
                hd, qt = divmod(u, 2)
                if u >= 2:
                    pe.wait_ge(s("exps"), u - 1)
                for p in range(2):
                    a = slice(p * HD, (p + 1) * HD)
                    ins = mm(ps[:, 2 * (u % 2) + p, :], qbuf[a, hd, qt * P:(qt + 1) * P], kbuf[a, hd, :], start=True, stop=True)
                ins.then_inc(s("scores"), 1)

            def turn_weights(u):
                pe.wait_ge(s("att_ready"), u + 1)
                if u >= 2:
                    pe.wait_ge(s("att_copied"), u - 1)
                for k in range(4):
                    ins = nc.tensor.transpose(ps[:, 4 + u % 2, k * P:(k + 1) * P], ebuf[:, u % 2, 0, k * P:(k + 1) * P], ident)
                ins.then_inc(s("att_turned"), 1)

            def values(hd):
                pe.wait_ge(s("att_copied"), 2 * hd + 2)
                if hd:
                    pe.wait_ge(s("o_copied"), hd)
                for k in range(4):
                    ins = mm(ps[:, 6, 0:T], vbuf[:, k, hd * P:(hd + 1) * P], atb[:, hd % 2, k, :], start=k == 0, stop=k == 3)
                ins.then_inc(s("o_ready"), 1)

            pe.wait_ge(s("roped_all"), 8)
            pe.wait_ge(s("qkv_drained"), 12)
            pe.wait_ge(s("filter_arg"), 3)
            for u in range(2 * HEADS + 3):
                if u < 2 * HEADS:
                    scores(u)
                    modulation(4 + u)
                if 1 <= u <= 2 * HEADS:
                    turn_weights(u - 1)
                if u >= 3 and u % 2:
                    values((u - 3) // 2)
            for c in range(4):
                pe.wait_ge(s("o_squares"), 2 * c + 2)
                pe.wait_ge(s("exps"), 16)
                mm(ps[:, c, :], ones, sq[:, 2 * c:2 * c + 2, :], start=True, stop=True).then_inc(s("o_sumsq"), 1)

            def out_rows(tag, i0, xs=(uhi, ulo), x_wait=None, wait_each=None):
                for g in range(4):
                    weights_ready(i0 + g)
                    used(tiles(i0 + g, lambda m, _: ps[:, g, m * T:(m + 1) * T], [xs], x_wait=x_wait if g == 0 else None))
                sum_squares(tag, 4, counts=4)

            for c in range(4):
                pe.wait_ge(s("o_std"), c + 1)
            pe.wait_ge(s("o_lo"), 4)
            out_rows("post0", I_AO)

            def mlp(layer, tag, i0):
                sum_squares(tag + "_in", 5)
                if layer == 0:
                    modulation(20)
                    modulation(21)
                with pe.Fori(0, 5) as n:
                    for g in range(3):
                        pe.wait_ge(*mlp_nth(tag, "free", up(g + 1, n, 3)))
                        weights_ready(i0 + g, n, 3)
                        used(tiles(i0 + g, lambda m, _: ps[:, g, m * T:(m + 1) * T], [(uhi, ulo)], x_wait=tag + "_in" if g == 0 else None))
                pe.wait_ge(*mlp_nth(tag, "free", 16))
                weights_ready(i0 + 15)
                used(tiles(i0 + 15, lambda m, _: ps[:, 0, m * T:(m + 1) * T], [(uhi, ulo)]))
                pe.wait_ge(*mlp_nth(tag, "free", 19))
                for g in range(16):
                    m0, kg = divmod(g, 4)
                    if kg == 0:
                        pe.wait_ge(*mlp_nth(tag, "yfree", m0 + 1))
                    if m0 == 0:
                        pe.wait_ge(*mlp_nth(tag, "hidden", 4 * kg + 4))
                    weights_ready(i0 + 16 + g)
                    used(tiles(i0 + 16 + g, lambda m, _: ps[:, 2 * (m0 % 2) + m, 0:T], [(hid_hi, hid_lo)], k0=8 * kg,
                               first=kg == 0, last=kg == 3))
                sum_squares(tag, 4, counts=4)

            if on("mlp0"):
                mlp(0, "mlp0", I_MLP0)

            def turn_v(j):
                pe.wait_ge(s("v_ready"), j + 1)
                if j >= 2:
                    pe.wait_ge(s("vtok_stored"), j - 1)
                for m in range(2):
                    for t0 in range(TT):
                        ins = nc.tensor.transpose(ps[:, 4 + j % 2, (2 * m + t0) * P:(2 * m + t0 + 1) * P],
                                                  hv[:, 2 * j + m, t0 * P:(t0 + 1) * P], ident)
                ins.then_inc(s("v_turned"), 1)

            if on("hyena"):
                sum_squares("hy_in", 5)
                modulation(22)
                modulation(23)
                for g in range(12):
                    if g >= 4:
                        pe.wait_ge(s("hy_drained"), g - 3)
                    weights_ready(I_HY + g)
                    used(tiles(I_HY + g, lambda m, _: ps[:, g % 4, m * T:(m + 1) * T], [(uhi, ulo)], x_wait="hy_in" if g == 0 else None))
                    if g == 0:
                        pe.wait_ge(s("mod_drained"), 24)
                    if g in (1, 2, 6, 7):
                        filter_taps(g // 6, (g - 1) % 5)
                    if g in (4, 5, 9, 10):
                        filter_spec(g // 9, (g - 4) % 5)
                    if 6 <= g <= 9:
                        turn_v(g - 6)
                pe.wait_ge(s("hy_drained"), 12)
                pe.wait_ge(s("vtok_stored"), 4)
                for half in range(2):
                    if half:
                        pe.wait_ge(s("vspec_used"), 1)
                    for k in range(4):
                        for t0 in range(TT):
                            ins = mm(ps[:, k, :], dft[:, t0, k * P:(k + 1) * P], vtok[:, t0, half * 512:half * 512 + 512],
                                     start=t0 == 0, stop=t0 == 1)
                    ins.then_inc(s("vspec"), 1)
                    pe.wait_ge(s("yspec_ready"), half + 1)
                    if half:
                        pe.wait_ge(s("conv_taken"), 4)
                    else:
                        pe.wait_ge(s("spec_stored"), 4)
                    for m in range(4):
                        for k in range(4):
                            ins = mm(ps[:, 4 + m, 0:T], yspec[:, k, m * P:(m + 1) * P], idft[:, k, :], start=k == 0, stop=k == 3)
                        ins.then_inc(s("conv"), 1)
                pe.wait_ge(s("vspec_used"), 2)
                out_rows("post1", I_HO, x_wait="hy")
            if on("mlp1"):
                mlp(1, "mlp1", I_MLP1)

            u_parts = (uhi, ulo)

            def compress():
                pe.wait_ge(s("blocks_ready"), 1)
                pe.wait_ge(s("cmp_loaded"), 16 * 2)
                for g in range(2):
                    a = slice(g * HD, (g + 1) * HD)
                    for c in range(2):
                        for l in range(CMP_LEN):
                            ins = mm(ps[a, 4, 16 * c:16 * c + NCMP], w1c[a, c, l * HD:(l + 1) * HD], blocks[a, c, l, :],
                                     start=l == 0, stop=l == CMP_LEN - 1)
                ins.then_inc(s("cmp_hidden"), 1)

            def compress_out():
                pe.wait_ge(s("cmp_gelu"), 1)
                for g in range(2):
                    a = slice(g * HD, (g + 1) * HD)
                    mm(ps[a, 5, 0:NCMP], w2c[a, 0, :], hidc[a, 0, 0:NCMP], start=True, stop=True)
                    ins = mm(ps[0:NCMP, 6 + g, 0:HD], hidc[a, 1, 0:NCMP], w2c[a, 1, :], start=True, stop=True)
                ins.then_inc(s("cmp_out"), 1)

            def head(u):
                return u // 4, (u // 2) % 2, u % 2

            def nsa_scores(u):
                j, g, qt = head(u)
                a = slice(g * HD, (g + 1) * HD)
                if u >= 2:
                    pe.wait_ge(s("nsa_exps"), u - 1)
                for b in range(2):
                    ins = mm(ps[:, u % 2, b * T:b * T + (qt + 1) * P], qn[a, j, qt * P:(qt + 1) * P], ksw[a, b, 0:(qt + 1) * P],
                             start=True, stop=True)
                ins.then_inc(s("nsa_scores"), 1)

            def nsa_turn(u):
                j, g, qt = head(u)
                pe.wait_ge(s("nsa_weights"), u + 1)
                if u >= 2:
                    pe.wait_ge(s("nsa_copied"), u - 1)
                for b in range(2):
                    for k in range(qt + 1):
                        n = b * (qt + 1) + k
                        ins = nc.tensor.transpose(ps[:, 2 + u % 2, n * P:(n + 1) * P], nsa_e[:, u % 2, b, k * P:(k + 1) * P], ident)
                ins.then_inc(s("nsa_turned"), 1)

            def nsa_values(u):
                j, g, qt = head(u)
                pe.wait_ge(s("nsa_copied"), u + 1)
                if u % 4 == 0 and j >= 2:
                    pe.wait_ge(s("nsa_out_lo"), j - 1)
                o = ps[g * HD:(g + 1) * HD, 4 + j % 2, qt * P:(qt + 1) * P]
                for b in range(2):
                    for k in range(qt + 1):
                        n = b * (qt + 1) + k
                        mm(o, vsw[:, k, b * P + g * HD:b * P + (g + 1) * HD], nsa_t[:, 2 * (u % 2) + n // 2, (n % 2) * P:(n % 2 + 1) * P],
                           start=n == 0, stop=False)
                mm(o, vc[0:NCMP, g * HD:(g + 1) * HD], cmp_t[:, qt * 8 + g * 4 + j, :], start=False, stop=True).then_inc(s("nsa_out"), 1)

            if on("mixer"):
                sum_squares("mix_in", 5)
                for g in range(16):
                    i = I_PROJ + g
                    if g >= 4:
                        pe.wait_ge(s("proj_drained"), g - 3)
                    weights_ready(i)
                    if g in (4, 12, 13):
                        ins = by_token(i, lambda tt: ps[:, g % 4, tt * 256:tt * 256 + 256], [u_parts])
                    elif g == 5:
                        ins = by_token(i, lambda tt: ps[:, g % 4, tt * 256:tt * 256 + 24], [u_parts], 24)
                    else:
                        ins = tiles(i, lambda m, _: ps[:, g % 4, m * T:(m + 1) * T], [u_parts], x_wait="mix_in" if g == 0 else None)
                    used(ins)
                    if g == 2:
                        compress()
                    if g == 4:
                        compress_out()
                pe.wait_ge(s("v_normed"), 1)
                pe.wait_ge(s("cmp_stored"), 1)
                for n in range(TT):
                    for g in range(MT):
                        ins = mm(ps[:, 4 + g // 2, (g % 2) * T + n * P:(g % 2) * T + (n + 1) * P], vg[:, n, g * P:(g + 1) * P], gmw[:, g, :],
                                 start=True, stop=True)
                ins.then_inc(s("gm_mixed"), 1)
                pe.wait_ge(s("pooled"), 1)
                for g in range(MT):
                    ins = mm(ps[:, 6 + g // 2, (g % 2) * T:(g % 2 + 1) * T], poolw[:, g, :], xd[:, g, 16:16 + T], start=True, stop=True)
                ins.then_inc(s("pool_mapped"), 1)
                pe.wait_ge(s("rec_conved"), 1)
                pe.wait_ge(s("lru_loaded"), 16 * 4)
                pe.wait_ge(s("proj_drained"), 16)
                for w in range(2):
                    for m in range(MT):
                        ins = mm(ps[:, 2 * w + m // 2, (m % 2) * T:(m % 2 + 1) * T], lruw[:, w, m, :], sq[:, m, :], start=True, stop=True)
                ins.then_inc(s("rec_gates"), 1)
                pe.wait_ge(s("lru_done"), 1)
                pe.wait_ge(s("pool_lo"), 1)
                pe.wait_ge(s("gm_lo"), 1)
                for qt in range(2):
                    for g in range(2):
                        a = slice(g * HD, (g + 1) * HD)
                        for j in range(4):
                            ins = mm(ps[:, 4 + 2 * qt + g, 16 * j:16 * j + NCMP], qn[a, j, qt * P:(qt + 1) * P], kc[a, 0:NCMP], start=True, stop=True)
                ins.then_inc(s("cmp_scores"), 1)
                pe.wait_ge(s("cmp_weights"), 1)
                for u in range(16):
                    ins = nc.tensor.transpose(ps[0:NCMP, u // 4, (u % 4) * P:(u % 4 + 1) * P], cmp_p[:, u // 8, u % 8, :], ident)
                ins.then_inc(s("cmp_turned"), 1)
                pe.wait_ge(s("cmp_t_ready"), 1)
                for u in range(19):
                    if u < 16:
                        nsa_scores(u)
                    if 1 <= u <= 16:
                        nsa_turn(u - 1)
                    if 3 <= u:
                        nsa_values(u - 3)
                pe.wait_ge(s("nsa_out_lo"), 4)
                pe.wait_ge(s("nsa_out_hi"), 4)
                with pe.Fori(0, 4) as n:
                    for g in range(6):
                        i = I_BR + g
                        if g < 4:
                            pe.wait_ge(s("mg_free"), up(g + 1, n, 4))
                        else:
                            pe.wait_ge(s("br_free"), up(g - 3, n, 2))
                        weights_ready(i, n, 6)
                        if g < 4:
                            used(tiles(i, lambda m, _: ps[:, g, m * T:(m + 1) * T], [u_parts]))
                        else:
                            w = i % RING
                            for m in range(4):
                                o = ps[:, 2 * g - 4 + m // 2, (m % 2) * T:(m % 2 + 1) * T]
                                for k in range(MT):
                                    x0, x1 = (v[:, bass.ds(n * MT + k, 1), :].rearrange("p a t -> p (a t)") for v in (yhi, ylo))
                                    c = k * 512 + m * P
                                    ins = three(o, whi[:, w, c:c + P], wlo[:, w, c:c + P], x0, x1, k == 0, k == MT - 1)
                            used(ins)
                pe.wait_ge(s("mg_free"), 20)
                for g in range(4):
                    weights_ready(I_WO + g)
                    used(tiles(I_WO + g, lambda m, _: ps[:, g, m * T:(m + 1) * T], [u_parts], x_wait="merged" if g == 0 else None))

            if on("all"):
                sum_squares("moe_in", 5)
                pe.wait_ge(*nth("moe_in", "lo", 2))
                pe.wait_ge(s("router_lo"), 1)
                for t0 in range(TT):
                    for k in range(KT):
                        a0, a1 = (x[:, k, t0 * P:(t0 + 1) * P] for x in u_parts)
                        ins = three_rows(mm, ps[:, 4, t0 * 32:t0 * 32 + 20], a0, a1, wrhi[:, k, :], wrlo[:, k, :], k == 0, k == KT - 1)
                ins.then_inc(s("router"), 1)
                pe.wait_ge(*nth("mixed", "h", 2))

                def up_rows(i, bank, n=None):
                    weights_ready(i, n, 6)
                    used(tiles(i, lambda m, _: ps[:, bank, m * T:(m + 1) * T], [u_parts]))

                def down_rows(i, j, n=None):
                    if n is None:
                        pe.wait_ge(s("moe_hid"), 2 * EXPERTS)
                        pe.wait_ge(s("moe_free"), 2 * EXPERTS - 2 + j + 1)
                    else:
                        pe.wait_ge(s("moe_hid"), n * 2 + 2)
                        pe.wait_ge(s("moe_free"), n * 2 + (j + 1))
                    weights_ready(i, n, 6)
                    used(tiles(i, lambda m, _: ps[:, 4 + 2 * j + m // 2, (m % 2) * T:(m % 2 + 1) * T], [(ehi, elo)], kts=4, width=4))

                for j in range(4):
                    up_rows(I_MOE + j, j)
                pe.wait_ge(s("combine_ready"), 1)
                for t0 in range(TT):
                    ins = nc.tensor.transpose(ps[0:EXPERTS, 5, t0 * P:(t0 + 1) * P], cb[:, t0, :], ident)
                ins.then_inc(s("combine_turned"), 1)
                pe.wait_ge(s("combine_copied"), 1)
                for e in range(EXPERTS):
                    if e >= 8 and e % 2 == 0:
                        pe.wait_ge(s("comb_stored"), (e - 8) // 2 + 1)
                    ins = mm(ps[:, 4 + (e // 2) % 4, (e % 2) * T:(e % 2 + 1) * T], ident[0:EXPERTS, e:e + 1].to_broadcast([EXPERTS, P]),
                             cbt[0:EXPERTS, :], start=True, stop=True)
                    if e % 2:
                        ins.then_inc(s("comb_spread"), 1)
                with pe.Fori(0, EXPERTS - 1) as n:
                    i = I_MOE + 4
                    for j in range(2):
                        pe.wait_ge(s("moe_silu"), n * 2 + (j + 1))
                        up_rows(i + j, j, n)
                    for j in range(2):
                        down_rows(i + 2 + j, j, n)
                    for j in range(2):
                        pe.wait_ge(s("moe_gated"), n * 2 + (j + 1))
                        up_rows(i + 4 + j, 2 + j, n)
                for j in range(2):
                    down_rows(N_CHUNKS - 2 + j, j)
                sum_squares("final", 0)

        @block.scalar
        def _(act):
            fn = nc.scalar.activation
            for dst, src in [(cvec[:], A["cvec"]), (con[:], A["const"]), (par[:], A["params"]),
                             (lamv, A["attn_lambda"].partition_broadcast(P))]:
                act.dma_start(dst, src).then_inc(s("small_loaded"), 16)
            act.dma_start(h[:], A["x"]).then_inc(s("x_loaded"), 16)
            act.dma_start(ctx[:], A["ctx"]).then_inc(s("x_loaded"), 16)

            def split(i, n=None, step=0):
                if i >= n_chunks and n is None:
                    return
                sl = i % RING
                act.wait_ge(s(f"raw_loaded{sl}"), up(16 * (i // RING + 1), n, 16 * step // RING))
                if i >= RING:
                    act.wait_ge(s("chunk_used"), up(i - RING + 1, n, step))
                fn(whi[:, sl, :], raw[:, sl, :], ACT.Copy).then_inc(s("hi_ready"), 1)

            def product(i, n=None, step=0):
                act.wait_ge(s("chunk_used"), up(i + 1, n, step))

            chain = Chain(act, "act_chain")
            eps = ccol("eps")

            def squares(tag, src, dst=sq):
                for c in range(2):
                    fn(dst[:, 4 * c:4 * c + 4, :], src[:, 4 * c:4 * c + 4, :], ACT.Square).then_inc(s("squares"), 1)

            def root(tag, bank):
                act.wait_ge(*nth(tag, "sumsq", 1))
                fn(std[:], ps[:, bank, 0:T], ACT.Sqrt, bias=eps, scale=1.0 / D).then_inc(s("std"), 1)

            def high(tag, src, dst):
                for c in range(2):
                    act.wait_ge(*nth(tag, "normed", c + 1))
                    fn(dst[:, 4 * c:4 * c + 4, :], src[:, 4 * c:4 * c + 4, :], ACT.Copy).then_inc(s("hi"), 1)

            def next_squares(tag, prev):
                for c in range(2):
                    act.wait_ge(*nth(prev, "h", c + 1))
                    fn(sq[:, 4 * c:4 * c + 4, :], h[:, 4 * c:4 * c + 4, :], ACT.Square).then_inc(s("squares"), 1)

            act.wait_ge(s("small_loaded"), 16 * 4)
            fn(csil[:], cvec[:], ACT.Tanh, scale=0.5).then_inc(s("c_tanh"), 1)
            act.wait_ge(s("x_loaded"), 32)
            act.wait_ge(s("lam_sums"), 1)
            for i in range(RING):
                split(i)
            squares("x", h)
            squares("ctx", ctx, y)
            root("x", 4)
            high("x", y, uhi)
            root("ctx", 5)
            high("ctx", ctx, ctx_hi)

            def filter_sin(j):
                act.wait_ge(s("filter_arg"), j + 1)
                fn(hdn[0:HD, :], farg[0:HD, :], ACT.Sin).then_inc(s("filter_sin"), 1)

            act.wait_ge(*nth("x", "lo", 2))
            for dst, src in [(zfeat[0:33, :], A["zfeat"]), (fw1[0:33, :], A["hy_filt_w1"]), (fw2[0:HD], A["hy_filt_w2"]),
                             (fpar[0:HD, :], A["fpar"])]:
                act.dma_start(dst, src).then_inc(s("filter_loaded"), 16)
            for g in range(12):
                i = I_QKV + g
                b = 2 * (g % 2)
                product(i)
                if g < 4:
                    ins = fn(kbuf[:, 2 * g:2 * g + 2, :], ps[:, b:b + 2, :], ACT.Copy)
                elif g < 8:
                    ins = fn(qbuf[:, 2 * (g - 4):2 * (g - 4) + 2, :], ps[:, b, :].rearrange("p (m t) -> p m t", m=2), ACT.Copy)
                else:
                    v0 = (g - 8) * 256
                    ins = fn(vbuf[:, :, v0:v0 + 256], ps[:, b:b + 2, :].rearrange("p b (t c) -> p (b t) c", t=2), ACT.Copy)
                ins.then_inc(s("qkv_drained"), 1)
                split(i + RING)
                if g >= 10:
                    filter_sin(g - 10)
            filter_sin(2)

            def exps(u):
                act.wait_ge(s("max_ready"), u + 1)
                if u >= 2:
                    act.wait_ge(s("att_turned"), u - 1)
                for p in range(2):
                    ins = fn(ebuf[:, u % 2, p, :], ps[:, 2 * (u % 2) + p, :], ACT.Exp, scale=SCALE,
                             bias=small[:, 4 * (u % 2) + p:4 * (u % 2) + p + 1],
                             accum_out=small[:, 8 + 4 * (u % 2) + p:9 + 4 * (u % 2) + p])
                ins.then_inc(s("exps"), 1)

            fn(small[:, 24:26], small[:, 22:24], ACT.Exp).then_inc(s("lam_exps"), 1)
            for u in range(2 * HEADS + 3):
                if u < 2 * HEADS:
                    exps(u)
                if 1 <= u <= 2 * HEADS:
                    v = u - 1
                    act.wait_ge(s("att_turned"), v + 1)
                    if v >= 4:
                        act.wait_ge(s("o_ready"), v // 2 - 1)
                    fn(atb[:, (v // 2) % 2, :, (v % 2) * P:(v % 2 + 1) * P], ps[:, 4 + v % 2, :].rearrange("p (k q) -> p k q", k=4),
                       ACT.Copy).then_inc(s("att_copied"), 1)
                if u >= 3 and u % 2:
                    hd = (u - 3) // 2
                    act.wait_ge(s("o_ready"), hd + 1)
                    fn(sq[:, hd, :], ps[:, 6, 0:T], ACT.Square).then_inc(s("o_squares"), 1)
                    fn(obuf[:, hd, :], ps[:, 6, 0:T], ACT.Copy).then_inc(s("o_copied"), 1)
            for c in range(4):
                act.wait_ge(s("o_sumsq"), c + 1)
                fn(y[:, 2 * c:2 * c + 2, :], ps[:, c, :].rearrange("p (m t) -> p m t", m=2), ACT.Sqrt, bias=eps, scale=1.0 / P).then_inc(s("o_std"), 1)
            for c in range(4):
                act.wait_ge(s("o_normed"), c + 1)
                fn(uhi[:, 2 * c:2 * c + 2, :], obuf[:, 2 * c:2 * c + 2, :], ACT.Copy).then_inc(s("o_hi"), 1)

            def take_rows(tag, i0, bias=None):
                for g in range(4):
                    product(i0 + g)
                    dst = slice(2 * g, 2 * g + 2)
                    if bias is None:
                        src = ps[:, g, :].rearrange("p (m t) -> p m t", m=2)
                        fn(y[:, dst, :], src, ACT.Copy)
                        fn(sq[:, dst, :], src, ACT.Square).then_inc(s("squares"), 1)
                    else:
                        for m in range(2):
                            b = pcol(bias, 2 * g + m, 1)
                            fn(y[:, 2 * g + m, :], ps[:, g, m * T:(m + 1) * T], ACT.Identity, bias=b)
                            ins = fn(sq[:, 2 * g + m, :], ps[:, g, m * T:(m + 1) * T], ACT.Square, bias=b)
                        ins.then_inc(s("squares"), 1)
                    split(i0 + g + RING)

            take_rows("post0", I_AO)
            root("post0", 4)

            def relu_squared(tag, g, c, n=None, step=0):
                act.wait_ge(*mlp_nth(tag, "rfree", up(c + 1, n, step)))
                r = y[:, 2 * g:2 * g + 2, :]
                chain(fn(r, ps[:, g, :].rearrange("p (m t) -> p m t", m=2), ACT.Relu))
                act.sem_inc(s("mlp_free"), 1)
                dst = hid_hi[:, 2 * c:2 * c + 2, :] if n is None else hid_hi[:, bass.ds(n * (2 * step) + 2 * c, 2), :]
                fn(dst, r, ACT.Square).then_inc(s("mlp_hid_hi"), 1)

            def mlp(layer, tag, i0, prev):
                next_squares(tag + "_in", prev)
                root(tag + "_in", 5)
                high(tag + "_in", y, uhi)
                act.drain().then_inc(s("mlp_free"), 3)
                with act.Fori(0, 5) as n:
                    chain.enter(n, 3)
                    for g in range(3):
                        product(i0 + g, n, 3)
                        relu_squared(tag, g, g, n, 3)
                        split(i0 + g + RING, n, 3)
                chain.leave(5)
                product(i0 + 15)
                relu_squared(tag, 0, 15)
                split(i0 + 15 + RING)
                act.drain().then_inc(s("mlp_yfree"), 2)
                act.wait_ge(*mlp_nth(tag, "hidden", 16))
                for g in range(16):
                    m0, kg = divmod(g, 4)
                    product(i0 + 16 + g)
                    if kg == 3:
                        src = ps[:, 2 * (m0 % 2):2 * (m0 % 2) + 2, 0:T]
                        fn(y[:, 2 * m0:2 * m0 + 2, :], src, ACT.Copy)
                        fn(sq[:, 2 * m0:2 * m0 + 2, :], src, ACT.Square).then_inc(s("squares"), 1)
                        act.drain().then_inc(s("mlp_yfree"), 1)
                    split(i0 + 16 + g + RING)
                root(tag, 4)

            if on("mlp0"):
                mlp(0, "mlp0", I_MLP0, "post0")

            def store_spec(half, kind):
                act.wait_ge(s("filter_spec"), 2 * half + kind + 1)
                fn(spec[:, 2 * kind:2 * kind + 2, half * 512:half * 512 + 512], ps[:, 6:8, :], ACT.Copy).then_inc(s("spec_stored"), 1)

            def turned(j):
                act.wait_ge(s("v_turned"), j + 1)
                fn(vtok[:, :, 2 * j * P:(2 * j + 2) * P].rearrange("p t (m c) -> p m t c", m=2),
                   ps[:, 4 + j % 2, :].rearrange("p (m t c) -> p m t c", m=2, t=TT), ACT.Copy).then_inc(s("vtok_stored"), 1)

            if on("hyena"):
                for dst, src in [(fwo[0:HD, :], A["hy_filt_w_out"]), (dft[:], A["dft"]), (idft[:], A["idft"])]:
                    act.dma_start(dst, src).then_inc(s("hyena_loaded"), 16)
                next_squares("hy_in", "mlp0")
                root("hy_in", 5)
                high("hy_in", y, uhi)
                act.wait_ge(*nth("hy_in", "lo", 2))
                act.dma_start(y[:].rearrange("p a c -> p (a c)"), A["decay"].rearrange("p t c -> p (t c)")).then_inc(s("decay_loaded"), 16)
                for g in range(12):
                    product(I_HY + g)
                    if g == 0:
                        act.wait_ge(s("zpad_clear"), 1)
                    if g >= 2:
                        act.wait_ge(s("hy_conved"), g - 1)
                    first = (16, 8, 0)[g // 4] + 2 * (g % 4)
                    for m in range(2):
                        ins = fn(zpad[:, g % 2, m, 1:T + 1], ps[:, g % 4, m * T:(m + 1) * T], ACT.Identity, bias=pcol("hy_b_in", first + m, 1))
                    ins.then_inc(s("hy_drained"), 1)
                    split(I_HY + g + RING)
                    if g in (5, 6, 10, 11):
                        store_spec(g // 10, (g - 5) % 5)
                    if 7 <= g <= 10:
                        turned(g - 7)
                for half in range(2):
                    a = slice(4 * half, 4 * half + 4)
                    act.wait_ge(*nth("hy", "normed", half + 1))
                    fn(uhi[:, a, :], hv[:, a, :], ACT.Copy).then_inc(s("hi"), 1)
                take_rows("post1", I_HO, "hy_b_out")
                root("post1", 4)
            if on("mlp1"):
                mlp(1, "mlp1", I_MLP1, "post1")

            def halves(m):
                return m.rearrange("p (m t) -> p m t", m=2)

            def head(u):
                return u // 4, (u // 2) % 2, u % 2

            def part(name, b, src):
                act.wait_ge(s(name + "_ready"), 1)
                fn(yhi[:, b:b + MT, :], src, ACT.Copy).then_inc(s(name + "_hi"), 1)

            if on("mixer"):
                for dst, src in [(w1c[:], A["cmp_w1"]), (w2c[:], A["cmp_w2"])]:
                    act.dma_start(dst, src).then_inc(s("cmp_loaded"), 16)
                act.wait_ge(s("lru_clear"), 1)
                for dst, src in [(conb[:], A["const_b"]), (cpe[:], A["cmp_pe"]), (gmw[:], A["gm_ws"]),
                                 (gmb[:].rearrange("p a b -> p (a b)"), A["gm_b"].partition_broadcast(P)), (poolw[:], A["pool_w"])]:
                    act.dma_start(dst, src).then_inc(s("mixer_loaded"), 16)
                for w, name in enumerate(("lru_wa", "lru_wx")):
                    for o in range(2):
                        act.dma_start(lruw[o * HD:(o + 1) * HD, w, :, o * HD:(o + 1) * HD], A[name][o]).then_inc(s("lru_loaded"), 16)
                next_squares("mix_in", "mlp1")
                root("mix_in", 5)
                high("mix_in", y, uhi)
                act.wait_ge(s("lam_abs"), 1)
                fn(lru[:, 1, :], lru[:, 0, :], ACT.Exp, scale=-1.0).then_inc(s("lam_exp"), 1)
                for g in range(16):
                    if g:
                        product(I_PROJ + g)
                    src = ps[:, g % 4, :]
                    a = slice(2 * (g % 2), 2 * (g % 2) + 2)
                    if g == 0:
                        act.wait_ge(s("blocks_ready"), 1)
                        act.sem_inc(s("proj_drained"), 1)
                    elif g == 1:
                        fn(ksw[:], halves(src), ACT.Copy).then_inc(s("proj_drained"), 1)
                    elif g in (2, 3):
                        fn(qn[:, a, :], halves(src), ACT.Copy).then_inc(s("proj_drained"), 1)
                    elif g == 4:
                        fn(vsw[:], halves(src), ACT.Copy).then_inc(s("proj_drained"), 1)
                    elif g == 5:
                        fn(gates[:], halves(src)[:, :, 0:24], ACT.Tanh, scale=0.5).then_inc(s("proj_drained"), 1)
                    elif g in (6, 7):
                        fn(rec[:, a, 3:3 + T], halves(src), ACT.Copy).then_inc(s("proj_drained"), 1)
                    elif g in (8, 9):
                        fn(gate[:, a, :], halves(src), ACT.Gelu_apprx_tanh).then_inc(s("proj_drained"), 1)
                    elif g in (10, 11):
                        fn(xd[:, a, 16:16 + T], halves(src), ACT.Copy).then_inc(s("proj_drained"), 1)
                    elif g in (12, 13):
                        fn(vg[:, :, (g - 12) * 256:(g - 12) * 256 + 256], halves(src), ACT.Gelu_apprx_tanh).then_inc(s("proj_drained"), 1)
                    else:
                        fn(ug[:, a, :], halves(src), ACT.Gelu_apprx_tanh).then_inc(s("proj_drained"), 1)
                    split(I_PROJ + g + RING)
                    if g == 3:
                        act.wait_ge(s("cmp_hidden"), 1)
                        fn(hidc[:, :, 0:NCMP], ps[:, 4, 0:32].rearrange("p (c n) -> p c n", c=2)[:, :, 0:NCMP], ACT.Gelu_apprx_tanh)\
                            .then_inc(s("cmp_gelu"), 1)
                    if g == 5:
                        act.wait_ge(s("cmp_out"), 1)
                        fn(kc[:, 0:NCMP], ps[:, 5, 0:NCMP], ACT.Copy)
                        fn(vc[0:NCMP, :].rearrange("p (g d) -> p g d", g=2), ps[0:NCMP, 6:8, 0:HD], ACT.Copy).then_inc(s("cmp_stored"), 1)
                act.wait_ge(s("proj_drained"), 16)
                for n in range(TT):
                    ins = fn(sq[:, 4 + 2 * n:6 + 2 * n, :].rearrange("p a c -> p (a c)"), vg[:, n, :], ACT.Square, accum_out=sm[:, n:n + 1])
                chain(ins)
                fn(sm[:, 2:4], sm[:, 0:2], ACT.Sqrt, bias=eps, scale=1.0 / MIX).then_inc(s("v_std"), 1)
                part("gm", slot_of[0], y[:, 0:MT, :])
                act.wait_ge(s("pool_mapped"), 1)
                for g in range(MT):
                    ins = fn(yhi[:, slot_of[3] + g, :], ps[:, 6 + g // 2, (g % 2) * T:(g % 2 + 1) * T], ACT.Copy, scale=pcol("pool_scale", g, 1))
                ins.then_inc(s("pool_hi"), 1)
                act.wait_ge(s("rec_gates"), 1)
                act.wait_ge(s("gm_lo"), 1)
                for w in range(2):
                    for m in range(MT):
                        ins = fn(y[:, 4 * w + m, :], ps[:, 2 * w + m // 2, (m % 2) * T:(m % 2 + 1) * T], ACT.Tanh, scale=0.5,
                                 bias=lru[:, 8 + w, m:m + 1])
                    ins.then_inc(s("rec_tanh"), 1)
                act.wait_ge(s("rec_rate"), 1)
                fn(rec[:, :, 0:T], y[:, 0:4, :], ACT.Tanh).then_inc(s("rate_tanh"), 1)
                act.wait_ge(s("rate_tanh"), 1)
                fn(y[:, 0:4, :], y[:, 0:4, :], ACT.Exp, scale=-1.0).then_inc(s("decay_ready"), 1)
                act.wait_ge(s("rec_power"), 1)
                fn(rec[:, :, 0:T], rec[:, :, 0:T], ACT.Sqrt).then_inc(s("rec_root"), 1)
                part("lru", slot_of[1], rec[:, :, 0:T])
                act.wait_ge(s("cmp_shifted"), 1)
                fn(cmp_p, cmp_p, ACT.Exp, scale=SCALE).then_inc(s("cmp_exp"), 1)
                act.wait_ge(s("cmp_turned"), 1)
                fn(cmp_t, ps[0:NCMP, 0:4, :].rearrange("p b (u q) -> p (b u) q", u=4), ACT.Copy).then_inc(s("cmp_t_ready"), 1)
                for u in range(20):
                    if u < 16:
                        j, g, qt = head(u)
                        act.wait_ge(s("nsa_max"), u + 1)
                        if u >= 2:
                            act.wait_ge(s("nsa_turned"), u - 1)
                        for b in range(2):
                            w = 4 * (u % 2) + b
                            ins = fn(nsa_e[:, u % 2, b, 0:(qt + 1) * P], ps[:, u % 2, b * T:b * T + (qt + 1) * P], ACT.Exp, scale=SCALE,
                                     bias=sm[:, 8 + w:9 + w], accum_out=sm[:, 16 + w:17 + w])
                        ins.then_inc(s("nsa_exps"), 1)
                    if 1 <= u <= 16:
                        v = u - 1
                        n = 2 * (v % 2 + 1)
                        act.wait_ge(s("nsa_turned"), v + 1)
                        if v >= 2:
                            act.wait_ge(s("nsa_out"), v - 1)
                        fn(nsa_t[:, 2 * (v % 2):2 * (v % 2) + n // 2, :].rearrange("p a c -> p (a c)"), ps[:, 2 + v % 2, 0:n * P], ACT.Copy)\
                            .then_inc(s("nsa_copied"), 1)
                    if u >= 7 and (u - 3) % 4 == 0 or u == 19:
                        j = (u - 3) // 4 - 1
                        act.wait_ge(s("nsa_out"), 4 * j + 4)
                        fn(yhi[:, slot_of[2] + j, :], ps[:, 4 + j % 2, 0:T], ACT.Copy).then_inc(s("nsa_out_hi"), 1)
                act.drain().then_inc(s("mg_free"), 4)
                with act.Fori(0, 4) as n:
                    for g in range(6):
                        i = I_BR + g
                        product(i, n, 6)
                        if g < 4:
                            act.wait_ge(s("gated_free"), up(1 + g // 2, n, 2))
                            fn(gated[:, 2 * g:2 * g + 2, :], halves(ps[:, g, :]), ACT.Tanh, scale=0.5).then_inc(s("mg_tanh"), 1)
                            act.drain().then_inc(s("mg_free"), 1)
                        split(i + RING, n, 6)
                high("merged", y, uhi)
                for g in range(4):
                    product(I_WO + g)
                    split(I_WO + g + RING)

            if on("all"):
                for dst, src in [(wr[:], A["router_w"]), (rb[:], A["router_b"].partition_broadcast(P)), (order4[:], A["order4"])]:
                    act.dma_start(dst, src).then_inc(s("router_loaded"), 16)
                next_squares("moe_in", "mixed")
                root("moe_in", 5)
                act.wait_ge(s("router_loaded"), 48)
                fn(wrhi[:], wr[:], ACT.Copy).then_inc(s("router_hi"), 1)
                high("moe_in", y, uhi)
                act.wait_ge(s("group_shifted"), 1)
                fn(ro[:, 2], ro[:, 1], ACT.Exp).then_inc(s("group_exp"), 1)
                act.wait_ge(s("top_gap"), 1)
                fn(ro[:, 12, :, 0:1], ro[:, 11, :, 0:1], ACT.Exp).then_inc(s("top_exp"), 1)

                def silu(i, j, n=None):
                    product(i, n, 6)
                    if n is not None:
                        act.wait_ge(s("moe_gated"), n * 2 + (j + 1))
                    fn(sg[:, 2 * j:2 * j + 2, :], halves(ps[:, j, :]), ACT.Silu).then_inc(s("moe_silu"), 1)
                    split(i + RING, n, 6)

                def expert_high(j, n=None):
                    act.wait_ge(s("moe_weighted"), j + 1 if n is None else n * 2 + (j + 3))
                    fn(ehi[:, 2 * j:2 * j + 2, :], hmid[:, 2 * j:2 * j + 2, :], ACT.Copy).then_inc(s("moe_hi"), 1)

                for j in range(2):
                    silu(I_MOE + j, j)
                for j in range(2):
                    split(I_MOE + 2 + j + RING)
                act.wait_ge(s("combine_turned"), 1)
                fn(cbt[0:EXPERTS, :], ps[0:EXPERTS, 5, 0:T], ACT.Copy).then_inc(s("combine_copied"), 1)
                for e in range(EXPERTS // 2):
                    act.wait_ge(s("comb_spread"), e + 1)
                    fn(comb[:, 2 * e:2 * e + 2, :], halves(ps[:, 4 + e % 4, :]), ACT.Copy).then_inc(s("comb_stored"), 1)
                for j in range(2):
                    expert_high(j)
                with act.Fori(0, EXPERTS - 1) as n:
                    i = I_MOE + 4
                    for j in range(2):
                        silu(i + j, j, n)
                    for j in range(2):
                        product(i + 2 + j, n, 6)
                        split(i + 2 + j + RING, n, 6)
                    for j in range(2):
                        product(i + 4 + j, n, 6)
                        split(i + 4 + j + RING, n, 6)
                    for j in range(2):
                        expert_high(j, n)
                for j in range(2):
                    product(N_CHUNKS - 2 + j)
                next_squares("final", "moe")
                root("final", 0)

        @block.vector
        def _(dve):
            tt, ts, stt = nc.vector.tensor_tensor, nc.vector.tensor_scalar, nc.vector.scalar_tensor_tensor
            chain = Chain(dve, "dve_chain")

            def split(i, n=None, step=0):
                if i >= n_chunks and n is None:
                    return
                sl = i % RING
                dve.wait_ge(s("hi_ready"), up(i + 1, n, step))
                tt(wlo[:, sl, :], raw[:, sl, :], f32(whi[:, sl, :]), ALU.subtract).then_inc(s("lo_ready"), 1)

            def modulation(g):
                dve.wait_ge(s("mraw_used"), 4 * g + 4)
                tt(modv[:, 4 * g:4 * g + 4, :], ps[:, 7, 0:8].rearrange("p (m w) -> p m w", m=4),
                   over_cols(pcol("b_mod", 4 * g, 4), 2), ALU.add).then_inc(s("mod_drained"), 1)

            def scale_of(slot, gain, layer, part, who=0):
                chain(stt(coef[:, slot, :], mod_scale(layer, part, who), 1.0, gain, ALU.add, ALU.mult))

            def gate_of(slot, gain, layer, part):
                chain(tt(coef[:, slot, :], mod_scale(layer, part, 0), gain, ALU.mult))

            def low(tag, src, hi, lo):
                for c in range(2):
                    a = slice(4 * c, 4 * c + 4)
                    dve.wait_ge(*nth(tag, "hi", c + 1))
                    tt(lo[:, a, :], src[:, a, :], f32(hi[:, a, :]), ALU.subtract).then_inc(s("lo"), 1)

            def prenorm(tag, src, dst, slot, shift=None, gain=None):
                dve.wait_ge(*nth(tag, "std", 1))
                chain(nc.vector.reciprocal(rstd[:], std[:]))
                marks = [chain.tick(tt(dst[:, 4 * c:4 * c + 4, :], src[:, 4 * c:4 * c + 4, :], over_tiles(rstd[:], 4), ALU.mult))
                         for c in range(2)]
                for c in range(2):
                    dve.wait_ge(chain.sem, marks[c])
                    for k in range(4 * c, 4 * c + 4):
                        if shift is None:
                            ins = ts(dst[:, k, :], dst[:, k, :], pcol(gain, k, 1), None, ALU.mult)
                        else:
                            ins = ts(dst[:, k, :], dst[:, k, :], coef[:, slot, k:k + 1], shift[:, k:k + 1], ALU.mult, ALU.add)
                    ins.then_inc(s("normed"), 1)

            def postnorm(tag, slot):
                dve.wait_ge(*nth(tag, "std", 1))
                chain(nc.vector.reciprocal(rstd[:], std[:]))
                marks = []
                for c in range(2):
                    for k in range(4 * c, 4 * c + 4):
                        ins = stt(y[:, k, :], y[:, k, :], coef[:, slot, k:k + 1], rstd[:], ALU.mult, ALU.mult)
                    marks.append(chain.tick(ins))
                for c in range(2):
                    a = slice(4 * c, 4 * c + 4)
                    dve.wait_ge(chain.sem, marks[c])
                    tt(h[:, a, :], h[:, a, :], y[:, a, :], ALU.add).then_inc(s("h"), 1)

            dve.wait_ge(s("c_tanh"), 1)
            chain(stt(csil[:], csil[:], 1.0, cvec[:], ALU.add, ALU.mult))
            ts(csil[:], csil[:], 0.5, None, ALU.mult).then_inc(s("c_silu"), 1)
            lv = lamv.rearrange("p (a b d) -> p a b d", a=2, b=2)
            lp = sq[:, 6, 0:2 * HD].rearrange("p (a d) -> p a d", a=2)
            chain(tt(lp, lv[:, :, 0, :], lv[:, :, 1, :], ALU.mult))
            nc.vector.tensor_reduce(small[:, 22:24], lp, AX, ALU.add).then_inc(s("lam_sums"), 1)
            for i in range(RING):
                split(i)
            for g in range(4):
                modulation(g)
            dve.wait_ge(s("mod_drained"), 4)
            scale_of(0, pcol("mix_pre", 0, 8), 0, 1, 0)
            scale_of(1, pcol("mix_pre", 0, 8), 0, 1, 1)
            dve.wait_ge(*nth("ctx", "sumsq", 1))
            prenorm("x", h, y, 0, mod_scale(0, 0, 0))
            low("x", y, uhi, ulo)
            prenorm("ctx", ctx, ctx, 1, mod_scale(0, 0, 1))
            low("ctx", ctx, ctx_hi, ctx_lo)
            cosb, sinb = over_tiles(ccol("cos"), 2), over_tiles(ccol("sin"), 2)

            def rope(r):
                dve.wait_ge(s("roped"), r + 1)
                tmp = sq[:, 2 * (r % 2):2 * (r % 2) + 2, :]
                x = kbuf[:, 2 * r:2 * r + 2, T:2 * T] if r < 4 else qbuf[:, 2 * (r - 4):2 * (r - 4) + 2, :]
                tt(tmp, ps[:, 4 + r % 2, :].rearrange("p (m t) -> p m t", m=2), sinb, ALU.mult).then_inc(s("rope_drained"), 1)
                chain(tt(x, x, cosb, ALU.mult))
                dve.wait_ge(s("rope_drained"), r + 1)
                tt(x, x, tmp, ALU.add).then_inc(s("roped_all"), 1)

            def filter_argument(j):
                c1 = 6.28125
                c2 = 2.0 * math.pi - c1
                magic = 1.5 * 2.0 ** 23
                top = math.pi * (1 - 2.0 ** -23)
                a, r = farg[0:HD, :], frnd[0:HD, :]
                dve.wait_ge(s("filter_layer"), j + 1)
                if j:
                    dve.wait_ge(s("filter_sin"), j)
                chain(ts(a, ps[0:HD, 6, 0:T], fpar[0:HD, j:j + 1], fpar[0:HD, 3:4], ALU.add, ALU.mult))
                chain(ts(r, a, 1.0 / (2.0 * math.pi), magic, ALU.mult, ALU.add))
                chain(ts(r, r, magic, None, ALU.subtract))
                chain(stt(a, r, -c1, a, ALU.mult, ALU.add))
                chain(stt(a, r, -c2, a, ALU.mult, ALU.add))
                ts(a, a, top, -top, ALU.min, ALU.max).then_inc(s("filter_arg"), 1)

            for g in range(12):
                split(I_QKV + g + RING)
                if 1 <= g <= 8:
                    rope(g - 1)
                if g >= 10:
                    filter_argument(g - 10)
            filter_argument(2)

            def max_of(u):
                dve.wait_ge(s("scores"), u + 1)
                w = 4 * (u % 2)
                chain(nc.vector.tensor_reduce(small[:, w + 2:w + 4], ps[:, 2 * (u % 2):2 * (u % 2) + 2, :], AX, ALU.max))
                ts(small[:, w:w + 2], small[:, w + 2:w + 4], -SCALE, None, ALU.mult).then_inc(s("max_ready"), 1)

            def combine(u):
                dve.wait_ge(s("exps"), u + 1)
                w = 8 + 4 * (u % 2)
                r = small[:, w + 2:w + 4]
                e0, e1 = ebuf[:, u % 2, 0, :], ebuf[:, u % 2, 1, :]
                chain(nc.vector.reciprocal(r, small[:, w:w + 2]))
                a = chain.tick(ts(e0, e0, r[:, 0:1], None, ALU.mult))
                b = chain.tick(ts(e1, e1, r[:, 1:2], small[:, 26:27], ALU.mult, ALU.mult))
                dve.wait_ge(chain.sem, b)
                tt(e0, e0, e1, ALU.add).then_inc(s("att_ready"), 1)

            dve.wait_ge(s("lam_exps"), 1)
            chain(tt(small[:, 26:27], small[:, 25:26], small[:, 24:25], ALU.subtract))
            chain(ts(small[:, 26:27], small[:, 26:27], -LAM_INIT, None, ALU.add))
            chain(ts(small[:, 27:28], pcol("subln"), 1.0 - LAM_INIT, None, ALU.mult))
            for u in range(2 * HEADS + 1):
                if u < 2 * HEADS:
                    max_of(u)
                if u:
                    combine(u - 1)
                    modulation(3 + u)
            dve.wait_ge(s("mod_drained"), 20)
            gate_of(2, pcol("mix_post", 0, 8), 0, 2)
            scale_of(3, pcol("mlp_pre", 0, 8), 0, 4)
            for c in range(4):
                a = slice(2 * c, 2 * c + 2)
                dve.wait_ge(s("o_std"), c + 1)
                chain(nc.vector.reciprocal(y[:, a, :], y[:, a, :]))
                stt(obuf[:, a, :], obuf[:, a, :], small[:, 27:28], y[:, a, :], ALU.mult, ALU.mult).then_inc(s("o_normed"), 1)
            for c in range(4):
                a = slice(2 * c, 2 * c + 2)
                dve.wait_ge(s("o_hi"), c + 1)
                tt(ulo[:, a, :], obuf[:, a, :], f32(uhi[:, a, :]), ALU.subtract).then_inc(s("o_lo"), 1)
            for g in range(4):
                split(I_AO + g + RING)
            postnorm("post0", 2)

            def low_squared(tag, g, c, n=None, step=0):
                dve.wait_ge(*mlp_nth(tag, "hid_hi", up(c + 1, n, step)))
                r, r2 = y[:, 2 * g:2 * g + 2, :], sq[:, 2 * g:2 * g + 2, :]
                chain(tt(r2, r, r, ALU.mult))
                dve.sem_inc(s("mlp_rfree"), 1)
                a = slice(2 * c, 2 * c + 2) if n is None else bass.ds(n * (2 * step) + 2 * c, 2)
                tt(hid_lo[:, a, :], r2, f32(hid_hi[:, a, :]), ALU.subtract).then_inc(s("mlp_hidden"), 1)

            def mlp(layer, tag, i0, gates):
                prenorm(tag + "_in", h, y, 3, mod_scale(layer, 3, 0))
                low(tag + "_in", y, uhi, ulo)
                dve.drain().then_inc(s("mlp_rfree"), 3)
                if layer == 0:
                    modulation(20)
                    modulation(21)
                with dve.Fori(0, 5) as n:
                    chain.enter(n, 3)
                    for g in range(3):
                        low_squared(tag, g, g, n, 3)
                        split(i0 + g + RING, n, 3)
                chain.leave(5)
                low_squared(tag, 0, 15)
                split(i0 + 15 + RING)
                for g in range(16):
                    split(i0 + 16 + g + RING)
                dve.wait_ge(s("mod_drained"), gates)
                gate_of(4, pcol("mlp_post", 8 * layer, 8), layer, 5)
                postnorm(tag, 4)

            if on("mlp0"):
                mlp(0, "mlp0", I_MLP0, 20)

            def short_conv(g):
                first = (16, 8, 0)[g // 4] + 2 * (g % 4)
                a = slice(2 * (g % 4), 2 * (g % 4) + 2)
                dst = (hv[:, a, :], hx1[:], hx0[:, a, :])[g // 4]
                dve.wait_ge(s("hy_drained"), g + 1)
                if 5 <= g <= 7:
                    dve.wait_ge(s("v_ready"), g - 4)
                for m in range(2):
                    ins = ts(dst[:, m, :], zpad[:, g % 2, m, 0:T], pcol("hy_w_short", first + m, 1), pcol("hy_b_short", first + m, 1),
                             ALU.mult, ALU.add)
                chain(ins)
                for tap in (1, 2):
                    for m in range(2):
                        ins = stt(dst[:, m, :], zpad[:, g % 2, m, tap:T + tap], pcol("hy_w_short", 24 * tap + first + m, 1), dst[:, m, :],
                                  ALU.mult, ALU.add)
                    if tap == 1:
                        chain(ins)
                ins.then_inc(s("hy_conved"), 1)
                if g // 4 == 1:
                    dve.wait_ge(s("hy_conved"), g + 1)
                    tt(hv[:, a, :], hv[:, a, :], hx1[:], ALU.mult).then_inc(s("v_ready"), 1)

            def taps_of(half, t0):
                a = slice(half * 512, half * 512 + 512)
                dve.wait_ge(s("filter_taps"), 2 * half + t0 + 1)
                if half == 0 and t0 == 0:
                    dve.wait_ge(s("decay_loaded"), 16)
                if half and t0 == 0:
                    dve.wait_ge(s("filter_spec"), 2)
                tt(tapf[:, t0, :], ps[:, 6, :], decay[:, t0, a], ALU.mult)
                if t0 == 0:
                    chain(stt(tapb[:, t0, :], ps[:, 7, :], ccol("notfirst"), decay[:, t0, a], ALU.mult, ALU.mult))
                else:
                    chain(tt(tapb[:, t0, :], ps[:, 7, :], decay[:, t0, a], ALU.mult))
                chain(tt(taps[:, t0, :], tapf[:, t0, :], tapb[:, t0, :], ALU.add))
                tt(tapf[:, t0, :], tapf[:, t0, :], tapb[:, t0, :], ALU.subtract).then_inc(s("taps_ready"), 1)

            if on("hyena"):
                scale_of(5, pcol("mix_pre", 8, 8), 1, 1)
                prenorm("hy_in", h, y, 5, mod_scale(1, 0, 0))
                low("hy_in", y, uhi, ulo)
                modulation(22)
                modulation(23)
                nc.vector.memset(zpad[:], 0.0).then_inc(s("zpad_clear"), 1)
                for g in range(12):
                    split(I_HY + g + RING)
                    short_conv(g)
                    if g in (2, 3, 7, 8):
                        taps_of(g // 7, (g - 2) % 5)
                dve.wait_ge(s("mod_drained"), 24)
                gate_of(6, pcol("mix_post", 8, 8), 1, 2)
                scale_of(3, pcol("mlp_pre", 8, 8), 1, 4)
                dve.wait_ge(s("spec_stored"), 4)
                for half in range(2):
                    a = slice(half * 512, half * 512 + 512)
                    dve.wait_ge(s("vspec"), half + 1)
                    if half:
                        dve.wait_ge(s("conv"), 4)
                    vc, vs, hc, hs = ps[:, 0:2, :], ps[:, 2:4, :], spec[:, 0:2, a], spec[:, 2:4, a]
                    tt(prod[:, 0], vc, hc, ALU.mult)
                    chain(tt(prod[:, 1], vs, hs, ALU.mult))
                    chain(tt(yspec[:, 0:2, :], prod[:, 0], prod[:, 1], ALU.subtract))
                    tt(prod[:, 0], vc, hs, ALU.mult)
                    chain(tt(prod[:, 1], vs, hc, ALU.mult))
                    dve.sem_inc(s("vspec_used"), 1)
                    tt(yspec[:, 2:4, :], prod[:, 0], prod[:, 1], ALU.add).then_inc(s("yspec_ready"), 1)
                    for m in range(4):
                        k = 4 * half + m
                        dve.wait_ge(s("conv"), k + 1)
                        ins = stt(hv[:, k, :], hv[:, k, :], pcol("hy_bias", k, 1), ps[:, 4 + m, 0:T], ALU.mult, ALU.add)
                        ins.then_inc(s("conv_taken"), 1)
                    dve.wait_ge(s("conv_taken"), 4 * half + 4)
                    a = slice(4 * half, 4 * half + 4)
                    tt(hv[:, a, :], hv[:, a, :], hx0[:, a, :], ALU.mult).then_inc(s("normed"), 1)
                low("hy", hv, uhi, ulo)
                for g in range(4):
                    split(I_HO + g + RING)
                postnorm("post1", 6)
            if on("mlp1"):
                mlp(1, "mlp1", I_MLP1, 24)

            def halves(m):
                return m.rearrange("p (m t) -> p m t", m=2)

            def head(u):
                return u // 4, (u // 2) % 2, u % 2

            def low_part(name, b, src):
                dve.wait_ge(s(name + "_hi"), 1)
                tt(ylo[:, b:b + MT, :], src, f32(yhi[:, b:b + MT, :]), ALU.subtract).then_inc(s(name + "_lo"), 1)

            def softplus_of_minus_lambda():
                lam, e, z, z2, acc = pcol("lam"), lru[:, 1, :], lru[:, 2, :], lru[:, 4, :], lru[:, 3, :]
                chain(ts(lru[:, 5, :], lam, -1.0, None, ALU.mult))
                tt(lru[:, 0, :], lam, lru[:, 5, :], ALU.max).then_inc(s("lam_abs"), 1)
                dve.wait_ge(s("lam_exp"), 1)
                chain(ts(z, e, 2.0, None, ALU.add))
                chain(nc.vector.reciprocal(z, z))
                chain(tt(z, z, e, ALU.mult))
                chain(tt(z2, z, z, ALU.mult))
                terms = 9
                chain(ts(acc, z2, 1.0 / (2 * terms + 1), 1.0 / (2 * terms - 1), ALU.mult, ALU.add))
                for k in range(terms - 2, -1, -1):
                    chain(tt(acc, acc, z2, ALU.mult))
                    chain(ts(acc, acc, 1.0 / (2 * k + 1), None, ALU.add))
                chain(stt(acc, acc, 2.0, z, ALU.mult, ALU.mult))
                chain(stt(acc, lru[:, 5, :], 0.0, acc, ALU.max, ALU.add))
                chain(ts(acc, acc, 4.0, None, ALU.mult))
                for w, name in enumerate(("ba", "bx")):
                    chain(ts(lru[:, 8 + w, :], pcol(name), 0.5, None, ALU.mult))

            def blocks_of(c):
                src = ps[:, 0, c * T:(c + 1) * T]
                for half in range(2):
                    a = slice(16 * half, 16 * half + 16)
                    ins = tt(blocks[:, c, a, :].rearrange("p l n -> p n l"),
                             src[:, 16 * half:16 * half + 240].rearrange("p (n l) -> p n l", l=16),
                             over_tiles(cpe[:, c, a], NCMP), ALU.add)
                return ins

            def trailing_sums():
                sa, sb, x = y[:, 0:4, :], y[:, 4:8, :], xd[:, :, 16:16 + T]
                chain(tt(sa, x, xd[:, :, 15:15 + T], ALU.add))
                for g0, w, old, new in ((1, 2, sa, sb), (2, 4, sb, sa), (3, 8, sa, sb)):
                    tt(new[:, g0:4, w:], old[:, g0:4, w:], old[:, g0:4, :-w], ALU.add)
                    chain(nc.vector.tensor_copy(new[:, g0:4, 0:w], old[:, g0:4, 0:w]))
                for g, b in enumerate((sa, sb, sa, sb)):
                    ins = tt(b[:, g, :], b[:, g, :], bcol("recip")[:, g * T:(g + 1) * T], ALU.mult)
                chain(ins)
                for g, b in enumerate((sa, sb, sa, sb)):
                    ins = tt(x[:, g, :], b[:, g, :], x[:, g, :], ALU.subtract)
                ins.then_inc(s("pooled"), 1)
                dve.wait_ge(s("pooled"), 1)

            if on("mixer"):
                for b in (lruw[:], rec[:, :, 0:3], xd[:, :, 0:16]):
                    ins = nc.vector.memset(b, 0.0)
                ins.then_inc(s("lru_clear"), 1)
                prenorm("mix_in", h, y, 0, gain="norm1")
                low("mix_in", y, uhi, ulo)
                softplus_of_minus_lambda()
                dve.wait_ge(s("mixer_loaded"), 16 * 5)
                dve.wait_ge(s("chunk_used"), I_PROJ + 1)
                blocks_of(0)
                blocks_of(1).then_inc(s("blocks_ready"), 1)
                chain(tt(gmw[:], gmw[:], over_tiles(tril, MT), ALU.mult))
                for g in range(16):
                    split(I_PROJ + g + RING)
                    if g == 6:
                        dve.wait_ge(s("proj_drained"), 6)
                        chain(ts(gates[:], gates[:], 0.5, 0.5, ALU.mult, ALU.add))
                    if g == 8:
                        dve.wait_ge(s("proj_drained"), 8)
                        dve.wait_ge(s("cmp_hidden"), 1)
                        for m in range(MT):
                            ins = ts(sq[:, m, :], rec[:, m, 0:T], pcol("conv_w", m, 1), pcol("conv_b", m, 1), ALU.mult, ALU.add)
                        chain(ins)
                    if 9 <= g <= 11:
                        for m in range(MT):
                            ins = stt(sq[:, m, :], rec[:, m, g - 8:g - 8 + T], pcol("conv_w", 4 * (g - 8) + m, 1), sq[:, m, :], ALU.mult, ALU.add)
                        if g < 11:
                            chain(ins)
                        else:
                            ins.then_inc(s("rec_conved"), 1)
                    if g == 12:
                        dve.wait_ge(s("proj_drained"), 12)
                        trailing_sums()
                dve.wait_ge(s("v_std"), 1)
                chain(nc.vector.reciprocal(sm[:, 4:6], sm[:, 2:4]))
                for n in range(TT):
                    ins = ts(vg[:, n, :], vg[:, n, :], sm[:, 4 + n:5 + n], None, ALU.mult)
                ins.then_inc(s("v_normed"), 1)
                dve.wait_ge(s("gm_mixed"), 1)
                for g in range(MT):
                    ins = stt(y[:, g, :].rearrange("p (n t) -> p n t", n=TT), halves(ps[:, 4 + g // 2, (g % 2) * T:(g % 2 + 1) * T]),
                              pcol("gm_norm", g, 1), over_tiles(gmb[:, g, :], TT), ALU.mult, ALU.add)
                chain(ins)
                tt(y[:, 0:MT, :], y[:, 0:MT, :], ug, ALU.mult).then_inc(s("gm_ready"), 1)
                dve.wait_ge(s("cmp_hidden"), 1)
                low_part("gm", slot_of[0], y[:, 0:MT, :])
                dve.wait_ge(s("pool_hi"), 1)
                for g in range(MT):
                    b = slot_of[3] + g
                    ins = stt(ylo[:, b, :], ps[:, 6 + g // 2, (g % 2) * T:(g % 2 + 1) * T], pcol("pool_scale", g, 1), f32(yhi[:, b, :]),
                              ALU.mult, ALU.subtract)
                ins.then_inc(s("pool_lo"), 1)
                rate, inp, pw = y[:, 0:4, :], y[:, 4:8, :], rec[:, :, 0:T]
                dve.wait_ge(s("rec_tanh"), 1)
                for m in range(MT):
                    ins = ts(rate[:, m, :], rate[:, m, :], 1.0, lru[:, 3, m:m + 1], ALU.add, ALU.mult)
                ins.then_inc(s("rec_rate"), 1)
                dve.wait_ge(s("rec_tanh"), 2)
                chain(stt(inp, inp, 1.0, sq[:, 0:4, :], ALU.add, ALU.mult))
                dve.wait_ge(s("decay_ready"), 1)
                chain(tt(sq[:, 4:8, :], rate, rate, ALU.mult))
                stt(pw, sq[:, 4:8, :], 1.0, pw, ALU.add, ALU.mult).then_inc(s("rec_power"), 1)
                dve.wait_ge(s("rec_root"), 1)
                chain(stt(inp, inp, 0.5, pw, ALU.mult, ALU.mult))
                for m in range(MT):
                    ins = nc.vector.tensor_tensor_scan(sq[:, m, :], rate[:, m, :], inp[:, m, :], 0.0, ALU.mult, ALU.add)
                chain(ins)
                tt(pw, sq[:, 0:4, :], gate[:], ALU.mult).then_inc(s("lru_ready"), 1)
                low_part("lru", slot_of[1], pw)
                dve.wait_ge(s("lru_lo"), 1)
                dve.sem_inc(s("lru_done"), 1)
                dve.wait_ge(s("cmp_scores"), 1)
                for qt in range(2):
                    for g in range(2):
                        ins = tt(cmp_p[:, qt, 4 * g:4 * g + 4], ps[:, 4 + 2 * qt + g, 0:64].rearrange("p (h n) -> p h n", n=16)[:, :, 0:NCMP],
                                 over_tiles(bcol("cmask")[:, qt * NCMP:(qt + 1) * NCMP], 4), ALU.add)
                chain(ins)
                flat = cmp_p.rearrange("p t h n -> p (t h) n")
                top, inv = sm[:, 24:40], sm[:, 40:56]
                chain(nc.vector.tensor_reduce(top, flat, AX, ALU.max))
                tt(flat, flat, over_cols(top, NCMP), ALU.subtract).then_inc(s("cmp_shifted"), 1)
                dve.wait_ge(s("cmp_exp"), 1)
                chain(nc.vector.tensor_reduce(top, flat, AX, ALU.add))
                chain(nc.vector.reciprocal(inv, top))
                for qt in range(2):
                    ins = stt(inv[:, 8 * qt:8 * qt + 8], inv[:, 8 * qt:8 * qt + 8], bcol("cvalid")[:, qt:qt + 1],
                              gates[:, qt, :].rearrange("p (h b) -> p b h", b=3)[:, 0, :], ALU.mult, ALU.mult)
                chain(ins)
                tt(flat, flat, over_cols(inv, NCMP), ALU.mult).then_inc(s("cmp_weights"), 1)

                def nsa_max(u):
                    j, g, qt = head(u)
                    dve.wait_ge(s("nsa_scores"), u + 1)
                    w = 8 + 4 * (u % 2)
                    sc = ps[:, u % 2, :].rearrange("p (b k) -> p b k", b=2)
                    diag = sc[:, :, qt * P:(qt + 1) * P]
                    chain(tt(diag, diag, over_tiles(causal, 2), ALU.add))
                    chain(nc.vector.tensor_reduce(sm[:, w + 2:w + 4], sc[:, :, 0:(qt + 1) * P], AX, ALU.max))
                    ts(sm[:, w:w + 2], sm[:, w + 2:w + 4], -SCALE, None, ALU.mult).then_inc(s("nsa_max"), 1)

                def nsa_weights(u):
                    j, g, qt = head(u)
                    dve.wait_ge(s("nsa_exps"), u + 1)
                    w = 16 + 4 * (u % 2)
                    r = sm[:, w + 2:w + 4]
                    hh = g * 4 + j
                    chain(nc.vector.reciprocal(r, sm[:, w:w + 2]))
                    chain(tt(r, r, gates[:, qt, 3 * hh + 1:3 * hh + 3], ALU.mult))
                    for b in range(2):
                        e = nsa_e[:, u % 2, b, 0:(qt + 1) * P]
                        ins = ts(e, e, r[:, b:b + 1], None, ALU.mult)
                    ins.then_inc(s("nsa_weights"), 1)

                dve.wait_ge(s("cmp_turned"), 1)
                for u in range(20):
                    if u < 16:
                        nsa_max(u)
                    if 1 <= u <= 16:
                        nsa_weights(u - 1)
                    if u >= 7 and (u - 3) % 4 == 0 or u == 19:
                        j = (u - 3) // 4 - 1
                        b = slot_of[2] + j
                        dve.wait_ge(s("nsa_out_hi"), j + 1)
                        tt(ylo[:, b, :], ps[:, 4 + j % 2, 0:T], f32(yhi[:, b, :]), ALU.subtract).then_inc(s("nsa_out_lo"), 1)
                dve.wait_ge(s("nsa_out"), 16)
                chain(nc.vector.memset(y[:], 0.0))
                dve.drain().then_inc(s("br_free"), 2)
                dve.drain().then_inc(s("gated_free"), 2)
                with dve.Fori(0, 4) as n:
                    chain.enter(n, 4)
                    for g in range(6):
                        i = I_BR + g
                        if g >= 4:
                            a = slice(4 * (g - 4), 4 * (g - 4) + 4)
                            dve.wait_ge(s("mg_tanh"), up(4, n, 4))
                            dve.wait_ge(s("chunk_used"), up(i + 1, n, 6))
                            src = ps[:, 2 * g - 4:2 * g - 2, :].rearrange("p b (m t) -> p (b m) t", m=2)
                            chain(stt(sq[:, a, :], gated[:, a, :], 1.0, src, ALU.add, ALU.mult))
                            dve.sem_inc(s("br_free"), 1)
                            dve.sem_inc(s("gated_free"), 1)
                            chain(tt(y[:, a, :], y[:, a, :], sq[:, a, :], ALU.add))
                        split(i + RING, n, 6)
                chain.leave(4)
                for c in range(2):
                    a = slice(4 * c, 4 * c + 4)
                    ts(y[:, a, :], y[:, a, :], 0.5, None, ALU.mult).then_inc(s("normed"), 1)
                low("merged", y, uhi, ulo)
                for g in range(4):
                    dve.wait_ge(s("chunk_used"), I_WO + g + 1)
                    a = slice(2 * g, 2 * g + 2)
                    ins = tt(h[:, a, :], h[:, a, :], halves(ps[:, g, :]), ALU.add)
                    if g % 2:
                        ins.then_inc(s("h"), 1)
                    split(I_WO + g + RING)

            if on("all"):
                prenorm("moe_in", h, y, 0, gain="norm2")
                dve.wait_ge(s("router_hi"), 1)
                tt(wrlo[:], wr[:], f32(wrhi[:]), ALU.subtract).then_inc(s("router_lo"), 1)
                low("moe_in", y, uhi, ulo)

                def row(k, n=4):
                    return ro[:, k, :, 0:n]

                def wide(x, n=4):
                    return x.to_broadcast([P, TT, n])

                def first_of(dst, src, top, tmp, tmp_top):
                    chain(tt(row(tmp), src, wide(top), ALU.is_equal))
                    chain(tt(row(tmp), row(tmp), order4[:].unsqueeze(1).to_broadcast([P, TT, 4]), ALU.mult))
                    chain(nc.vector.tensor_reduce(row(tmp_top, 1), row(tmp), AX, ALU.max))
                    chain(tt(dst, row(tmp), wide(row(tmp_top, 1)), ALU.is_equal))

                dve.wait_ge(s("router"), 1)
                chain(tt(lg[:], ps[:, 4, 0:64].rearrange("p (t c) -> p t c", t=2)[:, :, 0:20], rb[:].unsqueeze(1).to_broadcast([P, TT, 20]), ALU.add))
                grp = lg[:, :, 0:4]
                chain(nc.vector.tensor_reduce(row(0, 1), grp, AX, ALU.max))
                tt(row(1), grp, wide(row(0, 1)), ALU.subtract).then_inc(s("group_shifted"), 1)
                first_of(row(3), grp, row(0, 1), 4, 5)
                dve.wait_ge(s("group_exp"), 1)
                chain(nc.vector.tensor_reduce(row(6, 1), row(2), AX, ALU.add))
                chain(nc.vector.reciprocal(row(6, 1), row(6, 1)))
                for t0 in range(TT):
                    prod4 = ro[:, 14 + 2 * t0:16 + 2 * t0].rearrange("p a b c -> p (a b c)").rearrange("p (g e) -> p g e", g=4)
                    chain(tt(prod4, lg[:, t0, 4:20].rearrange("p (g e) -> p g e", g=4), over_cols(ro[:, 3, t0, :], 4), ALU.mult))
                    chain(nc.vector.tensor_reduce(ro[:, 7, t0, :], prod4.rearrange("p g e -> p e g"), AX, ALU.add))
                chain(nc.vector.tensor_reduce(row(8, 1), row(7), AX, ALU.max))
                first_of(row(9), row(7), row(8, 1), 4, 5)
                chain(stt(row(7), row(9), MASKED, row(7), ALU.mult, ALU.add))
                chain(nc.vector.tensor_reduce(row(10, 1), row(7), AX, ALU.max))
                tt(row(11, 1), row(10, 1), row(8, 1), ALU.subtract).then_inc(s("top_gap"), 1)
                first_of(row(13), row(7), row(10, 1), 4, 5)
                dve.wait_ge(s("top_exp"), 1)
                chain(ts(row(18, 1), row(12, 1), 1.0, None, ALU.add))
                chain(nc.vector.reciprocal(row(18, 1), row(18, 1)))
                chain(tt(row(18, 1), row(18, 1), row(6, 1), ALU.mult))
                chain(tt(row(19, 1), row(18, 1), row(12, 1), ALU.mult))
                chain(tt(row(9), row(9), wide(row(18, 1)), ALU.mult))
                chain(tt(row(13), row(13), wide(row(19, 1)), ALU.mult))
                chain(tt(row(9), row(9), row(13), ALU.add))
                for t0 in range(TT):
                    ins = tt(cb[:, t0, :].rearrange("p (g e) -> p g e", g=4), over_tiles(ro[:, 9, t0, :], 4), over_cols(ro[:, 3, t0, :], 4), ALU.mult)
                ins.then_inc(s("combine_ready"), 1)

                def weighted(i, j, n=None):
                    dve.wait_ge(s("chunk_used"), up(i + 1, n, 6))
                    dve.wait_ge(s("moe_silu"), j + 1 if n is None else n * 2 + (j + 3))
                    a = slice(2 * j, 2 * j + 2)
                    tt(hmid[:, a, :], sg[:, a, :], halves(ps[:, 2 + j, :]), ALU.mult).then_inc(s("moe_gated"), 1)
                    dve.wait_ge(s("moe_gated"), j + 1 if n is None else n * 2 + (j + 3))
                    c = comb[:, 0, :] if n is None else comb[:, bass.ds(n + 1, 1), :].rearrange("p a t -> p (a t)")
                    tt(hmid[:, a, :], hmid[:, a, :], over_tiles(c, 2), ALU.mult).then_inc(s("moe_weighted"), 1)

                def expert_low(j, n=None):
                    dve.wait_ge(s("moe_hi"), j + 1 if n is None else n * 2 + (j + 3))
                    a = slice(2 * j, 2 * j + 2)
                    tt(elo[:, a, :], hmid[:, a, :], f32(ehi[:, a, :]), ALU.subtract).then_inc(s("moe_hid"), 1)

                def add_rows(i, j, n=None, last=False):
                    dve.wait_ge(s("chunk_used"), up(i + 1, n, 6))
                    a = slice(4 * j, 4 * j + 4)
                    tt(h[:, a, :], h[:, a, :], ps[:, 4 + 2 * j:6 + 2 * j, :].rearrange("p b (m t) -> p (b m) t", m=2), ALU.add)\
                        .then_inc(s("h" if last else "moe_free"), 1)

                for j in range(4):
                    split(I_MOE + j + RING)
                dve.wait_ge(s("comb_stored"), EXPERTS // 2)
                for j in range(2):
                    weighted(I_MOE + 2 + j, j)
                for j in range(2):
                    expert_low(j)
                dve.drain().then_inc(s("moe_free"), 2)
                with dve.Fori(0, EXPERTS - 1) as n:
                    i = I_MOE + 4
                    for j in range(2):
                        split(i + j + RING, n, 6)
                    for j in range(2):
                        add_rows(i + 2 + j, j, n)
                        split(i + 2 + j + RING, n, 6)
                    for j in range(2):
                        weighted(i + 4 + j, j, n)
                        split(i + 4 + j + RING, n, 6)
                    for j in range(2):
                        expert_low(j, n)
                dve.wait_ge(s("moe_free"), 2 * EXPERTS)
                for j in range(2):
                    add_rows(N_CHUNKS - 2 + j, j, last=True)
                prenorm("final", h, y, 0, gain="final")
                dve.wait_ge(*nth("final", "normed", 2))
                dve.sem_inc(s("result_ready"), 1)

            if upto != "all":
                for c in range(2):
                    dve.wait_ge(*nth({"attn": "post0", "mlp0": "mlp0", "hyena": "post1", "mlp1": "mlp1", "mixer": "mixed"}[upto], "h", c + 1))
                nc.vector.tensor_copy(y[:], h[:]).then_inc(s("result_ready"), 1)


SPARAMS = ["b_mod", "norm_mix_pre", "norm_mix_post", "norm_mlp_pre", "norm_mlp_post", "attn_subln", "hy_b_in",
           "hy_w_short", "hy_b_short", "hy_bias", "hy_b_out", "norm1_g_2", "gm_norm_g_2", "conv_w_2", "conv_b_2",
           "lru_ba_2", "lru_bx_2", "lru_lambda_2", "pool_scale_2", "norm2_g_2", "final_norm_g_2"]


def laid_out(x):
    ac = np.ascontiguousarray
    a = {k: np.asarray(v) for k, v in x.items()}
    weights = np.zeros((N_CHUNKS + 1, P, CW), np.float32)
    for i, (name, lead, r0, rows, cols) in enumerate(weight_stream()):
        m = a[name][lead]
        lo, n = cols[0], len(cols)
        m = m[r0:r0 + rows, lo:lo + n] if cols == tuple(range(lo, lo + n)) else m[r0:r0 + rows][:, list(cols)]
        if name == "w_branch_2" and lead[1] == 2:
            order = [g * 256 + j * 64 + d for j in range(4) for g in range(2) for d in range(64)]
            m = m[order]
        k = rows // P
        width = CW // k
        weights[i].reshape(P, k, width)[:, :, :n] = m.reshape(k, P, n).transpose(1, 0, 2)

    def fm(v):
        return ac(v.reshape(T, KT, P).transpose(2, 1, 0))

    params = ac(np.concatenate([a[n].reshape(-1, P) for n in SPARAMS]).T)
    assert params.shape == (P, NPAR)
    out = {
        "weights": weights, "mods": ac(a["w_mod"].reshape(2, KT, P, 48, P).transpose(0, 3, 2, 1, 4).reshape(N_MODS, P, KT * P)), "params": params, "x": fm(a["x"]), "ctx": fm(a["ctx"]),
        "cvec": ac(np.stack([a["c"].reshape(KT, P).T, a["c_ctx"].reshape(KT, P).T], axis=2)),
        "attn_lambda": ac(a["attn_lambda"].reshape(-1)),
        "hy_filt_w1": ac(a["hy_filt_w1"][0]), "hy_filt_w2": ac(a["hy_filt_w2"][0].transpose(1, 0, 2)),
        "hy_filt_w_out": ac(a["hy_filt_w_out"][0]),
        "fpar": ac(np.stack([a["hy_filt_b1"][0], a["hy_filt_b2"][0, 0], a["hy_filt_b2"][0, 1], a["hy_filt_freq"][0]], axis=1)),
        "cmp_w1": ac(a["cmp_w1_2"][0].reshape(2, 2, CMP_LEN, HD, HD).transpose(1, 3, 0, 2, 4).reshape(P, 2, CMP_LEN * HD)),
        "cmp_w2": ac(a["cmp_w2_2"][0].transpose(1, 2, 0, 3).reshape(P, 2, HD)),
        "cmp_pe": ac(np.concatenate([a["cmp_pe_2"][0].transpose(2, 0, 1)] * 2)),
        "gm_ws": ac(a["gm_ws_2"][0].transpose(2, 0, 1)), "gm_b": ac(a["gm_b_2"][0].reshape(-1)),
        "pool_w": ac(a["pool_w_2"][0].transpose(1, 0, 2)),
        "lru_wa": ac(a["lru_wa_2"][0].reshape(4, 2, HD, HD).transpose(1, 2, 0, 3)),
        "lru_wx": ac(a["lru_wx_2"][0].reshape(4, 2, HD, HD).transpose(1, 2, 0, 3)),
        "router_w": ac(np.concatenate([a["router_w_group_2"][0], a["router_w_expert_2"][0]], axis=1)
                       .reshape(KT, P, 20).transpose(1, 0, 2)),
        "router_b": ac(np.concatenate([a["router_b_group_2"][0], a["router_b_expert_2"][0]])),
        "order4": np.broadcast_to(np.arange(4, 0, -1, dtype=np.float32), (P, 4)).copy(),
        **shape_constants(),
    }
    return out


UPTO = "all"


def kernel(**inputs):
    import concourse.bacc as bacc
    from concourse.bass_utils import run_bass_kernel_spmd

    nc = bacc.Bacc("TRN2", target_bir_lowering=False, num_devices=1)
    arrays = laid_out(inputs)
    aps = {n: nc.dram_tensor(n + "_in", v.shape, mybir.dt.from_np(v.dtype), kind="ExternalInput").ap()
           for n, v in arrays.items()}
    out = nc.dram_tensor("out_0", (P, KT, T), F32, kind="ExternalOutput").ap()
    program(nc, aps, out, UPTO)
    r = run_bass_kernel_spmd(nc, [{n + "_in": v for n, v in arrays.items()}], core_ids=[0])
    got = r.results[0]["out_0"]
    return np.ascontiguousarray(got.transpose(2, 1, 0)).reshape(1, T, D)
```

```python
from contextlib import ExitStack
import math

import numpy as np

import concourse.bass as bass
from concourse import mybir

F32 = mybir.dt.float32
F32R = mybir.dt.float32r
ACT = mybir.ActivationFunctionType
ALU = mybir.AluOpType
AX = mybir.AxisListType.X

P = 128
D = 1024
KT = D // P
T = 256
TT = T // P
DFF = 4096
HEADS = 8
RING = 3
CW = 2048
EXPERTS = 16
DE = 512
MIX = 512
MT = MIX // P
NCMP = 15
CMP_STRIDE, CMP_LEN = 16, 32
HD = 64
LAM_INIT = 0.8 - 0.6 * math.exp(0.0)
SCALE = HD ** -0.5
EPS = 1e-6
MASKED = -1e30
BRANCH_ORDER = (0, 3, 1, 2)
POOL_WINDOWS = (2, 4, 8, 16)

U0, V0, GATE0, REC0, Q0, KV0, NSAG0, XD0, MG0 = 0, 512, 1024, 1536, 2048, 2560, 3328, 3352, 3864


ATT_MODS = 8
START_TILES = 16

def weight_stream():
    def cols(a, n):
        return tuple(range(a, a + n))

    def mat(name, lead, c0):
        return (name, lead, 0, D, cols(c0, 256))

    def down(name, lead, c0):
        return (name, lead, 0, MIX, cols(c0, 512))

    def mlp(layer):
        return [mat("w_mlp_in", (layer,), 256 * j) for j in range(16)] + \
            [("w_mlp_out", (layer,), D * g, D, cols(256 * m, 256)) for m in range(4) for g in range(4)]

    out = [mat("attn_w_qkv", (0,), c0 + 256 * j) for c0 in (D, 0, 2 * D) for j in range(4)]
    out += [mat("attn_w_out", (0,), 256 * j) for j in range(4)]
    out += mlp(0)
    out += [mat("hy_w_in", (0,), c0 + 256 * j) for c0 in (2 * D, D, 0) for j in range(4)]
    out += [mat("hy_w_out", (0,), 256 * j) for j in range(4)]
    out += mlp(1)
    kv = lambda n: cols(KV0 + 128 * n, 128)
    qcol = lambda j: cols(Q0 + 64 * j, 64) + cols(Q0 + 256 + 64 * j, 64)
    for c in [kv(0) + kv(1), kv(2) + kv(4), qcol(0) + qcol(1), qcol(2) + qcol(3), kv(3) + kv(5), cols(NSAG0, 24)]:
        out.append(("w_in_2", (0,), 0, D, c))
    for c0 in (REC0, REC0 + 256, GATE0, GATE0 + 256, XD0, XD0 + 256, V0, V0 + 256, U0, U0 + 256):
        out.append(mat("w_in_2", (0,), c0))
    for n in BRANCH_ORDER:
        out += [mat("w_in_2", (0,), MG0 + D * n + 256 * j) for j in range(4)]
        out += [down("w_branch_2", (0, n), 512 * j) for j in range(2)]
    out += [mat("w_out_2", (0,), 256 * j) for j in range(4)]
    gate = lambda e: [mat("moe_w_gate_2", (0, e), 256 * j) for j in range(2)]
    upx = lambda e: [mat("moe_w_up_2", (0, e), 256 * j) for j in range(2)]
    dnx = lambda e: [down("moe_w_down_2", (0, e), 512 * j) for j in range(2)]
    out += gate(0) + upx(0)
    for e in range(1, EXPERTS):
        out += gate(e) + dnx(e - 1) + upx(e)
    out += dnx(EXPERTS - 1)

    after = {w: 1 for w in range(12)}
    after[11] += ATT_MODS
    after.update({16 + w: 1 for w in range(1, 16, 2)})
    after.update({32 + w: 1 for w in range(1, 16, 2)})
    after.update({80 + w: 1 for w in range(2, 16, 4)})
    stream, at, mods = [], [], []
    for w, entry in enumerate(out):
        at.append(len(stream))
        stream.append(entry)
        for _ in range(after.get(w, 0)):
            layer, tile = divmod(2 * len(mods) + START_TILES, 48)
            mods.append(len(stream))
            stream.append(mat("w_mod", (layer,), P * tile))
    assert 2 * len(mods) + START_TILES == 96
    return stream, at, mods


STREAM, AT, MODS = weight_stream()
N_CHUNKS = len(STREAM)
I_QKV, I_AO, I_MLP0, I_HY, I_HO, I_MLP1, I_PROJ, I_BR, I_WO, I_MOE = (AT[w] for w in (0, 12, 16, 48, 60, 64, 96, 112, 136, 140))
I_OUT0, I_OUT1 = AT[32], AT[80]
I_ATT = I_AO - ATT_MODS


def items(first, last):
    g = 0
    for i in range(first, last):
        if i in MODS:
            yield i, None, MODS.index(i)
        else:
            yield i, g, None
            g += 1


def weights_up_to(i):
    return i + 1 - sum(m <= i for m in MODS)


def param_columns():
    names = [("b_mod", 96), ("mix_pre", 16), ("mix_post", 16), ("mlp_pre", 16), ("mlp_post", 16),
             ("subln", 1), ("hy_b_in", 24), ("hy_w_short", 72), ("hy_b_short", 24), ("hy_bias", 8),
             ("hy_b_out", 8), ("norm1", 8), ("gm_norm", 4), ("conv_w", 16), ("conv_b", 4), ("ba", 4),
             ("bx", 4), ("lam", 4), ("pool_scale", 4), ("norm2", 8), ("final", 8)]
    out, at = {}, 0
    for n, k in names:
        out[n] = (at, k)
        at += k
    return out, at


PCOL, NPAR = param_columns()

CONST = {}
_at = 0
for _n, _k in (("ones", 128), ("ident", 128), ("rot", 128), ("cos", 256), ("sin", 256), ("notfirst", 1), ("eps", 1)):
    CONST[_n] = (_at, _k)
    _at += _k
NCONST = _at
CONST_B = {}
_at = 0
for _n, _k in (("causal", 128), ("tril", 128), ("cmask", 30), ("cvalid", 2), ("recip", 1024)):
    CONST_B[_n] = (_at, _k)
    _at += _k
NCONST_B = _at


def shape_constants():
    f = np.float32
    p = np.arange(P)
    t = np.arange(T)
    c = np.zeros((P, NCONST), f)

    def put(table, where, name, v):
        a, k = where[name]
        table[:, a:a + k] = v

    put(c, CONST, "ones", 1.0)
    put(c, CONST, "ident", np.eye(P))
    rot = np.zeros((P, P))
    first = (p % 32) < 16
    rot[p[first] + 16, p[first]] = -1.0
    rot[p[~first] - 16, p[~first]] = 1.0
    put(c, CONST, "rot", rot)
    inv = (f(10000.0) ** (-(np.arange(16, dtype=f)) / f(16))).astype(f)
    pos = np.where((p % 64)[:, None] < 32, (t // 64)[None, :], (t % 64)[None, :]).astype(f)
    ang = pos * inv[p % 16][:, None]
    put(c, CONST, "cos", np.cos(ang, dtype=f))
    put(c, CONST, "sin", np.sin(ang, dtype=f))
    put(c, CONST, "notfirst", (p > 0).astype(f)[:, None])
    put(c, CONST, "eps", EPS)
    b = np.zeros((P, NCONST_B), f)
    put(b, CONST_B, "causal", np.where(p[None, :] <= p[:, None], 0.0, MASKED))
    put(b, CONST_B, "tril", (p[:, None] <= p[None, :]).astype(f))
    cm = np.zeros((P, 2, NCMP))
    for qt in range(2):
        cm[:, qt] = np.where((16 * np.arange(NCMP) + 31)[None, :] <= (qt * P + p)[:, None], 0.0, MASKED)
    put(b, CONST_B, "cmask", cm.reshape(P, -1))
    put(b, CONST_B, "cvalid", np.stack([p >= 31, p >= 0], 1).astype(f))
    rec = np.stack([1.0 / np.minimum(t + 1, w) for w in POOL_WINDOWS]).astype(f)
    put(b, CONST_B, "recip", np.broadcast_to(rec.reshape(1, -1), (P, 1024)))
    tl = np.linspace(0.0, 1.0, T, dtype=f)[:, None]
    w = f(2.0 * math.pi) * np.arange(T, dtype=f)[:, None] / f(T)
    fr = np.linspace(1e-4, 15, 16, dtype=f)[None, :]
    z = np.concatenate([tl, np.cos(fr * w), -np.sin(fr * w)], axis=1).astype(f)
    deltas = np.abs(np.linspace(math.log(1e-2) / 1.5, math.log(1e-2) / 0.3, D, dtype=f))
    decay = np.exp(-tl * deltas[None, :]).astype(f)
    k = np.arange(T)
    th = 2.0 * np.pi * (k + 0.5)[None, :] * t[:, None] / (2 * T)
    fwd = np.concatenate([np.cos(th), np.sin(th)], axis=1)
    inv_ = np.concatenate([np.cos(th).T, np.sin(th).T], axis=0) / T
    return {
        "const": c, "const_b": b, "zfeat": np.ascontiguousarray(z.T),
        "decay": np.ascontiguousarray(decay.reshape(TT, P, D).transpose(1, 0, 2)),
        "dft": np.ascontiguousarray(fwd.reshape(TT, P, 2 * T).transpose(1, 0, 2).astype(f)),
        "idft": np.ascontiguousarray(inv_.reshape(4, P, T).transpose(1, 0, 2).astype(f)),
    }


def program(nc, A, out, upto="all"):
    stages = ["attn", "mlp0", "hyena", "mlp1", "mixer", "all"]
    ends = {"attn": I_MLP0, "mlp0": I_HY, "hyena": I_MLP1, "mlp1": I_PROJ, "mixer": I_MOE, "all": N_CHUNKS}
    n_chunks = ends[upto] + (upto == "all")

    def on(stage):
        return stages.index(stage) <= stages.index(upto)

    stack = ExitStack()
    sems = {}

    def s(name):
        if name not in sems:
            sems[name] = stack.enter_context(nc.semaphore(name))
        return sems[name]

    def up(value, n=None, step=0):
        return value if n is None else n * step + value

    normed_inputs = ["x", "ctx", "mlp0_in", "hy_in", "hy", "mlp1_in", "mix_in", "merged", "moe_in"]
    turns_of = {
        "squares": [("x", 2), ("ctx", 2), ("post0", 4), ("mlp0_in", 2), ("mlp0", 4), ("hy_in", 2), ("post1", 4), ("mlp1_in", 2),
                    ("mlp1", 4), ("mix_in", 2), ("moe_in", 2), ("final", 2)],
        "normed": [(t, 2) for t in normed_inputs + ["final"]],
        "hi": [(t, 2) for t in normed_inputs], "lo": [(t, 2) for t in normed_inputs],
        "h": [(t, 2) for t in ("post0", "mlp0", "post1", "mlp1", "mixed", "moe")],
    }
    turns_of["sumsq"] = turns_of["std"] = [(t, 1) for t, _ in turns_of["squares"]]

    def nth(tag, step, count):
        before = 0
        for t, n in turns_of[step]:
            if t == tag:
                return s(step), before + count
            before += n
        raise KeyError((tag, step))

    def mods_before(i):
        return sum(m < i for m in MODS)

    def mlp_plan(layer):
        if layer == 0:
            return 4, 4, 0, list(items(I_MLP0, I_MLP0 + 6)), MODS.index(I_MLP0 + 2)
        return 3, 5, 1, list(items(I_MLP1, I_MLP1 + 3)), None

    def out_span(layer):
        return (I_OUT1, I_PROJ) if layer else (I_OUT0, I_HY)

    def mlp_nth(tag, step, count):
        per_layer = {"free": 20, "rfree": 20, "hid_hi": 16, "hidden": 16, "yfree": 6}[step]
        return s("mlp_" + step), count + (per_layer if tag == "mlp1" else 0)

    class Chain:

        def __init__(self, eng, name):
            self.eng, self.sem, self.count, self.n, self.step = eng, s(name), 0, None, 0

        def tick(self, ins):
            self.count += 1
            ins.then_inc(self.sem, 1)
            return up(self.count, self.n, self.step)

        def __call__(self, ins):
            self.eng.wait_ge(self.sem, self.tick(ins))

        def enter(self, n, step):
            self.start, self.n, self.step = self.count, n, step

        def leave(self, turns):
            assert self.count == self.start + self.step, (self.count - self.start, self.step)
            self.count, self.n, self.step = self.start + self.step * turns, None, 0

    with stack:
        def alloc(where, name, shape, dt=F32):
            return where.enter_context(nc.sbuf_tensor(name, [P, *shape], dt))

        raw = alloc(stack, "raw", [RING, CW])
        macc = alloc(stack, "macc", [RING, 256])
        whi = alloc(stack, "whi", [RING, CW], F32R)
        wlo = alloc(stack, "wlo", [RING, CW], F32R)
        h = alloc(stack, "h", [KT, T])
        uhi = alloc(stack, "uhi", [KT, T], F32R)
        ulo = alloc(stack, "ulo", [KT, T], F32R)
        y = alloc(stack, "y", [KT, T])
        sq = alloc(stack, "sq", [KT, T])
        std = alloc(stack, "std", [T])
        rstd = alloc(stack, "rstd", [T])
        par = alloc(stack, "par", [NPAR])
        con = alloc(stack, "con", [NCONST])
        modv = alloc(stack, "modv", [96, 2])
        coef = alloc(stack, "coef", [10, KT])
        small = alloc(stack, "small", [64])
        cvec = alloc(stack, "cvec", [KT, 2])
        csil = alloc(stack, "csil", [KT, 2])
        hdn = alloc(stack, "hdn", [T])
        ps = stack.enter_context(nc.psum_tensor("ps", [P, 8, 512], F32))

        with ExitStack() as st:
            qbuf = alloc(st, "qbuf", [HEADS, T])
            kbuf = alloc(st, "kbuf", [HEADS, 2 * T])
            vbuf = alloc(st, "vbuf", [4, D])
            with ExitStack() as st2:
                ctx_hi = alloc(st2, "ctx_hi", [KT, T], F32R)
                ctx_lo = alloc(st2, "ctx_lo", [KT, T], F32R)
                gap = alloc(st2, "gap", [CW])
                ctx = alloc(st2, "ctx", [KT, T])
                start_acc = alloc(st2, "start_acc", [4, 2, 256])
            obuf = alloc(st, "obuf", [HEADS, T])
            ebuf = alloc(st, "ebuf", [2, 2, 512])
            atb = alloc(st, "atb", [2, 4, T])
        with ExitStack() as st:
            mstart = alloc(st, "mstart", [START_TILES // 2, CW])
        with ExitStack() as st:
            hid_hi = alloc(st, "hid_hi", [DFF // P, T], F32R)
            hid_lo = alloc(st, "hid_lo", [DFF // P, T], F32R)
        with ExitStack() as st:
            hv = alloc(st, "hv", [KT, T])
            hx0 = alloc(st, "hx0", [KT, T])
            hx1 = alloc(st, "hx1", [2, T])
            zpad = alloc(st, "zpad", [2, 2, T + 2])
            vtok = alloc(st, "vtok", [TT, D])
            dft = alloc(st, "dft", [TT, 2 * T])
            idft = alloc(st, "idft", [4, T])
            spec = alloc(st, "spec", [4, D])
            with ExitStack() as st2:
                fwo = alloc(st2, "fwo", [2 * D])
                taps = alloc(st2, "taps", [TT, 512])
            yspec = alloc(st, "yspec", [2, 4, 512])
            prod = alloc(st, "prod", [2, 2, 512])
        with ExitStack() as st:
            gm = alloc(st, "gm", [2, MT, T])
            gate = alloc(st, "gate", [MT, T])
            rec = alloc(st, "rec", [MT, T + 3])
            qn = alloc(st, "qn", [MT, T])
            ksw = alloc(st, "ksw", [2, T])
            vsw = alloc(st, "vsw", [TT, 256])
            xd = alloc(st, "xd", [MT, T + 16])
            yhi = alloc(st, "yhi", [4 * MT, T], F32R)
            with ExitStack() as st2:
                ylo = alloc(st2, "ylo", [4 * MT, T], F32R)
            w1c = alloc(st, "w1c", [2, CMP_LEN * HD])
            w2c = alloc(st, "w2c", [2, HD])
            conb = alloc(st, "conb", [NCONST_B])
            gmw = alloc(st, "gmw", [MT, P])
            gmb = alloc(st, "gmb", [MT, P])
            lruw = alloc(st, "lruw", [2, MT, P])
            poolw = alloc(st, "poolw", [MT, P])
            cpe = alloc(st, "cpe", [2, CMP_LEN])
            hidc = alloc(st, "hidc", [2, 16])
            kc = alloc(st, "kc", [16])
            vc = alloc(st, "vc", [P])
            gates = alloc(st, "gates", [TT, 24])
            lru = alloc(st, "lru", [12, MT])
            sm = alloc(st, "sm", [64])
        with ExitStack() as st:
            comb = alloc(st, "comb", [EXPERTS, T])
            sg = alloc(st, "sg", [DE // P, T])
            hmid = alloc(st, "hmid", [DE // P, T])
            ehi = alloc(st, "ehi", [DE // P, T], F32R)
            elo = alloc(st, "elo", [DE // P, T], F32R)
            wr = alloc(st, "wr", [KT, 20])
            wrhi = alloc(st, "wrhi", [KT, 20], F32R)
            wrlo = alloc(st, "wrlo", [KT, 20], F32R)
            rb = alloc(st, "rb", [20])
            order4 = alloc(st, "order4", [4])
            lg = alloc(st, "lg", [TT, 20])
            ro = alloc(st, "ro", [24, TT, 4])
            cb = alloc(st, "cb", [TT, EXPERTS])
            cbt = alloc(st, "cbt", [T])

        def pcol(name, a=0, k=None):
            c0, n = PCOL[name]
            return par[:, c0 + a:c0 + (a + k if k else n)]

        def ccol(name):
            c0, n = CONST[name]
            return con[:, c0:c0 + n]

        ones, ident, rot = ccol("ones"), ccol("ident"), ccol("rot")

        def over_tiles(x, n):
            return x.unsqueeze(1).to_broadcast([P, n, x.shape[1]])

        def over_cols(x, w):
            return x.unsqueeze(2).to_broadcast([P, x.shape[1], w])

        def f32(x):
            return x.bitcast(F32)

        def mod_scale(layer, part, who):
            return modv[:, layer * 48 + part * 8:layer * 48 + part * 8 + 8, who]

        lamv = std[:]
        zfeat, fw1, fw2 = y[:, 0, :], y[:, 1, 0:HD], y[:, 1, HD:3 * HD].rearrange("p (a d) -> p a d", a=2)
        farg, frnd, fpar = y[:, 2, :], y[:, 3, :], y[:, 5, 0:4]
        decay = y[:].rearrange("p (t a) c -> p t (a c)", t=TT)
        tapf, tapb = sq[:, 0:4, :].rearrange("p (t a) c -> p t (a c)", t=TT), sq[:, 4:8, :].rearrange("p (t a) c -> p t (a c)", t=TT)

        def bcol(name):
            c0, n = CONST_B[name]
            return conb[:, c0:c0 + n]

        ug, vg, gated = gm[:, 0], gm[:, 1].rearrange("p (t a) c -> p t (a c)", t=TT), gm[:].rearrange("p a m t -> p (a m) t")
        causal, tril = bcol("causal"), bcol("tril")
        blocks = sq[:, 0:4, :].rearrange("p a c -> p (a c)")[:, 0:2 * CMP_LEN * NCMP].rearrange("p (c l n) -> p c l n", c=2, l=CMP_LEN)
        cmp_t = sq[0:NCMP].rearrange("p a c -> p (a c)").rearrange("p (u q) -> p u q", u=16)
        cmp_p = sq[:, 0, 0:2 * HEADS * NCMP].rearrange("p (t h n) -> p t h n", t=TT, h=HEADS)
        nsa_e = y[:, 0:4, :].rearrange("p (a b) k -> p a b k", a=2)
        nsa_t = y[:, 4:8, :]
        slot_of = {n: MT * b for b, n in enumerate(BRANCH_ORDER)}

        TAPS_BANK = {(0, 0): 2, (0, 1): 4, (1, 0): 4, (1, 1): 6}
        SPEC_BANK = {(0, 0): 6, (0, 1): 2, (1, 0): 6, (1, 1): 4}
        CONV_BANKS = ((2, 3, 4, 5), (6, 7, 0, 1))

        block = stack.enter_context(nc.Block())

        @block.sync
        def _(sp):
            W = A["weights"]
            for dst, src in [(cvec[:], A["cvec"]), (con[:], A["const"]), (par[:], A["params"]),
                             (lamv, A["attn_lambda"].partition_broadcast(P))]:
                sp.dma_start(dst, src).then_inc(s("small_loaded"), 16)
            sp.dma_start(h[:], A["x"]).then_inc(s("x_loaded"), 16)
            for j in range(4):
                if j == 2:
                    sp.dma_start(ctx[:], A["ctx"]).then_inc(s("ctx_loaded"), 16)
                sp.dma_start(mstart[:, 2 * j:2 * j + 2, :], A["mod_start"][:, 2 * j:2 * j + 2, :]).then_inc(s(f"start_loaded{j}"), 16)
            for i in range(RING):
                sp.dma_start(raw[:, i, :], W[i]).then_inc(s(f"raw_loaded{i}"), 16)
            turns, rest = divmod(n_chunks - RING, RING)
            with sp.Fori(0, turns) as n:
                for j in range(RING):
                    sp.wait_ge(s("lo_ready"), n * RING + (j + 1))
                    sp.dma_start(raw[:, j, :], W[bass.ds(n * RING + (RING + j), 1)].rearrange("a p c -> (a p) c"))\
                        .then_inc(s(f"raw_loaded{j}"), 16)
            for j in range(rest):
                i = RING * (turns + 1) + j
                sp.wait_ge(s("lo_ready"), i - RING + 1)
                sp.dma_start(raw[:, j, :], W[i]).then_inc(s(f"raw_loaded{j}"), 16)
            sp.wait_ge(s("result_ready"), 1)
            sp.dma_start(out, y[:]).then_inc(s("stored"), 16)
            sp.wait_ge(s("stored"), 16)

        @block.tensor
        def _(pe):
            mm = nc.tensor.matmul

            def three(o, w0, w1, x0, x1, first, last, **kw):
                mm(o, w0, x0, start=first, stop=False, **kw)
                mm(o, w1, x0, start=False, stop=False, **kw)
                return mm(o, w0, x1, start=False, stop=last, **kw)

            def three_rows(mm, o, a0, a1, w0, w1, first, last):
                mm(o, a0, w0, start=first, stop=False)
                mm(o, a0, w1, start=False, stop=False)
                return mm(o, a1, w0, start=False, stop=last)

            def weights_ready(i, n=None, step=0):
                pe.wait_ge(s("lo_ready"), up(i + 1, n, step))

            def used(ins):
                ins.then_inc(s("chunk_used"), 1)

            def tiles(i, bank_of, xs, kts=8, width=2, cols=T, k0=0, first=True, last=True, x_wait=None):
                sl = i % RING
                span = P * width
                for m in range(width):
                    for x_i, (x0, x1) in enumerate(xs):
                        o = bank_of(m, x_i)
                        for k in range(kts):
                            if x_wait and m == 0 and k % 4 == 0 and x_i == len(xs) - 1:
                                pe.wait_ge(*nth(x_wait, "lo", k // 4 + 1))
                            w = k * span + m * P
                            ins = three(o, whi[:, sl, w:w + P], wlo[:, sl, w:w + P], x0[:, k0 + k, :], x1[:, k0 + k, :],
                                        first and k == 0, last and k == kts - 1)
                return ins

            def by_token(i, out_of, xs, ncols=256):
                sl = i % RING
                tt = 0
                for x0, x1 in xs:
                    for t0 in range(TT):
                        o = out_of(tt)
                        tt += 1
                        for k in range(KT):
                            w0, w1 = (w[:, sl, k * 256:k * 256 + ncols] for w in (whi, wlo))
                            a0, a1 = (x[:, k, t0 * P:(t0 + 1) * P] for x in (x0, x1))
                            mm(o, a0, w0, start=k == 0, stop=False)
                            mm(o, a0, w1, start=False, stop=False)
                            ins = mm(o, a1, w0, start=False, stop=k == KT - 1)
                return ins

            def modulation(i, q, n=None, step=0, turn=0):
                pe.wait_ge(s("mod_drained"), up(q + 1, n, turn))
                weights_ready(i, n, step)
                for m in range(2):
                    ins = mm(ps[:, 7, m:m + 1], macc[:, i % RING, m * P:(m + 1) * P], ones[:, 0:1], start=True, stop=True)
                used(ins)

            def sum_squares(tag, bank, src=sq, counts=2):
                per = KT // counts
                for c in range(counts):
                    pe.wait_ge(*nth(tag, "squares", c + 1))
                    for k in range(c * per, (c + 1) * per):
                        ins = mm(ps[:, bank, 0:T], ones, src[:, k, :], start=k == 0, stop=k == KT - 1)
                ins.then_inc(s("sumsq"), 1)

            def filter_layer(j):
                if j == 0:
                    pe.wait_ge(s("filter_loaded"), 16 * 4)
                    w, x = fw1[0:33, :], zfeat[0:33, :]
                else:
                    pe.wait_ge(s("filter_sin"), j)
                    w, x = fw2[0:HD, j - 1, :], hdn[0:HD, :]
                mm(ps[0:HD, 6, 0:T], w, x, start=True, stop=True).then_inc(s("filter_layer"), 1)

            def filter_taps(half, t0):
                r, b = 2 * half + t0, TAPS_BANK[half, t0]
                if r == 0:
                    pe.wait_ge(s("hyena_loaded"), 16 * 3)
                elif r == 2:
                    pe.wait_ge(s("taps_ready"), 2)
                elif r == 3:
                    pe.wait_ge(s("spec_stored"), 1)
                for d in range(2):
                    ins = mm(ps[:, b + d, :], hdn[0:HD, t0 * P:(t0 + 1) * P],
                             fwo[0:HD, d * D + half * 512:d * D + half * 512 + 512], start=True, stop=True)
                ins.then_inc(s("filter_taps"), 1)

            def filter_spec(half, kind):
                pe.wait_ge(s("taps_ready"), 2 * half + 2)
                b = SPEC_BANK[half, kind]
                for k in range(2):
                    for t0 in range(TT):
                        ins = mm(ps[:, b + k, :], dft[:, t0, (2 * kind + k) * P:(2 * kind + k + 1) * P],
                                 (tapf if kind else taps)[:, t0, :], start=t0 == 0, stop=t0 == 1)
                ins.then_inc(s("filter_spec"), 1)

            pe.wait_ge(s("c_silu"), 1)
            for j in range(0, START_TILES // 2, 2):
                pe.wait_ge(s(f"start_loaded{j // 2}"), 16)
                if j == 2:
                    sum_squares("x", 4)
                for m in range(2):
                    for k in range(KT):
                        w = k * 2 * P + m * P
                        mm(ps[:, 7, 4 * j + 2 * m:4 * j + 2 * m + 2], mstart[:, j, w:w + P], csil[:, k, :], start=k == 0, stop=k == KT - 1)
            for j in range(1, START_TILES // 2, 2):
                pe.wait_ge(s("start_weighted"), (j + 1) // 2)
                for w in range(2):
                    for m in range(2):
                        c = 4 * j + 2 * m + w
                        ins = mm(ps[:, 7, c:c + 1], start_acc[:, j // 2, w, m * P:(m + 1) * P], ones[:, 0:1], start=True, stop=True)
            ins.then_inc(s("mod_start"), 1)

            sum_squares("ctx", 5, src=y)
            lat, con_x = (uhi, ulo), (ctx_hi, ctx_lo)

            def rope(r):
                pe.wait_ge(s("qkv_drained"), r + 1)
                if r >= 2:
                    pe.wait_ge(s("rope_drained"), r - 1)
                src = kbuf[:, 2 * r:2 * r + 2, T:2 * T] if r < 4 else qbuf[:, 2 * (r - 4):2 * (r - 4) + 2, :]
                mm(ps[:, 4 + r % 2, :], rot, src, start=True, stop=True).then_inc(s("roped"), 1)

            pe.wait_ge(*nth("ctx", "lo", 2))
            pe.wait_ge(*nth("x", "std", 1))
            pe.wait_ge(*nth("ctx", "std", 1))
            for i, g, q in items(I_QKV, I_ATT):
                if g is None:
                    modulation(i, q)
                    continue
                b = 2 * (g % 2)
                if g >= 2:
                    pe.wait_ge(s("qkv_drained"), g - 1)
                weights_ready(i)
                if g < 4:
                    ins = tiles(i, lambda m, x_i: ps[:, b + m, x_i * T:(x_i + 1) * T], [con_x, lat],
                                x_wait="x" if g == 0 else None)
                elif g < 8:
                    ins = tiles(i, lambda m, _: ps[:, b, m * T:(m + 1) * T], [lat])
                else:
                    ins = by_token(i, lambda tt: ps[:, b + tt // 2, (tt % 2) * 256:(tt % 2) * 256 + 256], [con_x, lat])
                used(ins)
                if 1 <= g <= 8:
                    rope(g - 1)
                if g >= 9:
                    filter_layer(g - 9)

            def scores(u):
                hd, qt = divmod(u, 2)
                if u >= 2:
                    pe.wait_ge(s("exps"), u - 1)
                for p in range(2):
                    a = slice(p * HD, (p + 1) * HD)
                    ins = mm(ps[:, 2 * (u % 2) + p, :], qbuf[a, hd, qt * P:(qt + 1) * P], kbuf[a, hd, :], start=True, stop=True)
                ins.then_inc(s("scores"), 1)

            def turn_weights(u):
                pe.wait_ge(s("att_ready"), u + 1)
                if u >= 2:
                    pe.wait_ge(s("att_copied"), u - 1)
                for k in range(4):
                    ins = nc.tensor.transpose(ps[:, 4 + u % 2, k * P:(k + 1) * P], ebuf[:, u % 2, 0, k * P:(k + 1) * P], ident)
                ins.then_inc(s("att_turned"), 1)

            def values(hd):
                pe.wait_ge(s("att_copied"), 2 * hd + 2)
                if hd:
                    pe.wait_ge(s("o_copied"), hd)
                for k in range(4):
                    ins = mm(ps[:, 6, 0:T], vbuf[:, k, hd * P:(hd + 1) * P], atb[:, hd % 2, k, :], start=k == 0, stop=k == 3)
                ins.then_inc(s("o_ready"), 1)

            pe.wait_ge(s("roped_all"), 8)
            pe.wait_ge(s("qkv_drained"), 12)
            pe.wait_ge(s("filter_arg"), 3)
            for u in range(2 * HEADS + 4):
                if u < 2 * HEADS:
                    scores(u)
                if 2 <= u <= 2 * HEADS + 1:
                    turn_weights(u - 2)
                if u >= 5 and u % 2:
                    values((u - 5) // 2)
                if u % 2 == 0 and u < 2 * HEADS:
                    modulation(I_ATT + u // 2, MODS.index(I_ATT + u // 2))
            for c in range(4):
                pe.wait_ge(s("o_squares"), 2 * c + 2)
                pe.wait_ge(s("exps"), 16)
                mm(ps[:, c, :], ones, sq[:, 2 * c:2 * c + 2, :], start=True, stop=True).then_inc(s("o_sumsq"), 1)

            def out_rows(tag, i0, xs=(uhi, ulo), x_wait=None, wait_each=None):
                for g in range(4):
                    weights_ready(i0 + g)
                    used(tiles(i0 + g, lambda m, _: ps[:, g, m * T:(m + 1) * T], [xs], x_wait=x_wait if g == 0 else None))
                sum_squares(tag, 4, counts=4)

            for c in range(4):
                pe.wait_ge(s("o_std"), c + 1)
            pe.wait_ge(s("o_lo"), 4)
            out_rows("post0", I_AO)

            def mlp(layer, tag, i0):
                sum_squares(tag + "_in", 5)
                slots, turns, rest, body, first_mod = mlp_plan(layer)
                with pe.Fori(0, turns) as n:
                    for i, g, q in body:
                        if g is None:
                            modulation(i, q, n, len(body), len(body) - slots)
                            continue
                        pe.wait_ge(*mlp_nth(tag, "free", up(g + 1, n, slots)))
                        weights_ready(i, n, len(body))
                        used(tiles(i, lambda m, _: ps[:, g, m * T:(m + 1) * T], [(uhi, ulo)], x_wait=tag + "_in" if g == 0 else None))
                for r in range(rest):
                    pe.wait_ge(*mlp_nth(tag, "free", slots * turns + r + 1))
                    weights_ready(i0 + len(body) * turns + r)
                    used(tiles(i0 + len(body) * turns + r, lambda m, _: ps[:, r, m * T:(m + 1) * T], [(uhi, ulo)]))
                pe.wait_ge(*mlp_nth(tag, "free", 16 + slots))
                for i, g, q in items(*out_span(layer)):
                    if g is None:
                        modulation(i, q)
                        continue
                    m0, kg = divmod(g, 4)
                    if kg == 0:
                        pe.wait_ge(*mlp_nth(tag, "yfree", m0 + 1))
                    if m0 == 0:
                        pe.wait_ge(*mlp_nth(tag, "hidden", 4 * kg + 4))
                    weights_ready(i)
                    used(tiles(i, lambda m, _: ps[:, 2 * (m0 % 2) + m, 0:T], [(hid_hi, hid_lo)], k0=8 * kg,
                               first=kg == 0, last=kg == 3))
                sum_squares(tag, 4, counts=4)

            if on("mlp0"):
                mlp(0, "mlp0", I_MLP0)

            def turn_v(j):
                pe.wait_ge(s("v_ready"), j + 1)
                if j < 2:
                    pe.wait_ge(s("spec_stored"), 2)
                else:
                    pe.wait_ge(s("vtok_stored"), j - 1)
                for m in range(2):
                    for t0 in range(TT):
                        ins = nc.tensor.transpose(ps[:, 2 + j % 2, (2 * m + t0) * P:(2 * m + t0 + 1) * P],
                                                  hv[:, 2 * j + m, t0 * P:(t0 + 1) * P], ident)
                ins.then_inc(s("v_turned"), 1)

            if on("hyena"):
                sum_squares("hy_in", 5)
                for g in range(12):
                    if g >= 2:
                        pe.wait_ge(s("hy_drained"), g - 1)
                    weights_ready(I_HY + g)
                    used(tiles(I_HY + g, lambda m, _: ps[:, g % 2, m * T:(m + 1) * T], [(uhi, ulo)], x_wait="hy_in" if g == 0 else None))
                    if g == 0:
                        pe.wait_ge(s("mod_drained"), mods_before(I_HY) + 1)
                    if g in (1, 2):
                        filter_taps(0, g - 1)
                    if g in (4, 5):
                        filter_spec(0, g - 4)
                    if g in (5, 6):
                        filter_taps(1, g - 5)
                    if g in (7, 9):
                        turn_v(g - 7)
                        turn_v(g - 6)
                    if g in (8, 9):
                        filter_spec(1, g - 8)
                pe.wait_ge(s("vtok_stored"), 4)
                for half in range(2):
                    pe.wait_ge(s("spec_stored"), 4)
                    if half:
                        pe.wait_ge(s("hy_drained"), 12)
                    for k in range(4):
                        for t0 in range(TT):
                            ins = mm(ps[:, CONV_BANKS[half][k], :], dft[:, t0, k * P:(k + 1) * P], vtok[:, t0, half * 512:half * 512 + 512],
                                     start=t0 == 0, stop=t0 == 1)
                    ins.then_inc(s("vspec"), 1)
                for half in range(2):
                    pe.wait_ge(s("yspec_ready"), half + 1)
                    for m in range(4):
                        for k in range(4):
                            ins = mm(ps[:, CONV_BANKS[half][m], 0:T], yspec[:, half, k, m * P:(m + 1) * P], idft[:, k, :], start=k == 0, stop=k == 3)
                        ins.then_inc(s("conv"), 1)
                out_rows("post1", I_HO, x_wait="hy")
            if on("mlp1"):
                mlp(1, "mlp1", I_MLP1)

            u_parts = (uhi, ulo)

            def compress():
                pe.wait_ge(s("blocks_ready"), 1)
                pe.wait_ge(s("cmp_loaded"), 16 * 2)
                for g in range(2):
                    a = slice(g * HD, (g + 1) * HD)
                    for c in range(2):
                        for l in range(CMP_LEN):
                            ins = mm(ps[a, 4, 16 * c:16 * c + NCMP], w1c[a, c, l * HD:(l + 1) * HD], blocks[a, c, l, :],
                                     start=l == 0, stop=l == CMP_LEN - 1)
                ins.then_inc(s("cmp_hidden"), 1)

            def compress_out():
                pe.wait_ge(s("cmp_gelu"), 1)
                for g in range(2):
                    a = slice(g * HD, (g + 1) * HD)
                    mm(ps[a, 5, 0:NCMP], w2c[a, 0, :], hidc[a, 0, 0:NCMP], start=True, stop=True)
                    ins = mm(ps[0:NCMP, 6 + g, 0:HD], hidc[a, 1, 0:NCMP], w2c[a, 1, :], start=True, stop=True)
                ins.then_inc(s("cmp_out"), 1)

            def head(u):
                return u // 4, (u // 2) % 2, u % 2

            def nsa_scores(u):
                j, g, qt = head(u)
                a = slice(g * HD, (g + 1) * HD)
                if u >= 2:
                    pe.wait_ge(s("nsa_exps"), u - 1)
                for b in range(2):
                    ins = mm(ps[:, u % 2, b * T:b * T + (qt + 1) * P], qn[a, j, qt * P:(qt + 1) * P], ksw[a, b, 0:(qt + 1) * P],
                             start=True, stop=True)
                ins.then_inc(s("nsa_scores"), 1)

            def nsa_turn(u):
                j, g, qt = head(u)
                pe.wait_ge(s("nsa_weights"), u + 1)
                if u >= 2:
                    pe.wait_ge(s("nsa_copied"), u - 1)
                for b in range(2):
                    for k in range(qt + 1):
                        n = b * (qt + 1) + k
                        ins = nc.tensor.transpose(ps[:, 2 + u % 2, n * P:(n + 1) * P], nsa_e[:, u % 2, b, k * P:(k + 1) * P], ident)
                ins.then_inc(s("nsa_turned"), 1)

            def nsa_values(u):
                j, g, qt = head(u)
                pe.wait_ge(s("nsa_copied"), u + 1)
                if u % 4 == 0 and j >= 2:
                    pe.wait_ge(s("nsa_out_lo"), j - 1)
                o = ps[g * HD:(g + 1) * HD, 4 + j % 2, qt * P:(qt + 1) * P]
                for b in range(2):
                    for k in range(qt + 1):
                        n = b * (qt + 1) + k
                        mm(o, vsw[:, k, b * P + g * HD:b * P + (g + 1) * HD], nsa_t[:, 2 * (u % 2) + n // 2, (n % 2) * P:(n % 2 + 1) * P],
                           start=n == 0, stop=False)
                mm(o, vc[0:NCMP, g * HD:(g + 1) * HD], cmp_t[:, qt * 8 + g * 4 + j, :], start=False, stop=True).then_inc(s("nsa_out"), 1)

            if on("mixer"):
                sum_squares("mix_in", 5)
                for g in range(16):
                    i = I_PROJ + g
                    if g >= 4:
                        pe.wait_ge(s("proj_drained"), g - 3)
                    weights_ready(i)
                    if g in (4, 12, 13):
                        ins = by_token(i, lambda tt: ps[:, g % 4, tt * 256:tt * 256 + 256], [u_parts])
                    elif g == 5:
                        ins = by_token(i, lambda tt: ps[:, g % 4, tt * 256:tt * 256 + 24], [u_parts], 24)
                    else:
                        ins = tiles(i, lambda m, _: ps[:, g % 4, m * T:(m + 1) * T], [u_parts], x_wait="mix_in" if g == 0 else None)
                    used(ins)
                    if g == 2:
                        compress()
                    if g == 4:
                        compress_out()
                pe.wait_ge(s("v_normed"), 1)
                pe.wait_ge(s("cmp_stored"), 1)
                for n in range(TT):
                    for g in range(MT):
                        ins = mm(ps[:, 4 + g // 2, (g % 2) * T + n * P:(g % 2) * T + (n + 1) * P], vg[:, n, g * P:(g + 1) * P], gmw[:, g, :],
                                 start=True, stop=True)
                ins.then_inc(s("gm_mixed"), 1)
                pe.wait_ge(s("pooled"), 1)
                for g in range(MT):
                    ins = mm(ps[:, 6 + g // 2, (g % 2) * T:(g % 2 + 1) * T], poolw[:, g, :], xd[:, g, 16:16 + T], start=True, stop=True)
                ins.then_inc(s("pool_mapped"), 1)
                pe.wait_ge(s("rec_conved"), 1)
                pe.wait_ge(s("lru_loaded"), 16 * 4)
                pe.wait_ge(s("proj_drained"), 16)
                for w in range(2):
                    for m in range(MT):
                        ins = mm(ps[:, 2 * w + m // 2, (m % 2) * T:(m % 2 + 1) * T], lruw[:, w, m, :], sq[:, m, :], start=True, stop=True)
                ins.then_inc(s("rec_gates"), 1)
                pe.wait_ge(s("lru_done"), 1)
                pe.wait_ge(s("pool_lo"), 1)
                pe.wait_ge(s("gm_lo"), 1)
                for qt in range(2):
                    for g in range(2):
                        a = slice(g * HD, (g + 1) * HD)
                        for j in range(4):
                            ins = mm(ps[:, 4 + 2 * qt + g, 16 * j:16 * j + NCMP], qn[a, j, qt * P:(qt + 1) * P], kc[a, 0:NCMP], start=True, stop=True)
                ins.then_inc(s("cmp_scores"), 1)
                pe.wait_ge(s("cmp_weights"), 1)
                for u in range(16):
                    ins = nc.tensor.transpose(ps[0:NCMP, u // 4, (u % 4) * P:(u % 4 + 1) * P], cmp_p[:, u // 8, u % 8, :], ident)
                ins.then_inc(s("cmp_turned"), 1)
                pe.wait_ge(s("cmp_t_ready"), 1)
                for u in range(19):
                    if u < 16:
                        nsa_scores(u)
                    if 2 <= u <= 17:
                        nsa_turn(u - 2)
                    if 3 <= u:
                        nsa_values(u - 3)
                pe.wait_ge(s("nsa_out_lo"), 4)
                pe.wait_ge(s("nsa_out_hi"), 4)
                with pe.Fori(0, 4) as n:
                    for g in range(6):
                        i = I_BR + g
                        if g < 4:
                            pe.wait_ge(s("mg_free"), up(g + 1, n, 4))
                        else:
                            pe.wait_ge(s("br_free"), up(g - 3, n, 2))
                        weights_ready(i, n, 6)
                        if g < 4:
                            used(tiles(i, lambda m, _: ps[:, g, m * T:(m + 1) * T], [u_parts]))
                        else:
                            w = i % RING
                            for m in range(4):
                                o = ps[:, 2 * g - 4 + m // 2, (m % 2) * T:(m % 2 + 1) * T]
                                for k in range(MT):
                                    x0, x1 = (v[:, bass.ds(n * MT + k, 1), :].rearrange("p a t -> p (a t)") for v in (yhi, ylo))
                                    c = k * 512 + m * P
                                    ins = three(o, whi[:, w, c:c + P], wlo[:, w, c:c + P], x0, x1, k == 0, k == MT - 1)
                            used(ins)
                pe.wait_ge(s("mg_free"), 20)
                for g in range(4):
                    weights_ready(I_WO + g)
                    used(tiles(I_WO + g, lambda m, _: ps[:, g, m * T:(m + 1) * T], [u_parts], x_wait="merged" if g == 0 else None))

            if on("all"):
                sum_squares("moe_in", 5)
                pe.wait_ge(*nth("moe_in", "lo", 2))
                pe.wait_ge(s("router_lo"), 1)
                for t0 in range(TT):
                    for k in range(KT):
                        a0, a1 = (x[:, k, t0 * P:(t0 + 1) * P] for x in u_parts)
                        ins = three_rows(mm, ps[:, 4, t0 * 32:t0 * 32 + 20], a0, a1, wrhi[:, k, :], wrlo[:, k, :], k == 0, k == KT - 1)
                ins.then_inc(s("router"), 1)
                pe.wait_ge(*nth("mixed", "h", 2))

                def up_rows(i, bank, n=None):
                    weights_ready(i, n, 6)
                    used(tiles(i, lambda m, _: ps[:, bank, m * T:(m + 1) * T], [u_parts]))

                def down_rows(i, j, n=None):
                    if n is None:
                        pe.wait_ge(s("moe_hid"), 2 * EXPERTS)
                        pe.wait_ge(s("moe_free"), 2 * EXPERTS - 2 + j + 1)
                    else:
                        pe.wait_ge(s("moe_hid"), n * 2 + 2)
                        pe.wait_ge(s("moe_free"), n * 2 + (j + 1))
                    weights_ready(i, n, 6)
                    used(tiles(i, lambda m, _: ps[:, 4 + 2 * j + m // 2, (m % 2) * T:(m % 2 + 1) * T], [(ehi, elo)], kts=4, width=4))

                for j in range(4):
                    up_rows(I_MOE + j, j)
                pe.wait_ge(s("combine_ready"), 1)
                for t0 in range(TT):
                    ins = nc.tensor.transpose(ps[0:EXPERTS, 5, t0 * P:(t0 + 1) * P], cb[:, t0, :], ident)
                ins.then_inc(s("combine_turned"), 1)
                pe.wait_ge(s("combine_copied"), 1)
                for e in range(EXPERTS):
                    if e >= 8 and e % 2 == 0:
                        pe.wait_ge(s("comb_stored"), (e - 8) // 2 + 1)
                    ins = mm(ps[:, 4 + (e // 2) % 4, (e % 2) * T:(e % 2 + 1) * T], ident[0:EXPERTS, e:e + 1].to_broadcast([EXPERTS, P]),
                             cbt[0:EXPERTS, :], start=True, stop=True)
                    if e % 2:
                        ins.then_inc(s("comb_spread"), 1)
                with pe.Fori(0, EXPERTS - 1) as n:
                    i = I_MOE + 4
                    for j in range(2):
                        pe.wait_ge(s("moe_silu"), n * 2 + (j + 1))
                        up_rows(i + j, j, n)
                    for j in range(2):
                        down_rows(i + 2 + j, j, n)
                    for j in range(2):
                        pe.wait_ge(s("moe_gated"), n * 2 + (j + 1))
                        up_rows(i + 4 + j, 2 + j, n)
                for j in range(2):
                    down_rows(N_CHUNKS - 2 + j, j)
                sum_squares("final", 0)

        @block.scalar
        def _(act):
            fn = nc.scalar.activation
            def split(i, n=None, step=0):
                if i >= n_chunks and n is None or i in MODS:
                    return
                sl = i % RING
                act.wait_ge(s(f"raw_loaded{sl}"), up(16 * (i // RING + 1), n, 16 * step // RING))
                if i >= RING:
                    act.wait_ge(s("chunk_used"), up(i - RING + 1, n, step))
                fn(whi[:, sl, :], raw[:, sl, :], ACT.Copy).then_inc(s("hi_ready"), 1)

            def product(i, n=None, step=0):
                act.wait_ge(s("chunk_used"), up(i + 1, n, step))

            chain = Chain(act, "act_chain")
            eps = ccol("eps")

            def squares(tag, src, dst=sq):
                for c in range(2):
                    fn(dst[:, 4 * c:4 * c + 4, :], src[:, 4 * c:4 * c + 4, :], ACT.Square).then_inc(s("squares"), 1)

            def root(tag, bank):
                act.wait_ge(*nth(tag, "sumsq", 1))
                fn(std[:], ps[:, bank, 0:T], ACT.Sqrt, bias=eps, scale=1.0 / D).then_inc(s("std"), 1)

            def high(tag, src, dst):
                for c in range(2):
                    act.wait_ge(*nth(tag, "normed", c + 1))
                    fn(dst[:, 4 * c:4 * c + 4, :], src[:, 4 * c:4 * c + 4, :], ACT.Copy).then_inc(s("hi"), 1)

            def next_squares(tag, prev):
                for c in range(2):
                    act.wait_ge(*nth(prev, "h", c + 1))
                    fn(sq[:, 4 * c:4 * c + 4, :], h[:, 4 * c:4 * c + 4, :], ACT.Square).then_inc(s("squares"), 1)

            act.wait_ge(s("small_loaded"), 16 * 4)
            fn(csil[:], cvec[:], ACT.Tanh, scale=0.5).then_inc(s("c_tanh"), 1)
            act.wait_ge(s("x_loaded"), 16)
            act.wait_ge(s("lam_sums"), 1)
            squares("x", h)
            root("x", 4)
            act.wait_ge(s("ctx_loaded"), 16)
            squares("ctx", ctx, y)
            split(0)
            high("x", y, uhi)
            root("ctx", 5)
            high("ctx", ctx, ctx_hi)
            for i in range(1, RING):
                split(i)

            def filter_sin(j):
                act.wait_ge(s("filter_arg"), j + 1)
                fn(hdn[0:HD, :], farg[0:HD, :], ACT.Sin).then_inc(s("filter_sin"), 1)

            act.wait_ge(*nth("x", "lo", 2))
            for dst, src in [(zfeat[0:33, :], A["zfeat"]), (fw1[0:33, :], A["hy_filt_w1"]), (fw2[0:HD], A["hy_filt_w2"]),
                             (fpar[0:HD, :], A["fpar"])]:
                act.dma_start(dst, src).then_inc(s("filter_loaded"), 16)
            for i, g, q in items(I_QKV, I_ATT):
                if g is None:
                    split(i + RING)
                    continue
                b = 2 * (g % 2)
                product(i)
                if g < 4:
                    ins = fn(kbuf[:, 2 * g:2 * g + 2, :], ps[:, b:b + 2, :], ACT.Copy)
                elif g < 8:
                    ins = fn(qbuf[:, 2 * (g - 4):2 * (g - 4) + 2, :], ps[:, b, :].rearrange("p (m t) -> p m t", m=2), ACT.Copy)
                else:
                    v0 = (g - 8) * 256
                    ins = fn(vbuf[:, :, v0:v0 + 256], ps[:, b:b + 2, :].rearrange("p b (t c) -> p (b t) c", t=2), ACT.Copy)
                ins.then_inc(s("qkv_drained"), 1)
                split(i + RING)
                if g >= 10:
                    filter_sin(g - 10)
            filter_sin(2)

            def exps(u):
                act.wait_ge(s("max_ready"), u + 1)
                if u >= 2:
                    act.wait_ge(s("att_turned"), u - 1)
                for p in range(2):
                    ins = fn(ebuf[:, u % 2, p, :], ps[:, 2 * (u % 2) + p, :], ACT.Exp, scale=SCALE,
                             bias=small[:, 4 * (u % 2) + p:4 * (u % 2) + p + 1],
                             accum_out=small[:, 8 + 4 * (u % 2) + p:9 + 4 * (u % 2) + p])
                ins.then_inc(s("exps"), 1)

            fn(small[:, 24:26], small[:, 22:24], ACT.Exp).then_inc(s("lam_exps"), 1)
            for u in range(2 * HEADS + 4):
                if u < 2 * HEADS:
                    exps(u)
                if 2 <= u <= 2 * HEADS + 1:
                    v = u - 2
                    act.wait_ge(s("att_turned"), v + 1)
                    if v >= 4:
                        act.wait_ge(s("o_ready"), v // 2 - 1)
                    fn(atb[:, (v // 2) % 2, :, (v % 2) * P:(v % 2 + 1) * P], ps[:, 4 + v % 2, :].rearrange("p (k q) -> p k q", k=4),
                       ACT.Copy).then_inc(s("att_copied"), 1)
                if u % 2 == 0 and u < 2 * HEADS:
                    split(I_ATT + u // 2 + RING)
                if u >= 5 and u % 2:
                    hd = (u - 5) // 2
                    act.wait_ge(s("o_ready"), hd + 1)
                    fn(sq[:, hd, :], ps[:, 6, 0:T], ACT.Square).then_inc(s("o_squares"), 1)
                    fn(obuf[:, hd, :], ps[:, 6, 0:T], ACT.Copy).then_inc(s("o_copied"), 1)
            for c in range(4):
                act.wait_ge(s("o_sumsq"), c + 1)
                fn(y[:, 2 * c:2 * c + 2, :], ps[:, c, :].rearrange("p (m t) -> p m t", m=2), ACT.Sqrt, bias=eps, scale=1.0 / P).then_inc(s("o_std"), 1)
            for c in range(4):
                act.wait_ge(s("o_normed"), c + 1)
                fn(uhi[:, 2 * c:2 * c + 2, :], obuf[:, 2 * c:2 * c + 2, :], ACT.Copy).then_inc(s("o_hi"), 1)

            def take_rows(tag, i0, bias=None):
                for g in range(4):
                    product(i0 + g)
                    dst = slice(2 * g, 2 * g + 2)
                    if bias is None:
                        src = ps[:, g, :].rearrange("p (m t) -> p m t", m=2)
                        fn(y[:, dst, :], src, ACT.Copy)
                        fn(sq[:, dst, :], src, ACT.Square).then_inc(s("squares"), 1)
                    else:
                        for m in range(2):
                            b = pcol(bias, 2 * g + m, 1)
                            fn(y[:, 2 * g + m, :], ps[:, g, m * T:(m + 1) * T], ACT.Identity, bias=b)
                            ins = fn(sq[:, 2 * g + m, :], ps[:, g, m * T:(m + 1) * T], ACT.Square, bias=b)
                        ins.then_inc(s("squares"), 1)
                    split(i0 + g + RING)

            take_rows("post0", I_AO)
            root("post0", 4)

            def relu_squared(tag, g, c, n=None, step=0):
                act.wait_ge(*mlp_nth(tag, "rfree", up(c + 1, n, step)))
                r = y[:, 2 * g:2 * g + 2, :]
                chain(fn(r, ps[:, g, :].rearrange("p (m t) -> p m t", m=2), ACT.Relu))
                act.sem_inc(s("mlp_free"), 1)
                dst = hid_hi[:, 2 * c:2 * c + 2, :] if n is None else hid_hi[:, bass.ds(n * (2 * step) + 2 * c, 2), :]
                fn(dst, r, ACT.Square).then_inc(s("mlp_hid_hi"), 1)

            def mlp(layer, tag, i0, prev):
                next_squares(tag + "_in", prev)
                root(tag + "_in", 5)
                high(tag + "_in", y, uhi)
                slots, turns, rest, body, _ = mlp_plan(layer)
                act.drain().then_inc(s("mlp_free"), slots)
                with act.Fori(0, turns) as n:
                    chain.enter(n, slots)
                    for i, g, q in body:
                        if g is not None:
                            product(i, n, len(body))
                            relu_squared(tag, g, g, n, slots)
                        split(i + RING, n, len(body))
                chain.leave(turns)
                for r in range(rest):
                    i = i0 + len(body) * turns + r
                    product(i)
                    relu_squared(tag, r, slots * turns + r)
                    split(i + RING)
                act.drain().then_inc(s("mlp_yfree"), 2)
                act.wait_ge(*mlp_nth(tag, "hidden", 16))
                for i, g, q in items(*out_span(layer)):
                    if g is None:
                        split(i + RING)
                        continue
                    m0, kg = divmod(g, 4)
                    product(i)
                    if kg == 3:
                        src = ps[:, 2 * (m0 % 2):2 * (m0 % 2) + 2, 0:T]
                        fn(y[:, 2 * m0:2 * m0 + 2, :], src, ACT.Copy)
                        fn(sq[:, 2 * m0:2 * m0 + 2, :], src, ACT.Square).then_inc(s("squares"), 1)
                        act.drain().then_inc(s("mlp_yfree"), 1)
                    split(i + RING)
                root(tag, 4)

            if on("mlp0"):
                mlp(0, "mlp0", I_MLP0, "post0")

            def store_spec(half, kind):
                act.wait_ge(s("filter_spec"), 2 * half + kind + 1)
                fn(spec[:, 2 * kind:2 * kind + 2, half * 512:half * 512 + 512],
                   ps[:, SPEC_BANK[half, kind]:SPEC_BANK[half, kind] + 2, :], ACT.Copy).then_inc(s("spec_stored"), 1)

            def turned(j):
                act.wait_ge(s("v_turned"), j + 1)
                fn(vtok[:, :, 2 * j * P:(2 * j + 2) * P].rearrange("p t (m c) -> p m t c", m=2),
                   ps[:, 2 + j % 2, :].rearrange("p (m t c) -> p m t c", m=2, t=TT), ACT.Copy).then_inc(s("vtok_stored"), 1)

            if on("hyena"):
                for dst, src in [(fwo[0:HD, :], A["hy_filt_w_out"]), (dft[:], A["dft"]), (idft[:], A["idft"])]:
                    act.dma_start(dst, src).then_inc(s("hyena_loaded"), 16)
                next_squares("hy_in", "mlp0")
                root("hy_in", 5)
                high("hy_in", y, uhi)
                act.wait_ge(*nth("hy_in", "lo", 2))
                act.dma_start(y[:].rearrange("p a c -> p (a c)"), A["decay"].rearrange("p t c -> p (t c)")).then_inc(s("decay_loaded"), 16)
                for g in range(12):
                    product(I_HY + g)
                    if g == 0:
                        act.wait_ge(s("zpad_clear"), 1)
                    if g >= 2:
                        act.wait_ge(s("hy_conved"), g - 1)
                    first = (16, 8, 0)[g // 4] + 2 * (g % 4)
                    for m in range(2):
                        ins = fn(zpad[:, g % 2, m, 1:T + 1], ps[:, g % 2, m * T:(m + 1) * T], ACT.Identity, bias=pcol("hy_b_in", first + m, 1))
                    ins.then_inc(s("hy_drained"), 1)
                    split(I_HY + g + RING)
                    if g in (5, 6):
                        store_spec(0, g - 5)
                    if g in (9, 10):
                        store_spec(1, g - 9)
                    if g in (8, 10):
                        turned(g - 8)
                        turned(g - 7)
                for half in range(2):
                    a = slice(4 * half, 4 * half + 4)
                    act.wait_ge(*nth("hy", "normed", half + 1))
                    fn(uhi[:, a, :], hv[:, a, :], ACT.Copy).then_inc(s("hi"), 1)
                take_rows("post1", I_HO, "hy_b_out")
                root("post1", 4)
            if on("mlp1"):
                mlp(1, "mlp1", I_MLP1, "post1")

            def halves(m):
                return m.rearrange("p (m t) -> p m t", m=2)

            def head(u):
                return u // 4, (u // 2) % 2, u % 2

            def part(name, b, src):
                act.wait_ge(s(name + "_ready"), 1)
                fn(yhi[:, b:b + MT, :], src, ACT.Copy).then_inc(s(name + "_hi"), 1)

            if on("mixer"):
                for dst, src in [(w1c[:], A["cmp_w1"]), (w2c[:], A["cmp_w2"])]:
                    act.dma_start(dst, src).then_inc(s("cmp_loaded"), 16)
                act.wait_ge(s("lru_clear"), 1)
                for dst, src in [(conb[:], A["const_b"]), (cpe[:], A["cmp_pe"]), (gmw[:], A["gm_ws"]),
                                 (gmb[:].rearrange("p a b -> p (a b)"), A["gm_b"].partition_broadcast(P)), (poolw[:], A["pool_w"])]:
                    act.dma_start(dst, src).then_inc(s("mixer_loaded"), 16)
                for w, name in enumerate(("lru_wa", "lru_wx")):
                    for o in range(2):
                        act.dma_start(lruw[o * HD:(o + 1) * HD, w, :, o * HD:(o + 1) * HD], A[name][o]).then_inc(s("lru_loaded"), 16)
                next_squares("mix_in", "mlp1")
                root("mix_in", 5)
                high("mix_in", y, uhi)
                act.wait_ge(s("lam_abs"), 1)
                fn(lru[:, 1, :], lru[:, 0, :], ACT.Exp, scale=-1.0).then_inc(s("lam_exp"), 1)
                for g in range(16):
                    if g:
                        product(I_PROJ + g)
                    src = ps[:, g % 4, :]
                    a = slice(2 * (g % 2), 2 * (g % 2) + 2)
                    if g == 0:
                        act.wait_ge(s("blocks_ready"), 1)
                        act.sem_inc(s("proj_drained"), 1)
                    elif g == 1:
                        fn(ksw[:], halves(src), ACT.Copy).then_inc(s("proj_drained"), 1)
                    elif g in (2, 3):
                        fn(qn[:, a, :], halves(src), ACT.Copy).then_inc(s("proj_drained"), 1)
                    elif g == 4:
                        fn(vsw[:], halves(src), ACT.Copy).then_inc(s("proj_drained"), 1)
                    elif g == 5:
                        fn(gates[:], halves(src)[:, :, 0:24], ACT.Tanh, scale=0.5).then_inc(s("proj_drained"), 1)
                    elif g in (6, 7):
                        fn(rec[:, a, 3:3 + T], halves(src), ACT.Copy).then_inc(s("proj_drained"), 1)
                    elif g in (8, 9):
                        fn(gate[:, a, :], halves(src), ACT.Gelu_apprx_tanh).then_inc(s("proj_drained"), 1)
                    elif g in (10, 11):
                        fn(xd[:, a, 16:16 + T], halves(src), ACT.Copy).then_inc(s("proj_drained"), 1)
                    elif g in (12, 13):
                        fn(vg[:, :, (g - 12) * 256:(g - 12) * 256 + 256], halves(src), ACT.Gelu_apprx_tanh).then_inc(s("proj_drained"), 1)
                    else:
                        fn(ug[:, a, :], halves(src), ACT.Gelu_apprx_tanh).then_inc(s("proj_drained"), 1)
                    split(I_PROJ + g + RING)
                    if g == 3:
                        act.wait_ge(s("cmp_hidden"), 1)
                        fn(hidc[:, :, 0:NCMP], ps[:, 4, 0:32].rearrange("p (c n) -> p c n", c=2)[:, :, 0:NCMP], ACT.Gelu_apprx_tanh)\
                            .then_inc(s("cmp_gelu"), 1)
                    if g == 5:
                        act.wait_ge(s("cmp_out"), 1)
                        fn(kc[:, 0:NCMP], ps[:, 5, 0:NCMP], ACT.Copy)
                        fn(vc[0:NCMP, :].rearrange("p (g d) -> p g d", g=2), ps[0:NCMP, 6:8, 0:HD], ACT.Copy).then_inc(s("cmp_stored"), 1)
                act.wait_ge(s("proj_drained"), 16)
                for n in range(TT):
                    ins = fn(sq[:, 4 + 2 * n:6 + 2 * n, :].rearrange("p a c -> p (a c)"), vg[:, n, :], ACT.Square, accum_out=sm[:, n:n + 1])
                chain(ins)
                fn(sm[:, 2:4], sm[:, 0:2], ACT.Sqrt, bias=eps, scale=1.0 / MIX).then_inc(s("v_std"), 1)
                part("gm", slot_of[0], y[:, 0:MT, :])
                act.wait_ge(s("pool_mapped"), 1)
                for g in range(MT):
                    ins = fn(yhi[:, slot_of[3] + g, :], ps[:, 6 + g // 2, (g % 2) * T:(g % 2 + 1) * T], ACT.Copy, scale=pcol("pool_scale", g, 1))
                ins.then_inc(s("pool_hi"), 1)
                act.wait_ge(s("rec_gates"), 1)
                act.wait_ge(s("gm_lo"), 1)
                for w in range(2):
                    for m in range(MT):
                        ins = fn(y[:, 4 * w + m, :], ps[:, 2 * w + m // 2, (m % 2) * T:(m % 2 + 1) * T], ACT.Tanh, scale=0.5,
                                 bias=lru[:, 8 + w, m:m + 1])
                    ins.then_inc(s("rec_tanh"), 1)
                act.wait_ge(s("rec_rate"), 1)
                fn(rec[:, :, 0:T], y[:, 0:4, :], ACT.Tanh).then_inc(s("rate_tanh"), 1)
                act.wait_ge(s("rate_tanh"), 1)
                fn(y[:, 0:4, :], y[:, 0:4, :], ACT.Exp, scale=-1.0).then_inc(s("decay_ready"), 1)
                act.wait_ge(s("rec_power"), 1)
                fn(rec[:, :, 0:T], rec[:, :, 0:T], ACT.Sqrt).then_inc(s("rec_root"), 1)
                part("lru", slot_of[1], rec[:, :, 0:T])
                act.wait_ge(s("cmp_shifted"), 1)
                fn(cmp_p, cmp_p, ACT.Exp, scale=SCALE).then_inc(s("cmp_exp"), 1)
                act.wait_ge(s("cmp_turned"), 1)
                fn(cmp_t, ps[0:NCMP, 0:4, :].rearrange("p b (u q) -> p (b u) q", u=4), ACT.Copy).then_inc(s("cmp_t_ready"), 1)
                for u in range(20):
                    if u < 16:
                        j, g, qt = head(u)
                        act.wait_ge(s("nsa_max"), u + 1)
                        if u >= 2:
                            act.wait_ge(s("nsa_turned"), u - 1)
                        for b in range(2):
                            w = 4 * (u % 2) + b
                            ins = fn(nsa_e[:, u % 2, b, 0:(qt + 1) * P], ps[:, u % 2, b * T:b * T + (qt + 1) * P], ACT.Exp, scale=SCALE,
                                     bias=sm[:, 8 + w:9 + w], accum_out=sm[:, 16 + w:17 + w])
                        ins.then_inc(s("nsa_exps"), 1)
                    if 2 <= u <= 17:
                        v = u - 2
                        n = 2 * (v % 2 + 1)
                        act.wait_ge(s("nsa_turned"), v + 1)
                        if v >= 2:
                            act.wait_ge(s("nsa_out"), v - 1)
                        fn(nsa_t[:, 2 * (v % 2):2 * (v % 2) + n // 2, :].rearrange("p a c -> p (a c)"), ps[:, 2 + v % 2, 0:n * P], ACT.Copy)\
                            .then_inc(s("nsa_copied"), 1)
                    if u >= 7 and (u - 3) % 4 == 0 or u == 19:
                        j = (u - 3) // 4 - 1
                        act.wait_ge(s("nsa_out"), 4 * j + 4)
                        fn(yhi[:, slot_of[2] + j, :], ps[:, 4 + j % 2, 0:T], ACT.Copy).then_inc(s("nsa_out_hi"), 1)
                act.drain().then_inc(s("mg_free"), 4)
                with act.Fori(0, 4) as n:
                    for g in range(6):
                        i = I_BR + g
                        product(i, n, 6)
                        if g < 4:
                            act.wait_ge(s("gated_free"), up(1 + g // 2, n, 2))
                            fn(gated[:, 2 * g:2 * g + 2, :], halves(ps[:, g, :]), ACT.Tanh, scale=0.5).then_inc(s("mg_tanh"), 1)
                            act.drain().then_inc(s("mg_free"), 1)
                        split(i + RING, n, 6)
                high("merged", y, uhi)
                for g in range(4):
                    product(I_WO + g)
                    split(I_WO + g + RING)

            if on("all"):
                for dst, src in [(wr[:], A["router_w"]), (rb[:], A["router_b"].partition_broadcast(P)), (order4[:], A["order4"])]:
                    act.dma_start(dst, src).then_inc(s("router_loaded"), 16)
                next_squares("moe_in", "mixed")
                root("moe_in", 5)
                act.wait_ge(s("router_loaded"), 48)
                fn(wrhi[:], wr[:], ACT.Copy).then_inc(s("router_hi"), 1)
                high("moe_in", y, uhi)
                act.wait_ge(s("group_shifted"), 1)
                fn(ro[:, 2], ro[:, 1], ACT.Exp).then_inc(s("group_exp"), 1)
                act.wait_ge(s("top_gap"), 1)
                fn(ro[:, 12, :, 0:1], ro[:, 11, :, 0:1], ACT.Exp).then_inc(s("top_exp"), 1)

                def silu(i, j, n=None):
                    product(i, n, 6)
                    if n is not None:
                        act.wait_ge(s("moe_gated"), n * 2 + (j + 1))
                    fn(sg[:, 2 * j:2 * j + 2, :], halves(ps[:, j, :]), ACT.Silu).then_inc(s("moe_silu"), 1)
                    split(i + RING, n, 6)

                def expert_high(j, n=None):
                    act.wait_ge(s("moe_weighted"), j + 1 if n is None else n * 2 + (j + 3))
                    fn(ehi[:, 2 * j:2 * j + 2, :], hmid[:, 2 * j:2 * j + 2, :], ACT.Copy).then_inc(s("moe_hi"), 1)

                for j in range(2):
                    silu(I_MOE + j, j)
                for j in range(2):
                    split(I_MOE + 2 + j + RING)
                act.wait_ge(s("combine_turned"), 1)
                fn(cbt[0:EXPERTS, :], ps[0:EXPERTS, 5, 0:T], ACT.Copy).then_inc(s("combine_copied"), 1)
                for e in range(EXPERTS // 2):
                    act.wait_ge(s("comb_spread"), e + 1)
                    fn(comb[:, 2 * e:2 * e + 2, :], halves(ps[:, 4 + e % 4, :]), ACT.Copy).then_inc(s("comb_stored"), 1)
                for j in range(2):
                    expert_high(j)
                with act.Fori(0, EXPERTS - 1) as n:
                    i = I_MOE + 4
                    for j in range(2):
                        silu(i + j, j, n)
                    for j in range(2):
                        product(i + 2 + j, n, 6)
                        split(i + 2 + j + RING, n, 6)
                    for j in range(2):
                        product(i + 4 + j, n, 6)
                        split(i + 4 + j + RING, n, 6)
                    for j in range(2):
                        expert_high(j, n)
                for j in range(2):
                    product(N_CHUNKS - 2 + j)
                next_squares("final", "moe")
                root("final", 0)

        @block.vector
        def _(dve):
            tt, ts, stt = nc.vector.tensor_tensor, nc.vector.tensor_scalar, nc.vector.scalar_tensor_tensor
            chain = Chain(dve, "dve_chain")

            def split(i, n=None, step=0):
                if i >= n_chunks and n is None:
                    return
                sl = i % RING
                if i in MODS:
                    weigh(i, n, step)
                    return
                dve.wait_ge(s("hi_ready"), up(weights_up_to(i), n, weights_up_to(i + step) - weights_up_to(i)))
                tt(wlo[:, sl, :], raw[:, sl, :], f32(whi[:, sl, :]), ALU.subtract).then_inc(s("lo_ready"), 1)

            def weigh(i, n, step):
                sl = i % RING
                dve.wait_ge(s(f"raw_loaded{sl}"), up(16 * (i // RING + 1), n, 16 * step // RING))
                if i >= RING:
                    dve.wait_ge(s("chunk_used"), up(i - RING + 1, n, step))
                acc = macc[:, sl, :]
                for k in range(KT):
                    w, c = raw[:, sl, k * 256:(k + 1) * 256], csil[:, k, 0:1]
                    ins = ts(acc, w, c, None, ALU.mult) if k == 0 else stt(acc, w, c, acc, ALU.mult, ALU.add)
                    if k < KT - 1:
                        chain(ins)
                ins.then_inc(s("lo_ready"), 1)

            def modulation(i, q, n=None, step=0, turn=0):
                dve.wait_ge(s("chunk_used"), up(i + 1, n, step))
                t0 = START_TILES + 2 * q
                dst = slice(t0, t0 + 2) if n is None else bass.ds(n * (2 * turn) + t0, 2)
                b0 = PCOL["b_mod"][0]
                bias = par[:, b0 + t0:b0 + t0 + 2] if n is None else par[:, bass.ds(n * (2 * turn) + (b0 + t0), 2)]
                tt(modv[:, dst, 0:1].rearrange("p a b -> p (a b)"), ps[:, 7, 0:2], bias, ALU.add).then_inc(s("mod_drained"), 1)

            def modulated(i):
                dve.wait_ge(s("mod_drained"), mods_before(i) + 1)

            def scale_of(slot, gain, layer, part, who=0):
                chain(stt(coef[:, slot, :], mod_scale(layer, part, who), 1.0, gain, ALU.add, ALU.mult))

            def gate_of(slot, gain, layer, part):
                chain(tt(coef[:, slot, :], mod_scale(layer, part, 0), gain, ALU.mult))

            def low(tag, src, hi, lo):
                for c in range(2):
                    a = slice(4 * c, 4 * c + 4)
                    dve.wait_ge(*nth(tag, "hi", c + 1))
                    tt(lo[:, a, :], src[:, a, :], f32(hi[:, a, :]), ALU.subtract).then_inc(s("lo"), 1)

            def prenorm(tag, src, dst, slot, shift=None, gain=None):
                dve.wait_ge(*nth(tag, "std", 1))
                chain(nc.vector.reciprocal(rstd[:], std[:]))
                marks = [chain.tick(tt(dst[:, 4 * c:4 * c + 4, :], src[:, 4 * c:4 * c + 4, :], over_tiles(rstd[:], 4), ALU.mult))
                         for c in range(2)]
                for c in range(2):
                    dve.wait_ge(chain.sem, marks[c])
                    for k in range(4 * c, 4 * c + 4):
                        if shift is None:
                            ins = ts(dst[:, k, :], dst[:, k, :], pcol(gain, k, 1), None, ALU.mult)
                        else:
                            ins = ts(dst[:, k, :], dst[:, k, :], coef[:, slot, k:k + 1], shift[:, k:k + 1], ALU.mult, ALU.add)
                    ins.then_inc(s("normed"), 1)

            def postnorm(tag, slot):
                dve.wait_ge(*nth(tag, "std", 1))
                chain(nc.vector.reciprocal(rstd[:], std[:]))
                marks = []
                for c in range(2):
                    for k in range(4 * c, 4 * c + 4):
                        ins = stt(y[:, k, :], y[:, k, :], coef[:, slot, k:k + 1], rstd[:], ALU.mult, ALU.mult)
                    marks.append(chain.tick(ins))
                for c in range(2):
                    a = slice(4 * c, 4 * c + 4)
                    dve.wait_ge(chain.sem, marks[c])
                    tt(h[:, a, :], h[:, a, :], y[:, a, :], ALU.add).then_inc(s("h"), 1)

            dve.wait_ge(s("c_tanh"), 1)
            chain(stt(csil[:], csil[:], 1.0, cvec[:], ALU.add, ALU.mult))
            ts(csil[:], csil[:], 0.5, None, ALU.mult).then_inc(s("c_silu"), 1)
            lv = lamv.rearrange("p (a b d) -> p a b d", a=2, b=2)
            lp = rstd[:, 0:2 * HD].rearrange("p (a d) -> p a d", a=2)
            chain(tt(lp, lv[:, :, 0, :], lv[:, :, 1, :], ALU.mult))
            nc.vector.tensor_reduce(small[:, 22:24], lp, AX, ALU.add).then_inc(s("lam_sums"), 1)
            for j in range(4):
                dve.wait_ge(s(f"start_loaded{j}"), 16)
                marks = [None, None]
                for k in range(KT):
                    for w in range(2):
                        acc, m, c = start_acc[:, j, w], mstart[:, 2 * j + 1, k * 256:(k + 1) * 256], csil[:, k, w:w + 1]
                        if k:
                            dve.wait_ge(chain.sem, marks[w])
                        ins = stt(acc, m, c, acc, ALU.mult, ALU.add) if k else ts(acc, m, c, None, ALU.mult)
                        marks[w] = chain.tick(ins)
                dve.wait_ge(chain.sem, marks[1])
                dve.sem_inc(s("start_weighted"), 1)
            split(0)
            dve.wait_ge(s("mod_start"), 1)
            tt(modv[:, 0:START_TILES, :], ps[:, 7, 0:2 * START_TILES].rearrange("p (m w) -> p m w", m=START_TILES),
               over_cols(pcol("b_mod", 0, START_TILES), 2), ALU.add).then_inc(s("mod_drained"), 1)
            dve.wait_ge(s("mod_drained"), 1)
            scale_of(0, pcol("mix_pre", 0, 8), 0, 1, 0)
            scale_of(1, pcol("mix_pre", 0, 8), 0, 1, 1)
            dve.wait_ge(*nth("ctx", "sumsq", 1))
            prenorm("x", h, y, 0, mod_scale(0, 0, 0))
            low("x", y, uhi, ulo)
            prenorm("ctx", ctx, ctx, 1, mod_scale(0, 0, 1))
            low("ctx", ctx, ctx_hi, ctx_lo)
            for i in range(1, RING):
                split(i)
            cosb, sinb = over_tiles(ccol("cos"), 2), over_tiles(ccol("sin"), 2)

            def rope(r):
                dve.wait_ge(s("roped"), r + 1)
                tmp = sq[:, 2 * (r % 2):2 * (r % 2) + 2, :]
                x = kbuf[:, 2 * r:2 * r + 2, T:2 * T] if r < 4 else qbuf[:, 2 * (r - 4):2 * (r - 4) + 2, :]
                tt(tmp, ps[:, 4 + r % 2, :].rearrange("p (m t) -> p m t", m=2), sinb, ALU.mult).then_inc(s("rope_drained"), 1)
                chain(tt(x, x, cosb, ALU.mult))
                dve.wait_ge(s("rope_drained"), r + 1)
                tt(x, x, tmp, ALU.add).then_inc(s("roped_all"), 1)

            def filter_argument(j):
                c1 = 6.28125
                c2 = 2.0 * math.pi - c1
                magic = 1.5 * 2.0 ** 23
                top = math.pi * (1 - 2.0 ** -23)
                a, r = farg[0:HD, :], frnd[0:HD, :]
                dve.wait_ge(s("filter_layer"), j + 1)
                if j:
                    dve.wait_ge(s("filter_sin"), j)
                chain(ts(a, ps[0:HD, 6, 0:T], fpar[0:HD, j:j + 1], fpar[0:HD, 3:4], ALU.add, ALU.mult))
                chain(ts(r, a, 1.0 / (2.0 * math.pi), magic, ALU.mult, ALU.add))
                chain(ts(r, r, magic, None, ALU.subtract))
                chain(stt(a, r, -c1, a, ALU.mult, ALU.add))
                chain(stt(a, r, -c2, a, ALU.mult, ALU.add))
                ts(a, a, top, -top, ALU.min, ALU.max).then_inc(s("filter_arg"), 1)

            for i, g, q in items(I_QKV, I_ATT):
                split(i + RING)
                if g is None:
                    modulation(i, q)
                    continue
                if 1 <= g <= 8:
                    rope(g - 1)
                if g >= 10:
                    filter_argument(g - 10)
            filter_argument(2)

            def max_of(u):
                dve.wait_ge(s("scores"), u + 1)
                w = 4 * (u % 2)
                chain(nc.vector.tensor_reduce(small[:, w + 2:w + 4], ps[:, 2 * (u % 2):2 * (u % 2) + 2, :], AX, ALU.max))
                ts(small[:, w:w + 2], small[:, w + 2:w + 4], -SCALE, None, ALU.mult).then_inc(s("max_ready"), 1)

            def combine(u):
                dve.wait_ge(s("exps"), u + 1)
                w = 8 + 4 * (u % 2)
                r = small[:, w + 2:w + 4]
                e0, e1 = ebuf[:, u % 2, 0, :], ebuf[:, u % 2, 1, :]
                chain(nc.vector.reciprocal(r, small[:, w:w + 2]))
                a = chain.tick(ts(e0, e0, r[:, 0:1], None, ALU.mult))
                b = chain.tick(ts(e1, e1, r[:, 1:2], small[:, 26:27], ALU.mult, ALU.mult))
                dve.wait_ge(chain.sem, b)
                tt(e0, e0, e1, ALU.add).then_inc(s("att_ready"), 1)

            dve.wait_ge(s("lam_exps"), 1)
            chain(tt(small[:, 26:27], small[:, 25:26], small[:, 24:25], ALU.subtract))
            chain(ts(small[:, 26:27], small[:, 26:27], -LAM_INIT, None, ALU.add))
            chain(ts(small[:, 27:28], pcol("subln"), 1.0 - LAM_INIT, None, ALU.mult))
            for u in range(2 * HEADS + 1):
                if u < 2 * HEADS:
                    max_of(u)
                if u:
                    combine(u - 1)
                if u % 2 == 0 and u < 2 * HEADS:
                    split(I_ATT + u // 2 + RING)
                    modulation(I_ATT + u // 2, MODS.index(I_ATT + u // 2))
            modulated(I_AO)
            gate_of(2, pcol("mix_post", 0, 8), 0, 2)
            scale_of(3, pcol("mlp_pre", 0, 8), 0, 4)
            for c in range(4):
                a = slice(2 * c, 2 * c + 2)
                dve.wait_ge(s("o_std"), c + 1)
                chain(nc.vector.reciprocal(y[:, a, :], y[:, a, :]))
                stt(obuf[:, a, :], obuf[:, a, :], small[:, 27:28], y[:, a, :], ALU.mult, ALU.mult).then_inc(s("o_normed"), 1)
            for c in range(4):
                a = slice(2 * c, 2 * c + 2)
                dve.wait_ge(s("o_hi"), c + 1)
                tt(ulo[:, a, :], obuf[:, a, :], f32(uhi[:, a, :]), ALU.subtract).then_inc(s("o_lo"), 1)
            for g in range(4):
                split(I_AO + g + RING)
            postnorm("post0", 2)

            def low_squared(tag, g, c, n=None, step=0):
                dve.wait_ge(*mlp_nth(tag, "hid_hi", up(c + 1, n, step)))
                r, r2 = y[:, 2 * g:2 * g + 2, :], sq[:, 2 * g:2 * g + 2, :]
                chain(tt(r2, r, r, ALU.mult))
                dve.sem_inc(s("mlp_rfree"), 1)
                a = slice(2 * c, 2 * c + 2) if n is None else bass.ds(n * (2 * step) + 2 * c, 2)
                tt(hid_lo[:, a, :], r2, f32(hid_hi[:, a, :]), ALU.subtract).then_inc(s("mlp_hidden"), 1)

            def mlp(layer, tag, i0):
                prenorm(tag + "_in", h, y, 3, mod_scale(layer, 3, 0))
                low(tag + "_in", y, uhi, ulo)
                slots, turns, rest, body, _ = mlp_plan(layer)
                dve.drain().then_inc(s("mlp_rfree"), slots)
                with dve.Fori(0, turns) as n:
                    mods = len(body) - slots
                    chain.enter(n, slots + mods * (KT - 1))
                    for i, g, q in body:
                        if g is not None:
                            low_squared(tag, g, g, n, slots)
                        split(i + RING, n, len(body))
                        if g is None:
                            modulation(i, q, n, len(body), mods)
                chain.leave(turns)
                for r in range(rest):
                    low_squared(tag, r, slots * turns + r)
                    split(i0 + len(body) * turns + r + RING)
                for i, g, q in items(*out_span(layer)):
                    split(i + RING)
                    if g is None:
                        modulation(i, q)
                modulated(out_span(layer)[1])
                gate_of(4, pcol("mlp_post", 8 * layer, 8), layer, 5)
                postnorm(tag, 4)

            if on("mlp0"):
                mlp(0, "mlp0", I_MLP0)

            def short_conv(g):
                first = (16, 8, 0)[g // 4] + 2 * (g % 4)
                a = slice(2 * (g % 4), 2 * (g % 4) + 2)
                dst = (hv[:, a, :], hx1[:], hx0[:, a, :])[g // 4]
                dve.wait_ge(s("hy_drained"), g + 1)
                if 5 <= g <= 7:
                    dve.wait_ge(s("v_ready"), g - 4)
                for m in range(2):
                    ins = ts(dst[:, m, :], zpad[:, g % 2, m, 0:T], pcol("hy_w_short", first + m, 1), pcol("hy_b_short", first + m, 1),
                             ALU.mult, ALU.add)
                chain(ins)
                for tap in (1, 2):
                    for m in range(2):
                        ins = stt(dst[:, m, :], zpad[:, g % 2, m, tap:T + tap], pcol("hy_w_short", 24 * tap + first + m, 1), dst[:, m, :],
                                  ALU.mult, ALU.add)
                    if tap == 1:
                        chain(ins)
                ins.then_inc(s("hy_conved"), 1)
                if g // 4 == 1:
                    dve.wait_ge(s("hy_conved"), g + 1)
                    tt(hv[:, a, :], hv[:, a, :], hx1[:], ALU.mult).then_inc(s("v_ready"), 1)

            def taps_of(half, t0):
                a = slice(half * 512, half * 512 + 512)
                dve.wait_ge(s("filter_taps"), 2 * half + t0 + 1)
                if half == 0 and t0 == 0:
                    dve.wait_ge(s("decay_loaded"), 16)
                if half and t0 == 0:
                    dve.wait_ge(s("filter_spec"), 2)
                b = TAPS_BANK[half, t0]
                tt(tapf[:, t0, :], ps[:, b, :], decay[:, t0, a], ALU.mult)
                if t0 == 0:
                    chain(stt(tapb[:, t0, :], ps[:, b + 1, :], ccol("notfirst"), decay[:, t0, a], ALU.mult, ALU.mult))
                else:
                    chain(tt(tapb[:, t0, :], ps[:, b + 1, :], decay[:, t0, a], ALU.mult))
                chain(tt(taps[:, t0, :], tapf[:, t0, :], tapb[:, t0, :], ALU.add))
                tt(tapf[:, t0, :], tapf[:, t0, :], tapb[:, t0, :], ALU.subtract).then_inc(s("taps_ready"), 1)

            if on("hyena"):
                scale_of(5, pcol("mix_pre", 8, 8), 1, 1)
                prenorm("hy_in", h, y, 5, mod_scale(1, 0, 0))
                low("hy_in", y, uhi, ulo)
                nc.vector.memset(zpad[:], 0.0).then_inc(s("zpad_clear"), 1)
                for g in range(12):
                    split(I_HY + g + RING)
                    short_conv(g)
                    if g in (2, 3):
                        taps_of(0, g - 2)
                    if g in (6, 7):
                        taps_of(1, g - 6)
                gate_of(6, pcol("mix_post", 8, 8), 1, 2)
                scale_of(3, pcol("mlp_pre", 8, 8), 1, 4)
                dve.wait_ge(s("spec_stored"), 4)
                for half in range(2):
                    a = slice(half * 512, half * 512 + 512)
                    dve.wait_ge(s("vspec"), half + 1)
                    c, d = CONV_BANKS[half][0], CONV_BANKS[half][2]
                    vc, vs, hc, hs = ps[:, c:c + 2, :], ps[:, d:d + 2, :], spec[:, 0:2, a], spec[:, 2:4, a]
                    tt(prod[:, 0], vc, hc, ALU.mult)
                    chain(tt(prod[:, 1], vs, hs, ALU.mult))
                    chain(tt(yspec[:, half, 0:2, :], prod[:, 0], prod[:, 1], ALU.subtract))
                    tt(prod[:, 0], vc, hs, ALU.mult)
                    chain(tt(prod[:, 1], vs, hc, ALU.mult))
                    chain(tt(yspec[:, half, 2:4, :], prod[:, 0], prod[:, 1], ALU.add))
                    dve.sem_inc(s("yspec_ready"), 1)
                for half in range(2):
                    for m in range(4):
                        k = 4 * half + m
                        dve.wait_ge(s("conv"), k + 1)
                        ins = stt(hv[:, k, :], hv[:, k, :], pcol("hy_bias", k, 1), ps[:, CONV_BANKS[half][m], 0:T], ALU.mult, ALU.add)
                        ins.then_inc(s("conv_taken"), 1)
                    dve.wait_ge(s("conv_taken"), 4 * half + 4)
                    a = slice(4 * half, 4 * half + 4)
                    tt(hv[:, a, :], hv[:, a, :], hx0[:, a, :], ALU.mult).then_inc(s("normed"), 1)
                low("hy", hv, uhi, ulo)
                for g in range(4):
                    split(I_HO + g + RING)
                postnorm("post1", 6)
            if on("mlp1"):
                mlp(1, "mlp1", I_MLP1)

            def halves(m):
                return m.rearrange("p (m t) -> p m t", m=2)

            def head(u):
                return u // 4, (u // 2) % 2, u % 2

            def low_part(name, b, src):
                dve.wait_ge(s(name + "_hi"), 1)
                tt(ylo[:, b:b + MT, :], src, f32(yhi[:, b:b + MT, :]), ALU.subtract).then_inc(s(name + "_lo"), 1)

            def softplus_of_minus_lambda():
                lam, e, z, z2, acc = pcol("lam"), lru[:, 1, :], lru[:, 2, :], lru[:, 4, :], lru[:, 3, :]
                chain(ts(lru[:, 5, :], lam, -1.0, None, ALU.mult))
                tt(lru[:, 0, :], lam, lru[:, 5, :], ALU.max).then_inc(s("lam_abs"), 1)
                dve.wait_ge(s("lam_exp"), 1)
                chain(ts(z, e, 2.0, None, ALU.add))
                chain(nc.vector.reciprocal(z, z))
                chain(tt(z, z, e, ALU.mult))
                chain(tt(z2, z, z, ALU.mult))
                terms = 9
                chain(ts(acc, z2, 1.0 / (2 * terms + 1), 1.0 / (2 * terms - 1), ALU.mult, ALU.add))
                for k in range(terms - 2, -1, -1):
                    chain(tt(acc, acc, z2, ALU.mult))
                    chain(ts(acc, acc, 1.0 / (2 * k + 1), None, ALU.add))
                chain(stt(acc, acc, 2.0, z, ALU.mult, ALU.mult))
                chain(stt(acc, lru[:, 5, :], 0.0, acc, ALU.max, ALU.add))
                chain(ts(acc, acc, 4.0, None, ALU.mult))
                for w, name in enumerate(("ba", "bx")):
                    chain(ts(lru[:, 8 + w, :], pcol(name), 0.5, None, ALU.mult))

            def blocks_of(c):
                src = ps[:, 0, c * T:(c + 1) * T]
                for half in range(2):
                    a = slice(16 * half, 16 * half + 16)
                    ins = tt(blocks[:, c, a, :].rearrange("p l n -> p n l"),
                             src[:, 16 * half:16 * half + 240].rearrange("p (n l) -> p n l", l=16),
                             over_tiles(cpe[:, c, a], NCMP), ALU.add)
                return ins

            def trailing_sums():
                sa, sb, x = y[:, 0:4, :], y[:, 4:8, :], xd[:, :, 16:16 + T]
                chain(tt(sa, x, xd[:, :, 15:15 + T], ALU.add))
                for g0, w, old, new in ((1, 2, sa, sb), (2, 4, sb, sa), (3, 8, sa, sb)):
                    tt(new[:, g0:4, w:], old[:, g0:4, w:], old[:, g0:4, :-w], ALU.add)
                    chain(nc.vector.tensor_copy(new[:, g0:4, 0:w], old[:, g0:4, 0:w]))
                for g, b in enumerate((sa, sb, sa, sb)):
                    ins = tt(b[:, g, :], b[:, g, :], bcol("recip")[:, g * T:(g + 1) * T], ALU.mult)
                chain(ins)
                for g, b in enumerate((sa, sb, sa, sb)):
                    ins = tt(x[:, g, :], b[:, g, :], x[:, g, :], ALU.subtract)
                ins.then_inc(s("pooled"), 1)
                dve.wait_ge(s("pooled"), 1)

            if on("mixer"):
                for b in (lruw[:], rec[:, :, 0:3], xd[:, :, 0:16]):
                    ins = nc.vector.memset(b, 0.0)
                ins.then_inc(s("lru_clear"), 1)
                prenorm("mix_in", h, y, 0, gain="norm1")
                low("mix_in", y, uhi, ulo)
                softplus_of_minus_lambda()
                dve.wait_ge(s("mixer_loaded"), 16 * 5)
                dve.wait_ge(s("chunk_used"), I_PROJ + 1)
                blocks_of(0)
                blocks_of(1).then_inc(s("blocks_ready"), 1)
                chain(tt(gmw[:], gmw[:], over_tiles(tril, MT), ALU.mult))
                for g in range(16):
                    split(I_PROJ + g + RING)
                    if g == 6:
                        dve.wait_ge(s("proj_drained"), 6)
                        chain(ts(gates[:], gates[:], 0.5, 0.5, ALU.mult, ALU.add))
                    if g == 8:
                        dve.wait_ge(s("proj_drained"), 8)
                        dve.wait_ge(s("cmp_hidden"), 1)
                        for m in range(MT):
                            ins = ts(sq[:, m, :], rec[:, m, 0:T], pcol("conv_w", m, 1), pcol("conv_b", m, 1), ALU.mult, ALU.add)
                        chain(ins)
                    if 9 <= g <= 11:
                        for m in range(MT):
                            ins = stt(sq[:, m, :], rec[:, m, g - 8:g - 8 + T], pcol("conv_w", 4 * (g - 8) + m, 1), sq[:, m, :], ALU.mult, ALU.add)
                        if g < 11:
                            chain(ins)
                        else:
                            ins.then_inc(s("rec_conved"), 1)
                    if g == 12:
                        dve.wait_ge(s("proj_drained"), 12)
                        trailing_sums()
                dve.wait_ge(s("v_std"), 1)
                chain(nc.vector.reciprocal(sm[:, 4:6], sm[:, 2:4]))
                for n in range(TT):
                    ins = ts(vg[:, n, :], vg[:, n, :], sm[:, 4 + n:5 + n], None, ALU.mult)
                ins.then_inc(s("v_normed"), 1)
                dve.wait_ge(s("gm_mixed"), 1)
                for g in range(MT):
                    ins = stt(y[:, g, :].rearrange("p (n t) -> p n t", n=TT), halves(ps[:, 4 + g // 2, (g % 2) * T:(g % 2 + 1) * T]),
                              pcol("gm_norm", g, 1), over_tiles(gmb[:, g, :], TT), ALU.mult, ALU.add)
                chain(ins)
                tt(y[:, 0:MT, :], y[:, 0:MT, :], ug, ALU.mult).then_inc(s("gm_ready"), 1)
                dve.wait_ge(s("cmp_hidden"), 1)
                low_part("gm", slot_of[0], y[:, 0:MT, :])
                dve.wait_ge(s("pool_hi"), 1)
                for g in range(MT):
                    b = slot_of[3] + g
                    ins = stt(ylo[:, b, :], ps[:, 6 + g // 2, (g % 2) * T:(g % 2 + 1) * T], pcol("pool_scale", g, 1), f32(yhi[:, b, :]),
                              ALU.mult, ALU.subtract)
                ins.then_inc(s("pool_lo"), 1)
                rate, inp, pw = y[:, 0:4, :], y[:, 4:8, :], rec[:, :, 0:T]
                dve.wait_ge(s("rec_tanh"), 1)
                for m in range(MT):
                    ins = ts(rate[:, m, :], rate[:, m, :], 1.0, lru[:, 3, m:m + 1], ALU.add, ALU.mult)
                ins.then_inc(s("rec_rate"), 1)
                dve.wait_ge(s("rec_tanh"), 2)
                chain(stt(inp, inp, 1.0, sq[:, 0:4, :], ALU.add, ALU.mult))
                dve.wait_ge(s("decay_ready"), 1)
                chain(tt(sq[:, 4:8, :], rate, rate, ALU.mult))
                stt(pw, sq[:, 4:8, :], 1.0, pw, ALU.add, ALU.mult).then_inc(s("rec_power"), 1)
                dve.wait_ge(s("rec_root"), 1)
                chain(stt(inp, inp, 0.5, pw, ALU.mult, ALU.mult))
                for m in range(MT):
                    ins = nc.vector.tensor_tensor_scan(sq[:, m, :], rate[:, m, :], inp[:, m, :], 0.0, ALU.mult, ALU.add)
                chain(ins)
                tt(pw, sq[:, 0:4, :], gate[:], ALU.mult).then_inc(s("lru_ready"), 1)
                low_part("lru", slot_of[1], pw)
                dve.wait_ge(s("lru_lo"), 1)
                dve.sem_inc(s("lru_done"), 1)
                dve.wait_ge(s("cmp_scores"), 1)
                for qt in range(2):
                    for g in range(2):
                        ins = tt(cmp_p[:, qt, 4 * g:4 * g + 4], ps[:, 4 + 2 * qt + g, 0:64].rearrange("p (h n) -> p h n", n=16)[:, :, 0:NCMP],
                                 over_tiles(bcol("cmask")[:, qt * NCMP:(qt + 1) * NCMP], 4), ALU.add)
                chain(ins)
                flat = cmp_p.rearrange("p t h n -> p (t h) n")
                top, inv = sm[:, 24:40], sm[:, 40:56]
                chain(nc.vector.tensor_reduce(top, flat, AX, ALU.max))
                tt(flat, flat, over_cols(top, NCMP), ALU.subtract).then_inc(s("cmp_shifted"), 1)
                dve.wait_ge(s("cmp_exp"), 1)
                chain(nc.vector.tensor_reduce(top, flat, AX, ALU.add))
                chain(nc.vector.reciprocal(inv, top))
                for qt in range(2):
                    ins = stt(inv[:, 8 * qt:8 * qt + 8], inv[:, 8 * qt:8 * qt + 8], bcol("cvalid")[:, qt:qt + 1],
                              gates[:, qt, :].rearrange("p (h b) -> p b h", b=3)[:, 0, :], ALU.mult, ALU.mult)
                chain(ins)
                tt(flat, flat, over_cols(inv, NCMP), ALU.mult).then_inc(s("cmp_weights"), 1)

                def nsa_max(u):
                    j, g, qt = head(u)
                    dve.wait_ge(s("nsa_scores"), u + 1)
                    w = 8 + 4 * (u % 2)
                    sc = ps[:, u % 2, :].rearrange("p (b k) -> p b k", b=2)
                    diag = sc[:, :, qt * P:(qt + 1) * P]
                    chain(tt(diag, diag, over_tiles(causal, 2), ALU.add))
                    chain(nc.vector.tensor_reduce(sm[:, w + 2:w + 4], sc[:, :, 0:(qt + 1) * P], AX, ALU.max))
                    ts(sm[:, w:w + 2], sm[:, w + 2:w + 4], -SCALE, None, ALU.mult).then_inc(s("nsa_max"), 1)

                def nsa_weights(u):
                    j, g, qt = head(u)
                    dve.wait_ge(s("nsa_exps"), u + 1)
                    w = 16 + 4 * (u % 2)
                    r = sm[:, w + 2:w + 4]
                    hh = g * 4 + j
                    chain(nc.vector.reciprocal(r, sm[:, w:w + 2]))
                    chain(tt(r, r, gates[:, qt, 3 * hh + 1:3 * hh + 3], ALU.mult))
                    for b in range(2):
                        e = nsa_e[:, u % 2, b, 0:(qt + 1) * P]
                        ins = ts(e, e, r[:, b:b + 1], None, ALU.mult)
                    ins.then_inc(s("nsa_weights"), 1)

                dve.wait_ge(s("cmp_turned"), 1)
                for u in range(20):
                    if u < 16:
                        nsa_max(u)
                    if 1 <= u <= 16:
                        nsa_weights(u - 1)
                    if u >= 7 and (u - 3) % 4 == 0 or u == 19:
                        j = (u - 3) // 4 - 1
                        b = slot_of[2] + j
                        dve.wait_ge(s("nsa_out_hi"), j + 1)
                        tt(ylo[:, b, :], ps[:, 4 + j % 2, 0:T], f32(yhi[:, b, :]), ALU.subtract).then_inc(s("nsa_out_lo"), 1)
                dve.wait_ge(s("nsa_out"), 16)
                chain(nc.vector.memset(y[:], 0.0))
                dve.drain().then_inc(s("br_free"), 2)
                dve.drain().then_inc(s("gated_free"), 2)
                with dve.Fori(0, 4) as n:
                    chain.enter(n, 4)
                    for g in range(6):
                        i = I_BR + g
                        if g >= 4:
                            a = slice(4 * (g - 4), 4 * (g - 4) + 4)
                            dve.wait_ge(s("mg_tanh"), up(4, n, 4))
                            dve.wait_ge(s("chunk_used"), up(i + 1, n, 6))
                            src = ps[:, 2 * g - 4:2 * g - 2, :].rearrange("p b (m t) -> p (b m) t", m=2)
                            chain(stt(sq[:, a, :], gated[:, a, :], 1.0, src, ALU.add, ALU.mult))
                            dve.sem_inc(s("br_free"), 1)
                            dve.sem_inc(s("gated_free"), 1)
                            chain(tt(y[:, a, :], y[:, a, :], sq[:, a, :], ALU.add))
                        split(i + RING, n, 6)
                chain.leave(4)
                for c in range(2):
                    a = slice(4 * c, 4 * c + 4)
                    ts(y[:, a, :], y[:, a, :], 0.5, None, ALU.mult).then_inc(s("normed"), 1)
                low("merged", y, uhi, ulo)
                for g in range(4):
                    dve.wait_ge(s("chunk_used"), I_WO + g + 1)
                    a = slice(2 * g, 2 * g + 2)
                    ins = tt(h[:, a, :], h[:, a, :], halves(ps[:, g, :]), ALU.add)
                    if g % 2:
                        ins.then_inc(s("h"), 1)
                    split(I_WO + g + RING)

            if on("all"):
                prenorm("moe_in", h, y, 0, gain="norm2")
                dve.wait_ge(s("router_hi"), 1)
                tt(wrlo[:], wr[:], f32(wrhi[:]), ALU.subtract).then_inc(s("router_lo"), 1)
                low("moe_in", y, uhi, ulo)

                def row(k, n=4):
                    return ro[:, k, :, 0:n]

                def wide(x, n=4):
                    return x.to_broadcast([P, TT, n])

                def first_of(dst, src, top, tmp, tmp_top):
                    chain(tt(row(tmp), src, wide(top), ALU.is_equal))
                    chain(tt(row(tmp), row(tmp), order4[:].unsqueeze(1).to_broadcast([P, TT, 4]), ALU.mult))
                    chain(nc.vector.tensor_reduce(row(tmp_top, 1), row(tmp), AX, ALU.max))
                    chain(tt(dst, row(tmp), wide(row(tmp_top, 1)), ALU.is_equal))

                dve.wait_ge(s("router"), 1)
                chain(tt(lg[:], ps[:, 4, 0:64].rearrange("p (t c) -> p t c", t=2)[:, :, 0:20], rb[:].unsqueeze(1).to_broadcast([P, TT, 20]), ALU.add))
                grp = lg[:, :, 0:4]
                chain(nc.vector.tensor_reduce(row(0, 1), grp, AX, ALU.max))
                tt(row(1), grp, wide(row(0, 1)), ALU.subtract).then_inc(s("group_shifted"), 1)
                first_of(row(3), grp, row(0, 1), 4, 5)
                dve.wait_ge(s("group_exp"), 1)
                chain(nc.vector.tensor_reduce(row(6, 1), row(2), AX, ALU.add))
                chain(nc.vector.reciprocal(row(6, 1), row(6, 1)))
                for t0 in range(TT):
                    prod4 = ro[:, 14 + 2 * t0:16 + 2 * t0].rearrange("p a b c -> p (a b c)").rearrange("p (g e) -> p g e", g=4)
                    chain(tt(prod4, lg[:, t0, 4:20].rearrange("p (g e) -> p g e", g=4), over_cols(ro[:, 3, t0, :], 4), ALU.mult))
                    chain(nc.vector.tensor_reduce(ro[:, 7, t0, :], prod4.rearrange("p g e -> p e g"), AX, ALU.add))
                chain(nc.vector.tensor_reduce(row(8, 1), row(7), AX, ALU.max))
                first_of(row(9), row(7), row(8, 1), 4, 5)
                chain(stt(row(7), row(9), MASKED, row(7), ALU.mult, ALU.add))
                chain(nc.vector.tensor_reduce(row(10, 1), row(7), AX, ALU.max))
                tt(row(11, 1), row(10, 1), row(8, 1), ALU.subtract).then_inc(s("top_gap"), 1)
                first_of(row(13), row(7), row(10, 1), 4, 5)
                dve.wait_ge(s("top_exp"), 1)
                chain(ts(row(18, 1), row(12, 1), 1.0, None, ALU.add))
                chain(nc.vector.reciprocal(row(18, 1), row(18, 1)))
                chain(tt(row(18, 1), row(18, 1), row(6, 1), ALU.mult))
                chain(tt(row(19, 1), row(18, 1), row(12, 1), ALU.mult))
                chain(tt(row(9), row(9), wide(row(18, 1)), ALU.mult))
                chain(tt(row(13), row(13), wide(row(19, 1)), ALU.mult))
                chain(tt(row(9), row(9), row(13), ALU.add))
                for t0 in range(TT):
                    ins = tt(cb[:, t0, :].rearrange("p (g e) -> p g e", g=4), over_tiles(ro[:, 9, t0, :], 4), over_cols(ro[:, 3, t0, :], 4), ALU.mult)
                ins.then_inc(s("combine_ready"), 1)

                def weighted(i, j, n=None):
                    dve.wait_ge(s("chunk_used"), up(i + 1, n, 6))
                    dve.wait_ge(s("moe_silu"), j + 1 if n is None else n * 2 + (j + 3))
                    a = slice(2 * j, 2 * j + 2)
                    tt(hmid[:, a, :], sg[:, a, :], halves(ps[:, 2 + j, :]), ALU.mult).then_inc(s("moe_gated"), 1)
                    dve.wait_ge(s("moe_gated"), j + 1 if n is None else n * 2 + (j + 3))
                    c = comb[:, 0, :] if n is None else comb[:, bass.ds(n + 1, 1), :].rearrange("p a t -> p (a t)")
                    tt(hmid[:, a, :], hmid[:, a, :], over_tiles(c, 2), ALU.mult).then_inc(s("moe_weighted"), 1)

                def expert_low(j, n=None):
                    dve.wait_ge(s("moe_hi"), j + 1 if n is None else n * 2 + (j + 3))
                    a = slice(2 * j, 2 * j + 2)
                    tt(elo[:, a, :], hmid[:, a, :], f32(ehi[:, a, :]), ALU.subtract).then_inc(s("moe_hid"), 1)

                def add_rows(i, j, n=None, last=False):
                    dve.wait_ge(s("chunk_used"), up(i + 1, n, 6))
                    a = slice(4 * j, 4 * j + 4)
                    tt(h[:, a, :], h[:, a, :], ps[:, 4 + 2 * j:6 + 2 * j, :].rearrange("p b (m t) -> p (b m) t", m=2), ALU.add)\
                        .then_inc(s("h" if last else "moe_free"), 1)

                for j in range(4):
                    split(I_MOE + j + RING)
                dve.wait_ge(s("comb_stored"), EXPERTS // 2)
                for j in range(2):
                    weighted(I_MOE + 2 + j, j)
                for j in range(2):
                    expert_low(j)
                dve.drain().then_inc(s("moe_free"), 2)
                with dve.Fori(0, EXPERTS - 1) as n:
                    i = I_MOE + 4
                    for j in range(2):
                        split(i + j + RING, n, 6)
                    for j in range(2):
                        add_rows(i + 2 + j, j, n)
                        split(i + 2 + j + RING, n, 6)
                    for j in range(2):
                        weighted(i + 4 + j, j, n)
                        split(i + 4 + j + RING, n, 6)
                    for j in range(2):
                        expert_low(j, n)
                dve.wait_ge(s("moe_free"), 2 * EXPERTS)
                for j in range(2):
                    add_rows(N_CHUNKS - 2 + j, j, last=True)
                prenorm("final", h, y, 0, gain="final")
                dve.wait_ge(*nth("final", "normed", 2))
                dve.sem_inc(s("result_ready"), 1)

            if upto != "all":
                for c in range(2):
                    dve.wait_ge(*nth({"attn": "post0", "mlp0": "mlp0", "hyena": "post1", "mlp1": "mlp1", "mixer": "mixed"}[upto], "h", c + 1))
                nc.vector.tensor_copy(y[:], h[:]).then_inc(s("result_ready"), 1)


SPARAMS = ["b_mod", "norm_mix_pre", "norm_mix_post", "norm_mlp_pre", "norm_mlp_post", "attn_subln", "hy_b_in",
           "hy_w_short", "hy_b_short", "hy_bias", "hy_b_out", "norm1_g_2", "gm_norm_g_2", "conv_w_2", "conv_b_2",
           "lru_ba_2", "lru_bx_2", "lru_lambda_2", "pool_scale_2", "norm2_g_2", "final_norm_g_2"]


def laid_out(x):
    ac = np.ascontiguousarray
    a = {k: np.asarray(v) for k, v in x.items()}
    weights = np.zeros((N_CHUNKS + 1, P, CW), np.float32)
    for i, (name, lead, r0, rows, cols) in enumerate(STREAM):
        m = a[name][lead]
        lo, n = cols[0], len(cols)
        m = m[r0:r0 + rows, lo:lo + n] if cols == tuple(range(lo, lo + n)) else m[r0:r0 + rows][:, list(cols)]
        if name == "w_branch_2" and lead[1] == 2:
            order = [g * 256 + j * 64 + d for j in range(4) for g in range(2) for d in range(64)]
            m = m[order]
        k = rows // P
        width = CW // k
        weights[i].reshape(P, k, width)[:, :, :n] = m.reshape(k, P, n).transpose(1, 0, 2)

    def fm(v):
        return ac(v.reshape(T, KT, P).transpose(2, 1, 0))

    params = ac(np.concatenate([a[n].reshape(-1, P) for n in SPARAMS]).T)
    assert params.shape == (P, NPAR)
    out = {
        "weights": weights, 
        "mod_start": ac(a["w_mod"][0][:, 0:START_TILES * P].reshape(KT, P, START_TILES // 2, 2 * P).transpose(1, 2, 0, 3).reshape(P, START_TILES // 2, CW)),
         "params": params, "x": fm(a["x"]), "ctx": fm(a["ctx"]),
        "cvec": ac(np.stack([a["c"].reshape(KT, P).T, a["c_ctx"].reshape(KT, P).T], axis=2)),
        "attn_lambda": ac(a["attn_lambda"].reshape(-1)),
        "hy_filt_w1": ac(a["hy_filt_w1"][0]), "hy_filt_w2": ac(a["hy_filt_w2"][0].transpose(1, 0, 2)),
        "hy_filt_w_out": ac(a["hy_filt_w_out"][0]),
        "fpar": ac(np.stack([a["hy_filt_b1"][0], a["hy_filt_b2"][0, 0], a["hy_filt_b2"][0, 1], a["hy_filt_freq"][0]], axis=1)),
        "cmp_w1": ac(a["cmp_w1_2"][0].reshape(2, 2, CMP_LEN, HD, HD).transpose(1, 3, 0, 2, 4).reshape(P, 2, CMP_LEN * HD)),
        "cmp_w2": ac(a["cmp_w2_2"][0].transpose(1, 2, 0, 3).reshape(P, 2, HD)),
        "cmp_pe": ac(np.concatenate([a["cmp_pe_2"][0].transpose(2, 0, 1)] * 2)),
        "gm_ws": ac(a["gm_ws_2"][0].transpose(2, 0, 1)), "gm_b": ac(a["gm_b_2"][0].reshape(-1)),
        "pool_w": ac(a["pool_w_2"][0].transpose(1, 0, 2)),
        "lru_wa": ac(a["lru_wa_2"][0].reshape(4, 2, HD, HD).transpose(1, 2, 0, 3)),
        "lru_wx": ac(a["lru_wx_2"][0].reshape(4, 2, HD, HD).transpose(1, 2, 0, 3)),
        "router_w": ac(np.concatenate([a["router_w_group_2"][0], a["router_w_expert_2"][0]], axis=1)
                       .reshape(KT, P, 20).transpose(1, 0, 2)),
        "router_b": ac(np.concatenate([a["router_b_group_2"][0], a["router_b_expert_2"][0]])),
        "order4": np.broadcast_to(np.arange(4, 0, -1, dtype=np.float32), (P, 4)).copy(),
        **shape_constants(),
    }
    return out


UPTO = "all"


def kernel(**inputs):
    import concourse.bacc as bacc
    from concourse.bass_utils import run_bass_kernel_spmd

    nc = bacc.Bacc("TRN2", target_bir_lowering=False, num_devices=1)
    arrays = laid_out(inputs)
    aps = {n: nc.dram_tensor(n + "_in", v.shape, mybir.dt.from_np(v.dtype), kind="ExternalInput").ap()
           for n, v in arrays.items()}
    out = nc.dram_tensor("out_0", (P, KT, T), F32, kind="ExternalOutput").ap()
    program(nc, aps, out, UPTO)
    r = run_bass_kernel_spmd(nc, [{n + "_in": v for n, v in arrays.items()}], core_ids=[0])
    got = r.results[0]["out_0"]
    return np.ascontiguousarray(got.transpose(2, 1, 0)).reshape(1, T, D)
```

```python
from contextlib import ExitStack
import math

import numpy as np

import concourse.bass as bass
from concourse import mybir

F32 = mybir.dt.float32
F32R = mybir.dt.float32r
ACT = mybir.ActivationFunctionType
ALU = mybir.AluOpType
AX = mybir.AxisListType.X

P = 128
D = 1024
KT = D // P
T = 256
TT = T // P
DFF = 4096
HEADS = 8
RING = 3
CW = 2048
EXPERTS = 16
DE = 512
MIX = 512
MT = MIX // P
NCMP = 15
CMP_STRIDE, CMP_LEN = 16, 32
HD = 64
LAM_INIT = 0.8 - 0.6 * math.exp(0.0)
SCALE = HD ** -0.5
EPS = 1e-6
MASKED = -1e30
BRANCH_ORDER = (0, 3, 1, 2)
POOL_WINDOWS = (2, 4, 8, 16)

U0, V0, GATE0, REC0, Q0, KV0, NSAG0, XD0, MG0 = 0, 512, 1024, 1536, 2048, 2560, 3328, 3352, 3864


ATT_MODS = 8
START_TILES = 16

def weight_stream():
    def cols(a, n):
        return tuple(range(a, a + n))

    def mat(name, lead, c0):
        return (name, lead, 0, D, cols(c0, 256))

    def down(name, lead, c0):
        return (name, lead, 0, MIX, cols(c0, 512))

    def mlp(layer):
        return [mat("w_mlp_in", (layer,), 256 * j) for j in range(16)] + \
            [("w_mlp_out", (layer,), D * g, D, cols(256 * m, 256)) for m in range(4) for g in range(4)]

    out = [mat("attn_w_qkv", (0,), c0 + 256 * j) for c0 in (D, 0, 2 * D) for j in range(4)]
    out += [mat("attn_w_out", (0,), 256 * j) for j in range(4)]
    out += mlp(0)
    out += [mat("hy_w_in", (0,), c0 + 256 * j) for c0 in (2 * D, D, 0) for j in range(4)]
    out += [mat("hy_w_out", (0,), 256 * j) for j in range(4)]
    out += mlp(1)
    kv = lambda n: cols(KV0 + 128 * n, 128)
    qcol = lambda j: cols(Q0 + 64 * j, 64) + cols(Q0 + 256 + 64 * j, 64)
    for c in [kv(0) + kv(1), kv(2) + kv(4), qcol(0) + qcol(1), qcol(2) + qcol(3), kv(3) + kv(5), cols(NSAG0, 24)]:
        out.append(("w_in_2", (0,), 0, D, c))
    for c0 in (REC0, REC0 + 256, GATE0, GATE0 + 256, XD0, XD0 + 256, V0, V0 + 256, U0, U0 + 256):
        out.append(mat("w_in_2", (0,), c0))
    for n in BRANCH_ORDER:
        out += [mat("w_in_2", (0,), MG0 + D * n + 256 * j) for j in range(4)]
        out += [down("w_branch_2", (0, n), 512 * j) for j in range(2)]
    out += [mat("w_out_2", (0,), 256 * j) for j in range(4)]
    gate = lambda e: [mat("moe_w_gate_2", (0, e), 256 * j) for j in range(2)]
    upx = lambda e: [mat("moe_w_up_2", (0, e), 256 * j) for j in range(2)]
    dnx = lambda e: [down("moe_w_down_2", (0, e), 512 * j) for j in range(2)]
    out += gate(0) + upx(0)
    for e in range(1, EXPERTS):
        out += gate(e) + dnx(e - 1) + upx(e)
    out += dnx(EXPERTS - 1)

    after = {w: 1 for w in range(12)}
    after[11] += ATT_MODS
    after.update({16 + w: 1 for w in range(1, 16, 2)})
    after.update({32 + w: 1 for w in range(1, 16, 2)})
    after.update({80 + w: 1 for w in range(2, 16, 4)})
    stream, at, mods = [], [], []
    for w, entry in enumerate(out):
        at.append(len(stream))
        stream.append(entry)
        for _ in range(after.get(w, 0)):
            layer, tile = divmod(2 * len(mods) + START_TILES, 48)
            mods.append(len(stream))
            stream.append(mat("w_mod", (layer,), P * tile))
    assert 2 * len(mods) + START_TILES == 96
    return stream, at, mods


STREAM, AT, MODS = weight_stream()
N_CHUNKS = len(STREAM)
I_QKV, I_AO, I_MLP0, I_HY, I_HO, I_MLP1, I_PROJ, I_BR, I_WO, I_MOE = (AT[w] for w in (0, 12, 16, 48, 60, 64, 96, 112, 136, 140))
I_OUT0, I_OUT1 = AT[32], AT[80]
I_ATT = I_AO - ATT_MODS


def items(first, last):
    g = 0
    for i in range(first, last):
        if i in MODS:
            yield i, None, MODS.index(i)
        else:
            yield i, g, None
            g += 1


def weights_up_to(i):
    return i + 1 - sum(m <= i for m in MODS)


def param_columns():
    names = [("b_mod", 96), ("mix_pre", 16), ("mix_post", 16), ("mlp_pre", 16), ("mlp_post", 16),
             ("subln", 1), ("hy_b_in", 24), ("hy_w_short", 72), ("hy_b_short", 24), ("hy_bias", 8),
             ("hy_b_out", 8), ("norm1", 8), ("gm_norm", 4), ("conv_w", 16), ("conv_b", 4), ("ba", 4),
             ("bx", 4), ("lam", 4), ("pool_scale", 4), ("norm2", 8), ("final", 8)]
    out, at = {}, 0
    for n, k in names:
        out[n] = (at, k)
        at += k
    return out, at


PCOL, NPAR = param_columns()

CONST = {}
_at = 0
for _n, _k in (("ones", 128), ("ident", 128), ("rot", 128), ("cos", 256), ("sin", 256), ("notfirst", 1), ("eps", 1)):
    CONST[_n] = (_at, _k)
    _at += _k
NCONST = _at
CONST_B = {}
_at = 0
for _n, _k in (("causal", 128), ("tril", 128), ("cmask", 30), ("cvalid", 2), ("recip", 1024)):
    CONST_B[_n] = (_at, _k)
    _at += _k
NCONST_B = _at


def shape_constants():
    f = np.float32
    p = np.arange(P)
    t = np.arange(T)
    c = np.zeros((P, NCONST), f)

    def put(table, where, name, v):
        a, k = where[name]
        table[:, a:a + k] = v

    put(c, CONST, "ones", 1.0)
    put(c, CONST, "ident", np.eye(P))
    rot = np.zeros((P, P))
    first = (p % 32) < 16
    rot[p[first] + 16, p[first]] = -1.0
    rot[p[~first] - 16, p[~first]] = 1.0
    put(c, CONST, "rot", rot)
    inv = (f(10000.0) ** (-(np.arange(16, dtype=f)) / f(16))).astype(f)
    pos = np.where((p % 64)[:, None] < 32, (t // 64)[None, :], (t % 64)[None, :]).astype(f)
    ang = pos * inv[p % 16][:, None]
    put(c, CONST, "cos", np.cos(ang, dtype=f))
    put(c, CONST, "sin", np.sin(ang, dtype=f))
    put(c, CONST, "notfirst", (p > 0).astype(f)[:, None])
    put(c, CONST, "eps", EPS)
    b = np.zeros((P, NCONST_B), f)
    put(b, CONST_B, "causal", np.where(p[None, :] <= p[:, None], 0.0, MASKED))
    put(b, CONST_B, "tril", (p[:, None] <= p[None, :]).astype(f))
    cm = np.zeros((P, 2, NCMP))
    for qt in range(2):
        cm[:, qt] = np.where((16 * np.arange(NCMP) + 31)[None, :] <= (qt * P + p)[:, None], 0.0, MASKED)
    put(b, CONST_B, "cmask", cm.reshape(P, -1))
    put(b, CONST_B, "cvalid", np.stack([p >= 31, p >= 0], 1).astype(f))
    rec = np.stack([1.0 / np.minimum(t + 1, w) for w in POOL_WINDOWS]).astype(f)
    put(b, CONST_B, "recip", np.broadcast_to(rec.reshape(1, -1), (P, 1024)))
    tl = np.linspace(0.0, 1.0, T, dtype=f)[:, None]
    w = f(2.0 * math.pi) * np.arange(T, dtype=f)[:, None] / f(T)
    fr = np.linspace(1e-4, 15, 16, dtype=f)[None, :]
    z = np.concatenate([tl, np.cos(fr * w), -np.sin(fr * w)], axis=1).astype(f)
    deltas = np.abs(np.linspace(math.log(1e-2) / 1.5, math.log(1e-2) / 0.3, D, dtype=f))
    decay = np.exp(-tl * deltas[None, :]).astype(f)
    k = np.arange(T)
    th = 2.0 * np.pi * (k + 0.5)[None, :] * t[:, None] / (2 * T)
    fwd = np.concatenate([np.cos(th), np.sin(th)], axis=1)
    inv_ = np.concatenate([np.cos(th).T, np.sin(th).T], axis=0) / T
    return {
        "const": c, "const_b": b, "zfeat": np.ascontiguousarray(z.T),
        "decay": np.ascontiguousarray(decay.reshape(TT, P, D).transpose(1, 0, 2)),
        "dft": np.ascontiguousarray(fwd.reshape(TT, P, 2 * T).transpose(1, 0, 2).astype(f)),
        "idft": np.ascontiguousarray(inv_.reshape(4, P, T).transpose(1, 0, 2).astype(f)),
    }


def program(nc, A, out):
    n_chunks = N_CHUNKS + 1
    stack = ExitStack()
    sems = {}

    def s(name):
        if name not in sems:
            sems[name] = stack.enter_context(nc.semaphore(name))
        return sems[name]

    def up(value, n=None, step=0):
        return value if n is None else n * step + value

    normed_inputs = ["x", "ctx", "mlp0_in", "hy_in", "hy", "mlp1_in", "mix_in", "merged", "moe_in"]
    turns_of = {
        "squares": [("x", 4), ("ctx", 4), ("post0", 4), ("mlp0_in", 4), ("mlp0", 4), ("hy_in", 4), ("post1", 4), ("mlp1_in", 4),
                    ("mlp1", 4), ("mix_in", 4), ("moe_in", 4), ("final", 2)],
        "normed": [(t, 2 if t in ("hy", "merged") else 4) for t in normed_inputs + ["final"]],
        "h": [(t, 2 if t == "moe" else 4) for t in ("post0", "mlp0", "post1", "mlp1", "mixed", "moe")],
    }
    turns_of["hi"] = turns_of["lo"] = turns_of["normed"][:-1]
    turns_of["sumsq"] = turns_of["std"] = [(t, 1) for t, _ in turns_of["squares"]]

    def cuts(tag, step):
        n = dict(turns_of[step])[tag]
        return [(c, slice(KT // n * c, KT // n * (c + 1))) for c in range(n)]

    def nth(tag, step, count):
        before = 0
        for t, n in turns_of[step]:
            if t == tag:
                return s(step), before + count
            before += n
        raise KeyError((tag, step))

    def mods_before(i):
        return sum(m < i for m in MODS)

    def mlp_plan(layer):
        if layer == 0:
            return 4, 4, 0, list(items(I_MLP0, I_MLP0 + 6))
        return 3, 5, 1, list(items(I_MLP1, I_MLP1 + 3))

    def out_span(layer):
        return (I_OUT1, I_PROJ) if layer else (I_OUT0, I_HY)

    def mlp_nth(tag, step, count):
        per_layer = {"free": 20, "hid_hi": 16, "hidden": 20, "yfree": 6}[step]
        return s("mlp_" + step), count + (per_layer if tag == "mlp1" else 0)

    class Chain:

        def __init__(self, eng, name):
            self.eng, self.sem, self.count, self.n, self.step = eng, s(name), 0, None, 0

        def tick(self, ins):
            self.count += 1
            ins.then_inc(self.sem, 1)
            return up(self.count, self.n, self.step)

        def __call__(self, ins):
            self.eng.wait_ge(self.sem, self.tick(ins))

        def enter(self, n, step):
            self.start, self.n, self.step = self.count, n, step

        def leave(self, turns):
            assert self.count == self.start + self.step, (self.count - self.start, self.step)
            self.count, self.n, self.step = self.start + self.step * turns, None, 0

    with stack:
        def alloc(where, name, shape, dt=F32):
            return where.enter_context(nc.sbuf_tensor(name, [P, *shape], dt))

        raw = alloc(stack, "raw", [RING, CW])
        macc = alloc(stack, "macc", [RING, 256])
        whi = alloc(stack, "whi", [RING, CW], F32R)
        wlo = alloc(stack, "wlo", [RING, CW], F32R)
        h = alloc(stack, "h", [KT, T])
        uhi = alloc(stack, "uhi", [KT, T], F32R)
        ulo = alloc(stack, "ulo", [KT, T], F32R)
        y = alloc(stack, "y", [KT, T])
        sq = alloc(stack, "sq", [KT, T])
        std = alloc(stack, "std", [T])
        rstd = alloc(stack, "rstd", [T])
        par = alloc(stack, "par", [NPAR])
        con = alloc(stack, "con", [NCONST])
        modv = alloc(stack, "modv", [96, 2])
        coef = alloc(stack, "coef", [10, KT])
        small = alloc(stack, "small", [64])
        cvec = alloc(stack, "cvec", [KT, 2])
        csil = alloc(stack, "csil", [KT, 2])
        hdn = alloc(stack, "hdn", [T])
        ps = stack.enter_context(nc.psum_tensor("ps", [P, 8, 512], F32))

        with ExitStack() as st:
            qbuf = alloc(st, "qbuf", [HEADS, T])
            kbuf = alloc(st, "kbuf", [HEADS, 2 * T])
            vbuf = alloc(st, "vbuf", [4, D])
            with ExitStack() as st2:
                ctx_hi = alloc(st2, "ctx_hi", [KT, T], F32R)
                ctx_lo = alloc(st2, "ctx_lo", [KT, T], F32R)
                gap = alloc(st2, "gap", [CW])
                ctx = alloc(st2, "ctx", [KT, T])
                start_acc = alloc(st2, "start_acc", [4, 2, 256])
            obuf = alloc(st, "obuf", [HEADS, T])
            ebuf = alloc(st, "ebuf", [2, 2, 512])
            atb = alloc(st, "atb", [2, 4, T])
        with ExitStack() as st:
            mstart = alloc(st, "mstart", [START_TILES // 2, CW])
        with ExitStack() as st:
            hid_hi = alloc(st, "hid_hi", [DFF // P, T], F32R)
            hid_lo = alloc(st, "hid_lo", [DFF // P, T], F32R)
        with ExitStack() as st:
            hv = alloc(st, "hv", [KT, T])
            hx0 = alloc(st, "hx0", [KT, T])
            hx1 = alloc(st, "hx1", [2, T])
            zpad = alloc(st, "zpad", [2, 2, T + 2])
            vtok = alloc(st, "vtok", [TT, D])
            dft = alloc(st, "dft", [TT, 2 * T])
            idft = alloc(st, "idft", [4, T])
            spec = alloc(st, "spec", [4, D])
            with ExitStack() as st2:
                fwo = alloc(st2, "fwo", [2 * D])
                taps = alloc(st2, "taps", [TT, 512])
            yspec = alloc(st, "yspec", [2, 4, 512])
            prod = alloc(st, "prod", [2, 2, 512])
        with ExitStack() as st:
            gm = alloc(st, "gm", [2, MT, T])
            gate = alloc(st, "gate", [MT, T])
            rec = alloc(st, "rec", [MT, T + 3])
            qn = alloc(st, "qn", [MT, T])
            ksw = alloc(st, "ksw", [2, T])
            vsw = alloc(st, "vsw", [TT, 256])
            xd = alloc(st, "xd", [MT, T + 16])
            gated = alloc(st, "gated", [KT, T])
            yhi = alloc(st, "yhi", [4 * MT, T], F32R)
            with ExitStack() as st2:
                ylo = alloc(st2, "ylo", [4 * MT, T], F32R)
            w1c = alloc(st, "w1c", [2, CMP_LEN * HD])
            w2c = alloc(st, "w2c", [2, HD])
            conb = alloc(st, "conb", [NCONST_B])
            gmw = alloc(st, "gmw", [MT, P])
            gmb = alloc(st, "gmb", [MT, P])
            lruw = alloc(st, "lruw", [2, MT, P])
            hidc = alloc(st, "hidc", [2, 16])
            kc = alloc(st, "kc", [16])
            gates = alloc(st, "gates", [TT, 24])
            lru = alloc(st, "lru", [12, MT])
            sm = alloc(st, "sm", [64])
        with ExitStack() as st:
            comb = alloc(st, "comb", [EXPERTS, T])
            sg = alloc(st, "sg", [DE // P, T])
            hmid = alloc(st, "hmid", [DE // P, T])
            ehi = alloc(st, "ehi", [DE // P, T], F32R)
            elo = alloc(st, "elo", [DE // P, T], F32R)
            wr = alloc(st, "wr", [KT, 20])
            wrhi = alloc(st, "wrhi", [KT, 20], F32R)
            wrlo = alloc(st, "wrlo", [KT, 20], F32R)
            rb = alloc(st, "rb", [20])
            order4 = alloc(st, "order4", [4])
            lg = alloc(st, "lg", [TT, 20])
            ro = alloc(st, "ro", [24, TT, 4])
            cb = alloc(st, "cb", [TT, EXPERTS])
            cbt = alloc(st, "cbt", [T])

        def pcol(name, a=0, k=None):
            c0, n = PCOL[name]
            return par[:, c0 + a:c0 + (a + k if k else n)]

        def ccol(name):
            c0, n = CONST[name]
            return con[:, c0:c0 + n]

        ones, ident, rot = ccol("ones"), ccol("ident"), ccol("rot")

        def over_tiles(x, n):
            return x.unsqueeze(1).to_broadcast([P, n, x.shape[1]])

        def over_cols(x, w):
            return x.unsqueeze(2).to_broadcast([P, x.shape[1], w])

        def f32(x):
            return x.bitcast(F32)

        def mod_scale(layer, part, who):
            return modv[:, layer * 48 + part * 8:layer * 48 + part * 8 + 8, who]

        lamv = std[:]
        zfeat, fw1, fw2 = y[:, 0, :], y[:, 1, 0:HD], y[:, 1, HD:3 * HD].rearrange("p (a d) -> p a d", a=2)
        farg, frnd, fpar = y[:, 2, :], y[:, 3, :], y[:, 5, 0:4]
        decay = y[:].rearrange("p (t a) c -> p t (a c)", t=TT)
        tapf, tapb = sq[:, 0:4, :].rearrange("p (t a) c -> p t (a c)", t=TT), sq[:, 4:8, :].rearrange("p (t a) c -> p t (a c)", t=TT)

        poolw = macc[:].rearrange("p a c -> p (a c)")[:, 0:MT * P].rearrange("p (m c) -> p m c", m=MT)
        vc, cpe = hdn[:, 0:P], hdn[:, P:P + 2 * CMP_LEN].rearrange("p (c l) -> p c l", c=2)

        def bcol(name):
            c0, n = CONST_B[name]
            return conb[:, c0:c0 + n]

        ug, vg = gm[:, 0], gm[:, 1].rearrange("p (t a) c -> p t (a c)", t=TT)
        mixb = gm[:].rearrange("p a m t -> p (a m) t")
        causal, tril = bcol("causal"), bcol("tril")
        blocks = sq[:, 0:4, :].rearrange("p a c -> p (a c)")[:, 0:2 * CMP_LEN * NCMP].rearrange("p (c l n) -> p c l n", c=2, l=CMP_LEN)
        cmp_t = sq[0:NCMP].rearrange("p a c -> p (a c)").rearrange("p (u q) -> p u q", u=16)
        cmp_p = sq[:, 0, 0:2 * HEADS * NCMP].rearrange("p (t h n) -> p t h n", t=TT, h=HEADS)
        nsa_e = mixb[:, 0:4, :].rearrange("p (a b) k -> p a b k", a=2)
        nsa_t = mixb[:, 4:8, :]
        slot_of = {n: MT * b for b, n in enumerate(BRANCH_ORDER)}

        TAPS_BANK = {(0, 0): 2, (0, 1): 4, (1, 0): 4, (1, 1): 6}
        SPEC_BANK = {(0, 0): 6, (0, 1): 2, (1, 0): 6, (1, 1): 4}
        CONV_BANKS = ((2, 3, 4, 5), (6, 7, 0, 1))

        MID = {t: (2 * (t - 9) if t < 15 else t - 3) for t in range(9, 22)}
        END = {**{t: 2 * (t - 9) + 1 for t in range(9, 15)}, 21: 19}

        block = stack.enter_context(nc.Block())

        @block.sync
        def _(sp):
            W = A["weights"]
            for dst, src in [(cvec[:], A["cvec"]), (con[:], A["const"]), (par[:], A["params"]),
                             (lamv, A["attn_lambda"].partition_broadcast(P))]:
                sp.dma_start(dst, src).then_inc(s("small_loaded"), 16)
            sp.dma_start(h[:], A["x"]).then_inc(s("x_loaded"), 16)
            for j in range(4):
                if j == 2:
                    sp.dma_start(ctx[:], A["ctx"]).then_inc(s("ctx_loaded"), 16)
                sp.dma_start(mstart[:, 2 * j:2 * j + 2, :], A["mod_start"][:, 2 * j:2 * j + 2, :]).then_inc(s(f"start_loaded{j}"), 16)
            for i in range(RING):
                sp.dma_start(raw[:, i, :], W[i]).then_inc(s(f"raw_loaded{i}"), 16)
            turns, rest = divmod(n_chunks - RING, RING)
            with sp.Fori(0, turns) as n:
                for j in range(RING):
                    sp.wait_ge(s("lo_ready"), n * RING + (j + 1))
                    sp.dma_start(raw[:, j, :], W[bass.ds(n * RING + (RING + j), 1)].rearrange("a p c -> (a p) c"))\
                        .then_inc(s(f"raw_loaded{j}"), 16)
            for j in range(rest):
                i = RING * (turns + 1) + j
                sp.wait_ge(s("lo_ready"), i - RING + 1)
                sp.dma_start(raw[:, j, :], W[i]).then_inc(s(f"raw_loaded{j}"), 16)
            for c, part in cuts("final", "normed"):
                sp.wait_ge(*nth("final", "normed", c + 1))
                sp.dma_start(out[:, part, :], y[:, part, :]).then_inc(s("stored"), 16)
            sp.wait_ge(s("stored"), 16 * len(cuts("final", "normed")))

        @block.gpsimd
        def _(pool):
            pool.wait_ge(s("chunk_used"), I_HY)
            for dst, src in [(fwo[0:HD, :], A["hy_filt_w_out"]), (dft[:], A["dft"]), (idft[:], A["idft"])]:
                pool.dma_start(dst, src).then_inc(s("hyena_loaded"), 16)
            pool.wait_ge(s("chunk_used"), I_PROJ)
            for dst, src in [(cpe, A["cmp_pe"]), (conb[:], A["const_b"]), (gmw[:], A["gm_ws"]),
                             (gmb[:].rearrange("p a b -> p (a b)"), A["gm_b"].partition_broadcast(P)), (poolw, A["pool_w"])]:
                pool.dma_start(dst, src).then_inc(s("mixer_loaded"), 16)
            for dst, src in [(w1c[:], A["cmp_w1"]), (w2c[:], A["cmp_w2"])]:
                pool.dma_start(dst, src).then_inc(s("cmp_loaded"), 16)
            for b in (lruw[:], rec[:, :, 0:3], xd[:, :, 0:16]):
                ins = nc.gpsimd.memset(b, 0.0)
            ins.then_inc(s("lru_clear"), 1)
            pool.wait_ge(s("lru_clear"), 1)
            for w, name in enumerate(("lru_wa", "lru_wx")):
                for o in range(2):
                    pool.dma_start(lruw[o * HD:(o + 1) * HD, w, :, o * HD:(o + 1) * HD], A[name][o]).then_inc(s("lru_loaded"), 16)
            pool.wait_ge(s("chunk_used"), I_MOE)
            for dst, src in [(wr[:], A["router_w"]), (rb[:], A["router_b"].partition_broadcast(P)), (order4[:], A["order4"])]:
                pool.dma_start(dst, src).then_inc(s("router_loaded"), 16)

        @block.tensor
        def _(pe):
            mm = nc.tensor.matmul

            def three(o, w0, w1, x0, x1, first, last, **kw):
                mm(o, w0, x0, start=first, stop=False, **kw)
                mm(o, w1, x0, start=False, stop=False, **kw)
                return mm(o, w0, x1, start=False, stop=last, **kw)

            def three_rows(mm, o, a0, a1, w0, w1, first, last):
                mm(o, a0, w0, start=first, stop=False)
                mm(o, a0, w1, start=False, stop=False)
                return mm(o, a1, w0, start=False, stop=last)

            def weights_ready(i, n=None, step=0):
                pe.wait_ge(s("lo_ready"), up(i + 1, n, step))

            def used(ins):
                ins.then_inc(s("chunk_used"), 1)

            def tiles(i, bank_of, xs, kts=8, width=2, cols=T, k0=0, first=True, last=True, x_wait=None, between=None):
                sl = i % RING
                span = P * width
                for m in range(width):
                    for x_i, (x0, x1) in enumerate(xs):
                        o = bank_of(m, x_i)
                        for k in range(kts):
                            if x_wait and m == 0:
                                tag = x_wait[x_i] if len(xs) > 1 else x_wait
                                for c, part in cuts(tag, "lo"):
                                    if part.start == k:
                                        pe.wait_ge(*nth(tag, "lo", c + 1))
                            w = k * span + m * P
                            ins = three(o, whi[:, sl, w:w + P], wlo[:, sl, w:w + P], x0[:, k0 + k, :], x1[:, k0 + k, :],
                                        first and k == 0, last and k == kts - 1)
                    if between and m == width // 2 - 1:
                        between()
                return ins

            def by_token(i, out_of, xs, ncols=256):
                sl = i % RING
                tt = 0
                for x0, x1 in xs:
                    for t0 in range(TT):
                        o = out_of(tt)
                        tt += 1
                        for k in range(KT):
                            w0, w1 = (w[:, sl, k * 256:k * 256 + ncols] for w in (whi, wlo))
                            a0, a1 = (x[:, k, t0 * P:(t0 + 1) * P] for x in (x0, x1))
                            mm(o, a0, w0, start=k == 0, stop=False)
                            mm(o, a0, w1, start=False, stop=False)
                            ins = mm(o, a1, w0, start=False, stop=k == KT - 1)
                return ins

            def modulation(i, q, n=None, step=0, turn=0):
                pe.wait_ge(s("mod_drained"), up(q + 1, n, turn))
                weights_ready(i, n, step)
                for m in range(2):
                    ins = mm(ps[:, 7, m:m + 1], macc[:, i % RING, m * P:(m + 1) * P], ones[:, 0:1], start=True, stop=True)
                used(ins)

            def sum_squares(tag, bank, src=sq):
                for c, part in cuts(tag, "squares"):
                    pe.wait_ge(*nth(tag, "squares", c + 1))
                    for k in range(part.start, part.stop):
                        ins = mm(ps[:, bank, 0:T], ones, src[:, k, :], start=k == 0, stop=k == KT - 1)
                ins.then_inc(s("sumsq"), 1)

            def filter_layer(j):
                if j == 0:
                    pe.wait_ge(s("filter_loaded"), 16 * 4)
                    w, x = fw1[0:33, :], zfeat[0:33, :]
                else:
                    pe.wait_ge(s("filter_sin"), j)
                    w, x = fw2[0:HD, j - 1, :], hdn[0:HD, :]
                mm(ps[0:HD, 6, 0:T], w, x, start=True, stop=True).then_inc(s("filter_layer"), 1)

            def filter_taps(half, t0):
                r, b = 2 * half + t0, TAPS_BANK[half, t0]
                if r == 0:
                    pe.wait_ge(s("hyena_loaded"), 16 * 3)
                elif r == 2:
                    pe.wait_ge(s("taps_ready"), 2)
                elif r == 3:
                    pe.wait_ge(s("spec_stored"), 1)
                for d in range(2):
                    ins = mm(ps[:, b + d, :], hdn[0:HD, t0 * P:(t0 + 1) * P],
                             fwo[0:HD, d * D + half * 512:d * D + half * 512 + 512], start=True, stop=True)
                ins.then_inc(s("filter_taps"), 1)

            def filter_spec(half, kind):
                pe.wait_ge(s("taps_ready"), 2 * half + 2)
                b = SPEC_BANK[half, kind]
                for k in range(2):
                    for t0 in range(TT):
                        ins = mm(ps[:, b + k, :], dft[:, t0, (2 * kind + k) * P:(2 * kind + k + 1) * P],
                                 (tapf if kind else taps)[:, t0, :], start=t0 == 0, stop=t0 == 1)
                ins.then_inc(s("filter_spec"), 1)

            pe.wait_ge(s("c_silu"), 1)
            for j in range(0, START_TILES // 2, 2):
                pe.wait_ge(s(f"start_loaded{j // 2}"), 16)
                if j == 2:
                    sum_squares("x", 4)
                for m in range(2):
                    for k in range(KT):
                        w = k * 2 * P + m * P
                        mm(ps[:, 7, 4 * j + 2 * m:4 * j + 2 * m + 2], mstart[:, j, w:w + P], csil[:, k, :], start=k == 0, stop=k == KT - 1)
            for j in range(1, START_TILES // 2, 2):
                pe.wait_ge(s("start_weighted"), (j + 1) // 2)
                for w in range(2):
                    for m in range(2):
                        c = 4 * j + 2 * m + w
                        ins = mm(ps[:, 7, c:c + 1], start_acc[:, j // 2, w, m * P:(m + 1) * P], ones[:, 0:1], start=True, stop=True)
            ins.then_inc(s("mod_start"), 1)

            sum_squares("ctx", 5, src=y)
            lat, con_x = (uhi, ulo), (ctx_hi, ctx_lo)

            def rope(r):
                pe.wait_ge(s("qkv_drained"), r + 1)
                if r >= 2:
                    pe.wait_ge(s("rope_drained"), r - 1)
                src = kbuf[:, 2 * r:2 * r + 2, T:2 * T] if r < 4 else qbuf[:, 2 * (r - 4):2 * (r - 4) + 2, :]
                mm(ps[:, 4 + r % 2, :], rot, src, start=True, stop=True).then_inc(s("roped"), 1)

            for i, g, q in items(I_QKV, I_ATT):
                if g is None:
                    modulation(i, q)
                    continue
                b = 2 * (g % 2)
                if g >= 2:
                    pe.wait_ge(s("qkv_drained"), g - 1)
                weights_ready(i)
                if g < 4:
                    ins = tiles(i, lambda m, x_i: ps[:, b + m, (1 - x_i) * T:(2 - x_i) * T], [lat, con_x],
                                x_wait=("x", "ctx") if g == 0 else None)
                elif g < 8:
                    ins = tiles(i, lambda m, _: ps[:, b, m * T:(m + 1) * T], [lat])
                else:
                    ins = by_token(i, lambda tt: ps[:, b + tt // 2, (tt % 2) * 256:(tt % 2) * 256 + 256], [con_x, lat])
                used(ins)
                if 1 <= g <= 8:
                    rope(g - 1)
                if 7 <= g <= 9:
                    filter_layer(g - 7)

            def scores(u):
                hd, qt = divmod(u, 2)
                if u >= 2:
                    pe.wait_ge(s("exps"), u - 1)
                for p in range(2):
                    a = slice(p * HD, (p + 1) * HD)
                    ins = mm(ps[:, 2 * (u % 2) + p, :], qbuf[a, hd, qt * P:(qt + 1) * P], kbuf[a, hd, :], start=True, stop=True)
                ins.then_inc(s("scores"), 1)

            def turn_weights(u):
                pe.wait_ge(s("att_ready"), u + 1)
                if u >= 2:
                    pe.wait_ge(s("att_copied"), u - 1)
                for k in range(4):
                    ins = nc.tensor.transpose(ps[:, 4 + u % 2, k * P:(k + 1) * P], ebuf[:, u % 2, 0, k * P:(k + 1) * P], ident)
                ins.then_inc(s("att_turned"), 1)

            def values(hd):
                pe.wait_ge(s("att_copied"), 2 * hd + 2)
                if hd:
                    pe.wait_ge(s("o_copied"), hd)
                for k in range(4):
                    ins = mm(ps[:, 6, 0:T], vbuf[:, k, hd * P:(hd + 1) * P], atb[:, hd % 2, k, :], start=k == 0, stop=k == 3)
                ins.then_inc(s("o_ready"), 1)

            pe.wait_ge(s("roped_all"), 8)
            pe.wait_ge(s("qkv_drained"), 12)
            pe.wait_ge(s("filter_arg"), 3)
            def sum_head_squares(c):
                pe.wait_ge(s("o_squares"), 2 * c + 2)
                pe.wait_ge(s("exps"), 16)
                mm(ps[:, c, :], ones, sq[:, 2 * c:2 * c + 2, :], start=True, stop=True).then_inc(s("o_sumsq"), 1)

            for u in range(2 * HEADS + 4):
                if u < 2 * HEADS:
                    scores(u)
                if 2 <= u <= 2 * HEADS + 1:
                    turn_weights(u - 2)
                if u == 2 * HEADS + 1:
                    for c in range(3):
                        sum_head_squares(c)
                if u >= 5 and u % 2:
                    values((u - 5) // 2)
                if u % 2 == 0 and u < 2 * HEADS:
                    modulation(I_ATT + u // 2, MODS.index(I_ATT + u // 2))
            sum_head_squares(3)

            def out_rows(tag, i0, xs=(uhi, ulo), x_wait=None):
                for g in range(4):
                    weights_ready(i0 + g)
                    used(tiles(i0 + g, lambda m, _: ps[:, g, m * T:(m + 1) * T], [xs], x_wait=x_wait if g == 0 else None))
                sum_squares(tag, 4)

            pe.wait_ge(s("o_lo"), 4)
            out_rows("post0", I_AO)

            def mlp(layer, tag, i0):
                sum_squares(tag + "_in", 5)
                slots, turns, rest, body = mlp_plan(layer)
                with pe.Fori(0, turns) as n:
                    for i, g, q in body:
                        if g is None:
                            modulation(i, q, n, len(body), len(body) - slots)
                            continue
                        pe.wait_ge(*mlp_nth(tag, "free", up(g + 1, n, slots)))
                        weights_ready(i, n, len(body))
                        used(tiles(i, lambda m, _: ps[:, g, m * T:(m + 1) * T], [(uhi, ulo)], x_wait=tag + "_in" if g == 0 else None))
                for r in range(rest):
                    pe.wait_ge(*mlp_nth(tag, "free", slots * turns + r + 1))
                    weights_ready(i0 + len(body) * turns + r)
                    used(tiles(i0 + len(body) * turns + r, lambda m, _: ps[:, r, m * T:(m + 1) * T], [(uhi, ulo)]))
                pe.wait_ge(*mlp_nth(tag, "free", 16 + slots))
                for i, g, q in items(*out_span(layer)):
                    if g is None:
                        modulation(i, q)
                        continue
                    m0, kg = divmod(g, 4)
                    if kg == 0:
                        pe.wait_ge(*mlp_nth(tag, "yfree", m0 + 1))
                    if m0 == 0:
                        pe.wait_ge(*mlp_nth(tag, "hidden", slots + 4 * kg + 4))
                    weights_ready(i)
                    used(tiles(i, lambda m, _: ps[:, 2 * (m0 % 2) + m, 0:T], [(hid_hi, hid_lo)], k0=8 * kg,
                               first=kg == 0, last=kg == 3))
                sum_squares(tag, 4)

            mlp(0, "mlp0", I_MLP0)

            def turn_v(j):
                pe.wait_ge(s("v_ready"), j + 1)
                if j < 2:
                    pe.wait_ge(s("spec_stored"), 2)
                else:
                    pe.wait_ge(s("vtok_stored"), j - 1)
                for m in range(2):
                    for t0 in range(TT):
                        ins = nc.tensor.transpose(ps[:, 2 + j % 2, (2 * m + t0) * P:(2 * m + t0 + 1) * P],
                                                  hv[:, 2 * j + m, t0 * P:(t0 + 1) * P], ident)
                ins.then_inc(s("v_turned"), 1)

            sum_squares("hy_in", 5)
            for g in range(12):
                if g >= 2:
                    pe.wait_ge(s("hy_drained"), g - 1)
                weights_ready(I_HY + g)
                used(tiles(I_HY + g, lambda m, _: ps[:, g % 2, m * T:(m + 1) * T], [(uhi, ulo)], x_wait="hy_in" if g == 0 else None))
                if g == 0:
                    pe.wait_ge(s("mod_drained"), mods_before(I_HY) + 1)
                if g in (1, 2):
                    filter_taps(0, g - 1)
                if g in (4, 5):
                    filter_spec(0, g - 4)
                if g in (5, 6):
                    filter_taps(1, g - 5)
                if g in (7, 9):
                    turn_v(g - 7)
                    turn_v(g - 6)
                if g in (8, 9):
                    filter_spec(1, g - 8)
            pe.wait_ge(s("vtok_stored"), 4)
            for half in range(2):
                pe.wait_ge(s("spec_stored"), 4)
                if half:
                    pe.wait_ge(s("hy_drained"), 12)
                for k in range(4):
                    for t0 in range(TT):
                        ins = mm(ps[:, CONV_BANKS[half][k], :], dft[:, t0, k * P:(k + 1) * P], vtok[:, t0, half * 512:half * 512 + 512],
                                 start=t0 == 0, stop=t0 == 1)
                ins.then_inc(s("vspec"), 1)
            for half in range(2):
                pe.wait_ge(s("yspec_ready"), half + 1)
                for m in range(4):
                    for k in range(4):
                        ins = mm(ps[:, CONV_BANKS[half][m], 0:T], yspec[:, half, k, m * P:(m + 1) * P], idft[:, k, :], start=k == 0, stop=k == 3)
                    ins.then_inc(s("conv"), 1)
            out_rows("post1", I_HO, x_wait="hy")
            mlp(1, "mlp1", I_MLP1)

            u_parts = (uhi, ulo)

            def compress():
                pe.wait_ge(s("blocks_ready"), 1)
                pe.wait_ge(s("cmp_loaded"), 16 * 2)
                for g in range(2):
                    a = slice(g * HD, (g + 1) * HD)
                    for c in range(2):
                        for l in range(CMP_LEN):
                            ins = mm(ps[a, 4, 16 * c:16 * c + NCMP], w1c[a, c, l * HD:(l + 1) * HD], blocks[a, c, l, :],
                                     start=l == 0, stop=l == CMP_LEN - 1)
                ins.then_inc(s("cmp_hidden"), 1)

            def compress_out():
                pe.wait_ge(s("cmp_gelu"), 1)
                for g in range(2):
                    a = slice(g * HD, (g + 1) * HD)
                    mm(ps[a, 5, 0:NCMP], w2c[a, 0, :], hidc[a, 0, 0:NCMP], start=True, stop=True)
                    ins = mm(ps[0:NCMP, 6 + g, 0:HD], hidc[a, 1, 0:NCMP], w2c[a, 1, :], start=True, stop=True)
                ins.then_inc(s("cmp_out"), 1)

            def head(u):
                return u // 4, (u // 2) % 2, u % 2

            def nsa_scores(u):
                j, g, qt = head(u)
                a = slice(g * HD, (g + 1) * HD)
                if u >= 2:
                    pe.wait_ge(s("nsa_exps"), u - 1)
                for b in range(2):
                    ins = mm(ps[:, u % 2, b * T:b * T + (qt + 1) * P], qn[a, j, qt * P:(qt + 1) * P], ksw[a, b, 0:(qt + 1) * P],
                             start=True, stop=True)
                ins.then_inc(s("nsa_scores"), 1)

            def nsa_turn(u):
                j, g, qt = head(u)
                pe.wait_ge(s("nsa_weights"), u + 1)
                if u >= 2:
                    pe.wait_ge(s("nsa_copied"), u - 1)
                for b in range(2):
                    for k in range(qt + 1):
                        n = b * (qt + 1) + k
                        ins = nc.tensor.transpose(ps[:, 2 + u % 2, n * P:(n + 1) * P], nsa_e[:, u % 2, b, k * P:(k + 1) * P], ident)
                ins.then_inc(s("nsa_turned"), 1)

            def nsa_values(u):
                j, g, qt = head(u)
                pe.wait_ge(s("nsa_copied"), u + 1)
                if u % 4 == 0 and j >= 2:
                    pe.wait_ge(s("nsa_out_lo"), j - 1)
                o = ps[g * HD:(g + 1) * HD, 4 + j % 2, qt * P:(qt + 1) * P]
                for b in range(2):
                    for k in range(qt + 1):
                        n = b * (qt + 1) + k
                        mm(o, vsw[:, k, b * P + g * HD:b * P + (g + 1) * HD], nsa_t[:, 2 * (u % 2) + n // 2, (n % 2) * P:(n % 2 + 1) * P],
                           start=n == 0, stop=False)
                mm(o, vc[0:NCMP, g * HD:(g + 1) * HD], cmp_t[:, qt * 8 + g * 4 + j, :], start=False, stop=True).then_inc(s("nsa_out"), 1)

            sum_squares("mix_in", 5)
            for g in range(16):
                i = I_PROJ + g
                if g >= 4:
                    pe.wait_ge(s("proj_drained"), g - 3)
                weights_ready(i)
                if g in (4, 12, 13):
                    ins = by_token(i, lambda tt: ps[:, g % 4, tt * 256:tt * 256 + 256], [u_parts])
                elif g == 5:
                    ins = by_token(i, lambda tt: ps[:, g % 4, tt * 256:tt * 256 + 24], [u_parts], 24)
                else:
                    ins = tiles(i, lambda m, _: ps[:, g % 4, m * T:(m + 1) * T], [u_parts], x_wait="mix_in" if g == 0 else None)
                used(ins)
                if g == 2:
                    compress()
                if g == 4:
                    compress_out()
            def beside(t):
                if t == 0:
                    pe.wait_ge(s("pooled"), 1)
                    pe.wait_ge(s("cmp_stored"), 1)
                    for g in range(MT):
                        ins = mm(ps[:, 4 + g // 2, (g % 2) * T:(g % 2 + 1) * T], poolw[:, g, :], xd[:, g, 16:16 + T], start=True, stop=True)
                    ins.then_inc(s("pool_mapped"), 1)
                if t == 1:
                    pe.wait_ge(s("v_normed"), 1)
                    pe.wait_ge(s("proj_drained"), 16)
                    for n in range(TT):
                        for g in range(MT):
                            ins = mm(ps[:, g // 2, (g % 2) * T + n * P:(g % 2) * T + (n + 1) * P], vg[:, n, g * P:(g + 1) * P], gmw[:, g, :],
                                     start=True, stop=True)
                    ins.then_inc(s("gm_mixed"), 1)
                if t == 2:
                    pe.wait_ge(s("rec_conved"), 1)
                    pe.wait_ge(s("lru_loaded"), 16 * 4)
                    pe.wait_ge(s("pool_lo"), 1)
                    for w in range(2):
                        for m in range(MT):
                            ins = mm(ps[:, 2 + 2 * w + m // 2, (m % 2) * T:(m % 2 + 1) * T], lruw[:, w, m, :], sq[:, m, :], start=True, stop=True)
                    ins.then_inc(s("rec_gates"), 1)
                if t == 6:
                    pe.wait_ge(s("gm_ready"), 1)
                    pe.wait_ge(s("rec_tanh"), 2)
                    for qt in range(2):
                        for g in range(2):
                            a = slice(g * HD, (g + 1) * HD)
                            for j in range(4):
                                ins = mm(ps[:, 2 * qt + g, 16 * j:16 * j + NCMP], qn[a, j, qt * P:(qt + 1) * P], kc[a, 0:NCMP], start=True, stop=True)
                    ins.then_inc(s("cmp_scores"), 1)
                if t == 8:
                    pe.wait_ge(s("cmp_weights"), 1)
                    for u in range(16):
                        ins = nc.tensor.transpose(ps[0:NCMP, u // 4, (u % 4) * P:(u % 4 + 1) * P], cmp_p[:, u // 8, u % 8, :], ident)
                    ins.then_inc(s("cmp_turned"), 1)

            def attend(u):
                if u == 0:
                    pe.wait_ge(s("cmp_t_ready"), 1)
                if u < 16:
                    nsa_scores(u)
                if 2 <= u <= 17:
                    nsa_turn(u - 2)
                if 3 <= u <= 18:
                    nsa_values(u - 3)

            for t in range(24):
                n, g = divmod(t, 6)
                i = I_BR + t
                if g < 2:
                    if n:
                        pe.wait_ge(s("br_free"), 2 * n)
                elif g < 4:
                    pe.wait_ge(s("mg_free"), 4 * n + g - 1)
                elif g == 4:
                    pe.wait_ge(s("mg_free"), 4 * n + 4)
                    for name, count in (("gm_lo", 1), ("pool_lo", 1), ("lru_lo", 1), ("nsa_out_lo", 4))[n:n + 1]:
                        pe.wait_ge(s(name), count)
                else:
                    pe.wait_ge(s("br_free"), 2 * n + 1)
                weights_ready(i)
                mid = (lambda: attend(MID[t])) if t in MID else None
                if g < 4:
                    used(tiles(i, lambda m, _: ps[:, 6 + g % 2, m * T:(m + 1) * T], [u_parts], between=mid))
                else:
                    used(tiles(i, lambda m, _: ps[:, 6 + m // 2, (m % 2) * T:(m % 2 + 1) * T], [(yhi, ylo)], kts=MT, width=4, k0=MT * n,
                               between=mid))
                if t in END:
                    attend(END[t])
                beside(t)
            pe.wait_ge(s("nsa_out_hi"), 4)
            for g in range(4):
                weights_ready(I_WO + g)
                used(tiles(I_WO + g, lambda m, _: ps[:, g, m * T:(m + 1) * T], [u_parts], x_wait="merged" if g == 0 else None))

            sum_squares("moe_in", 5)
            pe.wait_ge(*nth("moe_in", "lo", 4))
            pe.wait_ge(s("router_lo"), 1)
            for t0 in range(TT):
                for k in range(KT):
                    a0, a1 = (x[:, k, t0 * P:(t0 + 1) * P] for x in u_parts)
                    ins = three_rows(mm, ps[:, 4, t0 * 32:t0 * 32 + 20], a0, a1, wrhi[:, k, :], wrlo[:, k, :], k == 0, k == KT - 1)
            ins.then_inc(s("router"), 1)
            pe.wait_ge(*nth("mixed", "h", 4))

            def up_rows(i, bank, n=None):
                weights_ready(i, n, 6)
                used(tiles(i, lambda m, _: ps[:, bank, m * T:(m + 1) * T], [u_parts]))

            def down_rows(i, j, n=None):
                if n is None:
                    pe.wait_ge(s("moe_hid"), 2 * EXPERTS)
                    pe.wait_ge(s("moe_free"), 2 * EXPERTS - 2 + j + 1)
                else:
                    pe.wait_ge(s("moe_hid"), n * 2 + 2)
                    pe.wait_ge(s("moe_free"), n * 2 + (j + 1))
                weights_ready(i, n, 6)
                used(tiles(i, lambda m, _: ps[:, 4 + 2 * j + m // 2, (m % 2) * T:(m % 2 + 1) * T], [(ehi, elo)], kts=4, width=4))

            for j in range(4):
                up_rows(I_MOE + j, j)
            pe.wait_ge(s("combine_ready"), 1)
            for t0 in range(TT):
                ins = nc.tensor.transpose(ps[0:EXPERTS, 5, t0 * P:(t0 + 1) * P], cb[:, t0, :], ident)
            ins.then_inc(s("combine_turned"), 1)
            pe.wait_ge(s("combine_copied"), 1)
            for e in range(EXPERTS):
                if e >= 8 and e % 2 == 0:
                    pe.wait_ge(s("comb_stored"), (e - 8) // 2 + 1)
                ins = mm(ps[:, 4 + (e // 2) % 4, (e % 2) * T:(e % 2 + 1) * T], ident[0:EXPERTS, e:e + 1].to_broadcast([EXPERTS, P]),
                         cbt[0:EXPERTS, :], start=True, stop=True)
                if e % 2:
                    ins.then_inc(s("comb_spread"), 1)
            with pe.Fori(0, EXPERTS - 1) as n:
                i = I_MOE + 4
                for j in range(2):
                    pe.wait_ge(s("moe_silu"), n * 2 + (j + 1))
                    up_rows(i + j, j, n)
                for j in range(2):
                    down_rows(i + 2 + j, j, n)
                for j in range(2):
                    pe.wait_ge(s("moe_gated"), n * 2 + (j + 1))
                    up_rows(i + 4 + j, 2 + j, n)
            for j in range(2):
                down_rows(N_CHUNKS - 2 + j, j)
            sum_squares("final", 0)

        @block.scalar
        def _(act):
            fn = nc.scalar.activation
            def split(i, n=None, step=0):
                if i >= n_chunks and n is None or i in MODS:
                    return
                sl = i % RING
                act.wait_ge(s(f"raw_loaded{sl}"), up(16 * (i // RING + 1), n, 16 * step // RING))
                if i >= RING:
                    act.wait_ge(s("chunk_used"), up(i - RING + 1, n, step))
                fn(whi[:, sl, :], raw[:, sl, :], ACT.Copy).then_inc(s("hi_ready"), 1)

            def product(i, n=None, step=0):
                act.wait_ge(s("chunk_used"), up(i + 1, n, step))

            chain = Chain(act, "act_chain")
            eps = ccol("eps")

            def squares(tag, src, dst=sq):
                for c, part in cuts(tag, "squares"):
                    fn(dst[:, part, :], src[:, part, :], ACT.Square).then_inc(s("squares"), 1)

            def root(tag, bank):
                act.wait_ge(*nth(tag, "sumsq", 1))
                fn(std[:], ps[:, bank, 0:T], ACT.Sqrt, bias=eps, scale=1.0 / D).then_inc(s("std"), 1)

            def high(tag, src, dst, shift=None):
                for c, part in cuts(tag, "hi"):
                    act.wait_ge(*nth(tag, "normed", c + 1))
                    if shift is None:
                        ins = fn(dst[:, part, :], src[:, part, :], ACT.Copy)
                    else:
                        for k in range(part.start, part.stop):
                            ins = fn(dst[:, k, :], src[:, k, :], ACT.Identity, bias=shift[:, k:k + 1])
                    ins.then_inc(s("hi"), 1)

            def next_squares(tag, prev):
                for c, part in cuts(tag, "squares"):
                    act.wait_ge(*nth(prev, "h", c + 1))
                    fn(sq[:, part, :], h[:, part, :], ACT.Square).then_inc(s("squares"), 1)

            act.wait_ge(s("small_loaded"), 16 * 4)
            fn(csil[:], cvec[:], ACT.Tanh, scale=0.5).then_inc(s("c_tanh"), 1)
            act.wait_ge(s("x_loaded"), 16)
            act.wait_ge(s("lam_sums"), 1)
            squares("x", h)
            root("x", 4)
            act.wait_ge(s("ctx_loaded"), 16)
            squares("ctx", ctx, y)
            split(0)
            high("x", y, uhi, mod_scale(0, 0, 0))
            root("ctx", 5)
            high("ctx", ctx, ctx_hi, mod_scale(0, 0, 1))
            for i in range(1, RING):
                split(i)

            def filter_sin(j):
                act.wait_ge(s("filter_arg"), j + 1)
                fn(hdn[0:HD, :], farg[0:HD, :], ACT.Sin).then_inc(s("filter_sin"), 1)

            act.wait_ge(*nth("x", "lo", 4))
            for dst, src in [(zfeat[0:33, :], A["zfeat"]), (fw1[0:33, :], A["hy_filt_w1"]), (fw2[0:HD], A["hy_filt_w2"]),
                             (fpar[0:HD, :], A["fpar"])]:
                act.dma_start(dst, src).then_inc(s("filter_loaded"), 16)
            for i, g, q in items(I_QKV, I_ATT):
                if g is None:
                    split(i + RING)
                    continue
                b = 2 * (g % 2)
                product(i)
                if g < 4:
                    ins = fn(kbuf[:, 2 * g:2 * g + 2, :], ps[:, b:b + 2, :], ACT.Copy)
                elif g < 8:
                    ins = fn(qbuf[:, 2 * (g - 4):2 * (g - 4) + 2, :], ps[:, b, :].rearrange("p (m t) -> p m t", m=2), ACT.Copy)
                else:
                    v0 = (g - 8) * 256
                    ins = fn(vbuf[:, :, v0:v0 + 256], ps[:, b:b + 2, :].rearrange("p b (t c) -> p (b t) c", t=2), ACT.Copy)
                ins.then_inc(s("qkv_drained"), 1)
                split(i + RING)
                if 7 <= g <= 9:
                    filter_sin(g - 7)

            def exps(u):
                act.wait_ge(s("max_ready"), u + 1)
                if u >= 2:
                    act.wait_ge(s("att_turned"), u - 1)
                for p in range(2):
                    ins = fn(ebuf[:, u % 2, p, :], ps[:, 2 * (u % 2) + p, :], ACT.Exp, scale=SCALE,
                             bias=small[:, 4 * (u % 2) + p:4 * (u % 2) + p + 1],
                             accum_out=small[:, 8 + 4 * (u % 2) + p:9 + 4 * (u % 2) + p])
                ins.then_inc(s("exps"), 1)

            def head_root(c):
                act.wait_ge(s("o_sumsq"), c + 1)
                fn(y[:, 2 * c:2 * c + 2, :], ps[:, c, :].rearrange("p (m t) -> p m t", m=2), ACT.Sqrt, bias=eps, scale=1.0 / P).then_inc(s("o_std"), 1)

            fn(small[:, 24:26], small[:, 22:24], ACT.Exp).then_inc(s("lam_exps"), 1)
            for u in range(2 * HEADS + 4):
                if u < 2 * HEADS:
                    exps(u)
                if 2 <= u <= 2 * HEADS + 1:
                    v = u - 2
                    act.wait_ge(s("att_turned"), v + 1)
                    if v >= 4:
                        act.wait_ge(s("o_ready"), v // 2 - 1)
                    fn(atb[:, (v // 2) % 2, :, (v % 2) * P:(v % 2 + 1) * P], ps[:, 4 + v % 2, :].rearrange("p (k q) -> p k q", k=4),
                       ACT.Copy).then_inc(s("att_copied"), 1)
                if u == 2 * HEADS + 1:
                    for c in range(3):
                        head_root(c)
                if u % 2 == 0 and u < 2 * HEADS:
                    split(I_ATT + u // 2 + RING)
                if u >= 5 and u % 2:
                    hd = (u - 5) // 2
                    act.wait_ge(s("o_ready"), hd + 1)
                    fn(sq[:, hd, :], ps[:, 6, 0:T], ACT.Square).then_inc(s("o_squares"), 1)
                    fn(obuf[:, hd, :], ps[:, 6, 0:T], ACT.Copy).then_inc(s("o_copied"), 1)
            head_root(3)
            for c in range(4):
                act.wait_ge(s("o_normed"), c + 1)
                fn(uhi[:, 2 * c:2 * c + 2, :], obuf[:, 2 * c:2 * c + 2, :], ACT.Copy).then_inc(s("o_hi"), 1)

            def take_rows(tag, i0, bias=None):
                for g in range(4):
                    product(i0 + g)
                    dst = slice(2 * g, 2 * g + 2)
                    if bias is None:
                        src = ps[:, g, :].rearrange("p (m t) -> p m t", m=2)
                        fn(y[:, dst, :], src, ACT.Copy)
                        fn(sq[:, dst, :], src, ACT.Square).then_inc(s("squares"), 1)
                    else:
                        for m in range(2):
                            b = pcol(bias, 2 * g + m, 1)
                            fn(y[:, 2 * g + m, :], ps[:, g, m * T:(m + 1) * T], ACT.Identity, bias=b)
                            ins = fn(sq[:, 2 * g + m, :], ps[:, g, m * T:(m + 1) * T], ACT.Square, bias=b)
                        ins.then_inc(s("squares"), 1)
                    split(i0 + g + RING)

            take_rows("post0", I_AO)
            root("post0", 4)

            def relu_squared(tag, g, c, n=None, step=0):
                act.wait_ge(*mlp_nth(tag, "hidden", up(c + 1, n, step)))
                r, r2 = y[:, 2 * g:2 * g + 2, :], sq[:, 2 * g:2 * g + 2, :]
                chain(fn(r, ps[:, g, :].rearrange("p (m t) -> p m t", m=2), ACT.Relu))
                act.sem_inc(s("mlp_free"), 1)
                dst = hid_hi[:, 2 * c:2 * c + 2, :] if n is None else hid_hi[:, bass.ds(n * (2 * step) + 2 * c, 2), :]
                chain(fn(r2, r, ACT.Square))
                fn(dst, r2, ACT.Copy).then_inc(s("mlp_hid_hi"), 1)

            def mlp(layer, tag, i0, prev):
                next_squares(tag + "_in", prev)
                root(tag + "_in", 5)
                high(tag + "_in", y, uhi, mod_scale(layer, 3, 0))
                slots, turns, rest, body = mlp_plan(layer)
                act.drain().then_inc(s("mlp_free"), slots)
                with act.Fori(0, turns) as n:
                    chain.enter(n, 2 * slots)
                    for i, g, q in body:
                        if g is not None:
                            product(i, n, len(body))
                            relu_squared(tag, g, g, n, slots)
                        split(i + RING, n, len(body))
                chain.leave(turns)
                for r in range(rest):
                    i = i0 + len(body) * turns + r
                    product(i)
                    relu_squared(tag, r, slots * turns + r)
                    split(i + RING)
                act.drain().then_inc(s("mlp_yfree"), 2)
                act.wait_ge(*mlp_nth(tag, "hidden", slots + 16))
                for i, g, q in items(*out_span(layer)):
                    if g is None:
                        split(i + RING)
                        continue
                    m0, kg = divmod(g, 4)
                    product(i)
                    if kg == 3:
                        src = ps[:, 2 * (m0 % 2):2 * (m0 % 2) + 2, 0:T]
                        fn(y[:, 2 * m0:2 * m0 + 2, :], src, ACT.Copy)
                        fn(sq[:, 2 * m0:2 * m0 + 2, :], src, ACT.Square).then_inc(s("squares"), 1)
                        act.drain().then_inc(s("mlp_yfree"), 1)
                    split(i + RING)
                root(tag, 4)

            mlp(0, "mlp0", I_MLP0, "post0")

            def store_spec(half, kind):
                act.wait_ge(s("filter_spec"), 2 * half + kind + 1)
                fn(spec[:, 2 * kind:2 * kind + 2, half * 512:half * 512 + 512],
                   ps[:, SPEC_BANK[half, kind]:SPEC_BANK[half, kind] + 2, :], ACT.Copy).then_inc(s("spec_stored"), 1)

            def turned(j):
                act.wait_ge(s("v_turned"), j + 1)
                fn(vtok[:, :, 2 * j * P:(2 * j + 2) * P].rearrange("p t (m c) -> p m t c", m=2),
                   ps[:, 2 + j % 2, :].rearrange("p (m t c) -> p m t c", m=2, t=TT), ACT.Copy).then_inc(s("vtok_stored"), 1)

            next_squares("hy_in", "mlp0")
            root("hy_in", 5)
            high("hy_in", y, uhi, mod_scale(1, 0, 0))
            act.wait_ge(*nth("hy_in", "lo", 4))
            act.dma_start(y[:].rearrange("p a c -> p (a c)"), A["decay"].rearrange("p t c -> p (t c)")).then_inc(s("decay_loaded"), 16)
            for g in range(12):
                product(I_HY + g)
                if g == 0:
                    act.wait_ge(s("zpad_clear"), 1)
                if g >= 2:
                    act.wait_ge(s("hy_conved"), g - 1)
                first = (16, 8, 0)[g // 4] + 2 * (g % 4)
                for m in range(2):
                    ins = fn(zpad[:, g % 2, m, 1:T + 1], ps[:, g % 2, m * T:(m + 1) * T], ACT.Identity, bias=pcol("hy_b_in", first + m, 1))
                ins.then_inc(s("hy_drained"), 1)
                split(I_HY + g + RING)
                if g in (5, 6):
                    store_spec(0, g - 5)
                if g in (9, 10):
                    store_spec(1, g - 9)
                if g in (8, 10):
                    turned(g - 8)
                    turned(g - 7)
            for half in range(2):
                a = slice(4 * half, 4 * half + 4)
                act.wait_ge(*nth("hy", "normed", half + 1))
                fn(uhi[:, a, :], hv[:, a, :], ACT.Copy).then_inc(s("hi"), 1)
            take_rows("post1", I_HO, "hy_b_out")
            root("post1", 4)
            mlp(1, "mlp1", I_MLP1, "post1")

            def halves(m):
                return m.rearrange("p (m t) -> p m t", m=2)

            def head(u):
                return u // 4, (u // 2) % 2, u % 2

            def part(name, b, src):
                act.wait_ge(s(name + "_ready"), 1)
                fn(yhi[:, b:b + MT, :], src, ACT.Copy).then_inc(s(name + "_hi"), 1)

            next_squares("mix_in", "mlp1")
            root("mix_in", 5)
            high("mix_in", y, uhi)
            act.wait_ge(s("lam_abs"), 1)
            fn(lru[:, 1, :], lru[:, 0, :], ACT.Exp, scale=-1.0).then_inc(s("lam_exp"), 1)
            for g in range(16):
                if g:
                    product(I_PROJ + g)
                src = ps[:, g % 4, :]
                a = slice(2 * (g % 2), 2 * (g % 2) + 2)
                if g == 0:
                    act.wait_ge(s("blocks_ready"), 1)
                    act.sem_inc(s("proj_drained"), 1)
                elif g == 1:
                    fn(ksw[:], halves(src), ACT.Copy).then_inc(s("proj_drained"), 1)
                elif g in (2, 3):
                    fn(qn[:, a, :], halves(src), ACT.Copy).then_inc(s("proj_drained"), 1)
                elif g == 4:
                    fn(vsw[:], halves(src), ACT.Copy).then_inc(s("proj_drained"), 1)
                elif g == 5:
                    fn(gates[:], halves(src)[:, :, 0:24], ACT.Tanh, scale=0.5).then_inc(s("proj_drained"), 1)
                elif g in (6, 7):
                    fn(rec[:, a, 3:3 + T], halves(src), ACT.Copy).then_inc(s("proj_drained"), 1)
                elif g in (8, 9):
                    fn(gate[:, a, :], halves(src), ACT.Gelu_apprx_tanh).then_inc(s("proj_drained"), 1)
                elif g in (10, 11):
                    fn(xd[:, a, 16:16 + T], halves(src), ACT.Copy).then_inc(s("proj_drained"), 1)
                elif g in (12, 13):
                    fn(vg[:, :, (g - 12) * 256:(g - 12) * 256 + 256], halves(src), ACT.Gelu_apprx_tanh).then_inc(s("proj_drained"), 1)
                else:
                    fn(ug[:, a, :], halves(src), ACT.Gelu_apprx_tanh).then_inc(s("proj_drained"), 1)
                split(I_PROJ + g + RING)
                if g == 3:
                    act.wait_ge(s("cmp_hidden"), 1)
                    fn(hidc[:, :, 0:NCMP], ps[:, 4, 0:32].rearrange("p (c n) -> p c n", c=2)[:, :, 0:NCMP], ACT.Gelu_apprx_tanh)\
                        .then_inc(s("cmp_gelu"), 1)
                if g == 5:
                    act.wait_ge(s("cmp_out"), 1)
                    fn(kc[:, 0:NCMP], ps[:, 5, 0:NCMP], ACT.Copy)
                    fn(vc[0:NCMP, :].rearrange("p (g d) -> p g d", g=2), ps[0:NCMP, 6:8, 0:HD], ACT.Copy).then_inc(s("cmp_stored"), 1)
            act.wait_ge(s("proj_drained"), 16)
            for n in range(TT):
                ins = fn(sq[:, 4 + 2 * n:6 + 2 * n, :].rearrange("p a c -> p (a c)"), vg[:, n, :], ACT.Square, accum_out=sm[:, n:n + 1])
            chain(ins)
            fn(sm[:, 2:4], sm[:, 0:2], ACT.Sqrt, bias=eps, scale=1.0 / MIX).then_inc(s("v_std"), 1)

            def beside(t):
                if t == 0:
                    act.wait_ge(s("pool_mapped"), 1)
                    for g in range(MT):
                        ins = fn(yhi[:, slot_of[3] + g, :], ps[:, 4 + g // 2, (g % 2) * T:(g % 2 + 1) * T], ACT.Copy, scale=pcol("pool_scale", g, 1))
                    ins.then_inc(s("pool_hi"), 1)
                if t == 2:
                    part("gm", slot_of[0], y[:, 0:MT, :])
                    act.wait_ge(s("rec_gates"), 1)
                    for w in range(2):
                        for m in range(MT):
                            ins = fn(mixb[:, 4 * w + m, :], ps[:, 2 + 2 * w + m // 2, (m % 2) * T:(m % 2 + 1) * T], ACT.Tanh, scale=0.5,
                                     bias=lru[:, 8 + w, m:m + 1])
                        ins.then_inc(s("rec_tanh"), 1)
                if t == 3:
                    act.wait_ge(s("rec_rate"), 1)
                    fn(rec[:, :, 0:T], mixb[:, 0:4, :], ACT.Tanh).then_inc(s("rate_tanh"), 1)
                    act.wait_ge(s("rate_tanh"), 1)
                    fn(mixb[:, 0:4, :], mixb[:, 0:4, :], ACT.Exp, scale=-1.0).then_inc(s("decay_ready"), 1)
                if t == 4:
                    act.wait_ge(s("rec_power"), 1)
                    fn(rec[:, :, 0:T], rec[:, :, 0:T], ACT.Sqrt).then_inc(s("rec_root"), 1)
                if t == 5:
                    part("lru", slot_of[1], rec[:, :, 0:T])
                if t == 6:
                    act.wait_ge(s("cmp_shifted"), 1)
                    fn(cmp_p, cmp_p, ACT.Exp, scale=SCALE).then_inc(s("cmp_exp"), 1)
                if t == 8:
                    act.wait_ge(s("cmp_turned"), 1)
                    fn(cmp_t, ps[0:NCMP, 0:4, :].rearrange("p b (u q) -> p (b u) q", u=4), ACT.Copy).then_inc(s("cmp_t_ready"), 1)

            def attend(u):
                if u < 16:
                    j, g, qt = head(u)
                    act.wait_ge(s("nsa_max"), u + 1)
                    if u >= 2:
                        act.wait_ge(s("nsa_turned"), u - 1)
                    for b in range(2):
                        w = 4 * (u % 2) + b
                        ins = fn(nsa_e[:, u % 2, b, 0:(qt + 1) * P], ps[:, u % 2, b * T:b * T + (qt + 1) * P], ACT.Exp, scale=SCALE,
                                 bias=sm[:, 8 + w:9 + w], accum_out=sm[:, 16 + w:17 + w])
                    ins.then_inc(s("nsa_exps"), 1)
                if 2 <= u <= 17:
                    v = u - 2
                    n = 2 * (v % 2 + 1)
                    act.wait_ge(s("nsa_turned"), v + 1)
                    if v >= 2:
                        act.wait_ge(s("nsa_out"), v - 1)
                    fn(nsa_t[:, 2 * (v % 2):2 * (v % 2) + n // 2, :].rearrange("p a c -> p (a c)"), ps[:, 2 + v % 2, 0:n * P], ACT.Copy)\
                        .then_inc(s("nsa_copied"), 1)
                if u >= 7 and (u - 3) % 4 == 0 or u == 19:
                    j = (u - 3) // 4 - 1
                    act.wait_ge(s("nsa_out"), 4 * j + 4)
                    fn(yhi[:, slot_of[2] + j, :], ps[:, 4 + j % 2, 0:T], ACT.Copy).then_inc(s("nsa_out_hi"), 1)

            for t in range(24):
                n, g = divmod(t, 6)
                i = I_BR + t
                if t in MID:
                    attend(MID[t])
                product(i)
                if g < 4:
                    if n:
                        act.wait_ge(s("gated_free"), 2 * n - 1 + g // 2)
                    fn(gated[:, 2 * g:2 * g + 2, :], halves(ps[:, 6 + g % 2, :]), ACT.Tanh, scale=0.5).then_inc(s("mg_tanh"), 1)
                    act.wait_ge(s("mg_tanh"), 4 * n + g + 1)
                    act.sem_inc(s("mg_free"), 1)
                if t in END:
                    attend(END[t])
                split(i + RING)
                beside(t)
            high("merged", y, uhi)
            for g in range(4):
                product(I_WO + g)
                split(I_WO + g + RING)

            next_squares("moe_in", "mixed")
            root("moe_in", 5)
            act.wait_ge(s("router_loaded"), 48)
            fn(wrhi[:], wr[:], ACT.Copy).then_inc(s("router_hi"), 1)
            high("moe_in", y, uhi)
            act.wait_ge(s("group_shifted"), 1)
            fn(ro[:, 2], ro[:, 1], ACT.Exp).then_inc(s("group_exp"), 1)
            act.wait_ge(s("top_gap"), 1)
            fn(ro[:, 12, :, 0:1], ro[:, 11, :, 0:1], ACT.Exp).then_inc(s("top_exp"), 1)

            def silu(i, j, n=None):
                product(i, n, 6)
                if n is not None:
                    act.wait_ge(s("moe_gated"), n * 2 + (j + 1))
                fn(sg[:, 2 * j:2 * j + 2, :], halves(ps[:, j, :]), ACT.Silu).then_inc(s("moe_silu"), 1)
                split(i + RING, n, 6)

            def expert_high(j, n=None):
                act.wait_ge(s("moe_weighted"), j + 1 if n is None else n * 2 + (j + 3))
                fn(ehi[:, 2 * j:2 * j + 2, :], hmid[:, 2 * j:2 * j + 2, :], ACT.Copy).then_inc(s("moe_hi"), 1)

            for j in range(2):
                silu(I_MOE + j, j)
            for j in range(2):
                split(I_MOE + 2 + j + RING)
            act.wait_ge(s("combine_turned"), 1)
            fn(cbt[0:EXPERTS, :], ps[0:EXPERTS, 5, 0:T], ACT.Copy).then_inc(s("combine_copied"), 1)
            for e in range(EXPERTS // 2):
                act.wait_ge(s("comb_spread"), e + 1)
                fn(comb[:, 2 * e:2 * e + 2, :], halves(ps[:, 4 + e % 4, :]), ACT.Copy).then_inc(s("comb_stored"), 1)
            for j in range(2):
                expert_high(j)
            with act.Fori(0, EXPERTS - 1) as n:
                i = I_MOE + 4
                for j in range(2):
                    silu(i + j, j, n)
                for j in range(2):
                    product(i + 2 + j, n, 6)
                    split(i + 2 + j + RING, n, 6)
                for j in range(2):
                    product(i + 4 + j, n, 6)
                    split(i + 4 + j + RING, n, 6)
                for j in range(2):
                    expert_high(j, n)
            for j in range(2):
                product(N_CHUNKS - 2 + j)
            next_squares("final", "moe")
            root("final", 0)

        @block.vector
        def _(dve):
            tt, ts, stt = nc.vector.tensor_tensor, nc.vector.tensor_scalar, nc.vector.scalar_tensor_tensor
            chain = Chain(dve, "dve_chain")

            def split(i, n=None, step=0):
                if i >= n_chunks and n is None:
                    return
                sl = i % RING
                if i in MODS:
                    weigh(i, n, step)
                    return
                dve.wait_ge(s("hi_ready"), up(weights_up_to(i), n, weights_up_to(i + step) - weights_up_to(i)))
                tt(wlo[:, sl, :], raw[:, sl, :], f32(whi[:, sl, :]), ALU.subtract).then_inc(s("lo_ready"), 1)

            def weigh(i, n, step):
                sl = i % RING
                dve.wait_ge(s(f"raw_loaded{sl}"), up(16 * (i // RING + 1), n, 16 * step // RING))
                if i >= RING:
                    dve.wait_ge(s("chunk_used"), up(i - RING + 1, n, step))
                acc = macc[:, sl, :]
                for k in range(KT):
                    w, c = raw[:, sl, k * 256:(k + 1) * 256], csil[:, k, 0:1]
                    ins = ts(acc, w, c, None, ALU.mult) if k == 0 else stt(acc, w, c, acc, ALU.mult, ALU.add)
                    if k < KT - 1:
                        chain(ins)
                ins.then_inc(s("lo_ready"), 1)

            def modulation(i, q, n=None, step=0, turn=0):
                dve.wait_ge(s("chunk_used"), up(i + 1, n, step))
                t0 = START_TILES + 2 * q
                dst = slice(t0, t0 + 2) if n is None else bass.ds(n * (2 * turn) + t0, 2)
                b0 = PCOL["b_mod"][0]
                bias = par[:, b0 + t0:b0 + t0 + 2] if n is None else par[:, bass.ds(n * (2 * turn) + (b0 + t0), 2)]
                tt(modv[:, dst, 0:1].rearrange("p a b -> p (a b)"), ps[:, 7, 0:2], bias, ALU.add).then_inc(s("mod_drained"), 1)

            def modulated(i):
                dve.wait_ge(s("mod_drained"), mods_before(i) + 1)

            def scale_of(slot, gain, layer, part, who=0):
                chain(stt(coef[:, slot, :], mod_scale(layer, part, who), 1.0, gain, ALU.add, ALU.mult))

            def gate_of(slot, gain, layer, part):
                chain(tt(coef[:, slot, :], mod_scale(layer, part, 0), gain, ALU.mult))

            def low(tag, src, hi, lo, shift=None):
                for c, part in cuts(tag, "lo"):
                    dve.wait_ge(*nth(tag, "hi", c + 1))
                    if shift is None:
                        ins = tt(lo[:, part, :], src[:, part, :], f32(hi[:, part, :]), ALU.subtract)
                    else:
                        for k in range(part.start, part.stop):
                            ins = stt(lo[:, k, :], src[:, k, :], shift[:, k:k + 1], f32(hi[:, k, :]), ALU.add, ALU.subtract)
                    ins.then_inc(s("lo"), 1)

            def prenorm(tag, src, dst, gain):
                if tag != "x":
                    dve.wait_ge(*nth(tag, "std", 1))
                    chain(nc.vector.reciprocal(rstd[:], std[:]))
                for c, part in cuts(tag, "normed"):
                    for k in range(part.start, part.stop):
                        ins = stt(dst[:, k, :], src[:, k, :], gain[:, k:k + 1], rstd[:], ALU.mult, ALU.mult)
                    ins.then_inc(s("normed"), 1)

            def postnorm(tag, slot):
                dve.wait_ge(*nth(tag, "std", 1))
                chain(nc.vector.reciprocal(rstd[:], std[:]))
                marks = []

                def add(c, part):
                    dve.wait_ge(chain.sem, marks[c])
                    tt(h[:, part, :], h[:, part, :], y[:, part, :], ALU.add).then_inc(s("h"), 1)

                for c, part in cuts(tag, "h"):
                    for k in range(part.start, part.stop):
                        ins = stt(y[:, k, :], y[:, k, :], coef[:, slot, k:k + 1], rstd[:], ALU.mult, ALU.mult)
                    marks.append(chain.tick(ins))
                    if c:
                        add(*cuts(tag, "h")[c - 1])
                add(*cuts(tag, "h")[-1])

            dve.wait_ge(s("c_tanh"), 1)
            chain(stt(csil[:], csil[:], 1.0, cvec[:], ALU.add, ALU.mult))
            ts(csil[:], csil[:], 0.5, None, ALU.mult).then_inc(s("c_silu"), 1)
            lv = lamv.rearrange("p (a b d) -> p a b d", a=2, b=2)
            lp = rstd[:, 0:2 * HD].rearrange("p (a d) -> p a d", a=2)
            chain(tt(lp, lv[:, :, 0, :], lv[:, :, 1, :], ALU.mult))
            nc.vector.tensor_reduce(small[:, 22:24], lp, AX, ALU.add).then_inc(s("lam_sums"), 1)
            for j in range(4):
                dve.wait_ge(s(f"start_loaded{j}"), 16)
                marks = [None, None]
                for k in range(KT):
                    for w in range(2):
                        acc, m, c = start_acc[:, j, w], mstart[:, 2 * j + 1, k * 256:(k + 1) * 256], csil[:, k, w:w + 1]
                        if k:
                            dve.wait_ge(chain.sem, marks[w])
                        ins = stt(acc, m, c, acc, ALU.mult, ALU.add) if k else ts(acc, m, c, None, ALU.mult)
                        marks[w] = chain.tick(ins)
                dve.wait_ge(chain.sem, marks[1])
                dve.sem_inc(s("start_weighted"), 1)
                if j == 2:
                    dve.wait_ge(*nth("x", "std", 1))
                    chain(nc.vector.reciprocal(rstd[:], std[:]))
            split(0)
            dve.wait_ge(s("mod_start"), 1)
            tt(modv[:, 0:START_TILES, :], ps[:, 7, 0:2 * START_TILES].rearrange("p (m w) -> p m w", m=START_TILES),
               over_cols(pcol("b_mod", 0, START_TILES), 2), ALU.add).then_inc(s("mod_drained"), 1)
            dve.wait_ge(s("mod_drained"), 1)
            scale_of(0, pcol("mix_pre", 0, 8), 0, 1, 0)
            scale_of(1, pcol("mix_pre", 0, 8), 0, 1, 1)
            dve.wait_ge(*nth("ctx", "sumsq", 1))
            prenorm("x", h, y, coef[:, 0])
            low("x", y, uhi, ulo, mod_scale(0, 0, 0))
            prenorm("ctx", ctx, ctx, coef[:, 1])
            low("ctx", ctx, ctx_hi, ctx_lo, mod_scale(0, 0, 1))
            for i in range(1, RING):
                split(i)
            cosb, sinb = over_tiles(ccol("cos"), 2), over_tiles(ccol("sin"), 2)

            def rope(r):
                dve.wait_ge(s("roped"), r + 1)
                tmp = sq[:, 2 * (r % 2):2 * (r % 2) + 2, :]
                x = kbuf[:, 2 * r:2 * r + 2, T:2 * T] if r < 4 else qbuf[:, 2 * (r - 4):2 * (r - 4) + 2, :]
                tt(tmp, ps[:, 4 + r % 2, :].rearrange("p (m t) -> p m t", m=2), sinb, ALU.mult).then_inc(s("rope_drained"), 1)
                chain(tt(x, x, cosb, ALU.mult))
                dve.wait_ge(s("rope_drained"), r + 1)
                tt(x, x, tmp, ALU.add).then_inc(s("roped_all"), 1)

            def filter_argument(j):
                c1 = 6.28125
                c2 = 2.0 * math.pi - c1
                magic = 1.5 * 2.0 ** 23
                top = math.pi * (1 - 2.0 ** -23)
                a, r = farg[0:HD, :], frnd[0:HD, :]
                dve.wait_ge(s("filter_layer"), j + 1)
                if j:
                    dve.wait_ge(s("filter_sin"), j)
                chain(ts(a, ps[0:HD, 6, 0:T], fpar[0:HD, j:j + 1], fpar[0:HD, 3:4], ALU.add, ALU.mult))
                chain(ts(r, a, 1.0 / (2.0 * math.pi), magic, ALU.mult, ALU.add))
                chain(ts(r, r, magic, None, ALU.subtract))
                chain(stt(a, r, -c1, a, ALU.mult, ALU.add))
                chain(stt(a, r, -c2, a, ALU.mult, ALU.add))
                ts(a, a, top, -top, ALU.min, ALU.max).then_inc(s("filter_arg"), 1)

            for i, g, q in items(I_QKV, I_ATT):
                split(i + RING)
                if g is None:
                    modulation(i, q)
                    continue
                if 1 <= g <= 8:
                    rope(g - 1)
                if 7 <= g <= 9:
                    filter_argument(g - 7)

            def max_of(u):
                dve.wait_ge(s("scores"), u + 1)
                w = 4 * (u % 2)
                chain(nc.vector.tensor_reduce(small[:, w + 2:w + 4], ps[:, 2 * (u % 2):2 * (u % 2) + 2, :], AX, ALU.max))
                ts(small[:, w:w + 2], small[:, w + 2:w + 4], -SCALE, None, ALU.mult).then_inc(s("max_ready"), 1)

            def combine(u):
                dve.wait_ge(s("exps"), u + 1)
                w = 8 + 4 * (u % 2)
                r = small[:, w + 2:w + 4]
                e0, e1 = ebuf[:, u % 2, 0, :], ebuf[:, u % 2, 1, :]
                chain(nc.vector.reciprocal(r, small[:, w:w + 2]))
                a = chain.tick(ts(e0, e0, r[:, 0:1], None, ALU.mult))
                b = chain.tick(ts(e1, e1, r[:, 1:2], small[:, 26:27], ALU.mult, ALU.mult))
                dve.wait_ge(chain.sem, b)
                tt(e0, e0, e1, ALU.add).then_inc(s("att_ready"), 1)

            dve.wait_ge(s("lam_exps"), 1)
            chain(tt(small[:, 26:27], small[:, 25:26], small[:, 24:25], ALU.subtract))
            chain(ts(small[:, 26:27], small[:, 26:27], -LAM_INIT, None, ALU.add))
            chain(ts(small[:, 27:28], pcol("subln"), 1.0 - LAM_INIT, None, ALU.mult))
            for u in range(2 * HEADS + 1):
                if u < 2 * HEADS:
                    max_of(u)
                if u:
                    combine(u - 1)
                if u % 2 == 0 and u < 2 * HEADS:
                    split(I_ATT + u // 2 + RING)
                    modulation(I_ATT + u // 2, MODS.index(I_ATT + u // 2))
            modulated(I_AO)
            gate_of(2, pcol("mix_post", 0, 8), 0, 2)
            scale_of(3, pcol("mlp_pre", 0, 8), 0, 4)
            for c in range(4):
                a = slice(2 * c, 2 * c + 2)
                dve.wait_ge(s("o_std"), c + 1)
                chain(nc.vector.reciprocal(y[:, a, :], y[:, a, :]))
                stt(obuf[:, a, :], obuf[:, a, :], small[:, 27:28], y[:, a, :], ALU.mult, ALU.mult).then_inc(s("o_normed"), 1)
            for c in range(4):
                a = slice(2 * c, 2 * c + 2)
                dve.wait_ge(s("o_hi"), c + 1)
                tt(ulo[:, a, :], obuf[:, a, :], f32(uhi[:, a, :]), ALU.subtract).then_inc(s("o_lo"), 1)
            for g in range(4):
                split(I_AO + g + RING)
            postnorm("post0", 2)

            def low_squared(tag, g, c, n=None, step=0):
                dve.wait_ge(*mlp_nth(tag, "hid_hi", up(c + 1, n, step)))
                r2 = sq[:, 2 * g:2 * g + 2, :]
                a = slice(2 * c, 2 * c + 2) if n is None else bass.ds(n * (2 * step) + 2 * c, 2)
                tt(hid_lo[:, a, :], r2, f32(hid_hi[:, a, :]), ALU.subtract).then_inc(s("mlp_hidden"), 1)

            def mlp(layer, tag, i0):
                prenorm(tag + "_in", h, y, coef[:, 3])
                low(tag + "_in", y, uhi, ulo, mod_scale(layer, 3, 0))
                slots, turns, rest, body = mlp_plan(layer)
                dve.drain().then_inc(s("mlp_hidden"), slots)
                with dve.Fori(0, turns) as n:
                    mods = len(body) - slots
                    chain.enter(n, mods * (KT - 1))
                    for i, g, q in body:
                        if g is not None:
                            low_squared(tag, g, g, n, slots)
                        split(i + RING, n, len(body))
                        if g is None:
                            modulation(i, q, n, len(body), mods)
                chain.leave(turns)
                for r in range(rest):
                    low_squared(tag, r, slots * turns + r)
                    split(i0 + len(body) * turns + r + RING)
                for i, g, q in items(*out_span(layer)):
                    split(i + RING)
                    if g is None:
                        modulation(i, q)
                modulated(out_span(layer)[1])
                gate_of(4, pcol("mlp_post", 8 * layer, 8), layer, 5)
                postnorm(tag, 4)

            mlp(0, "mlp0", I_MLP0)

            def short_conv(g):
                first = (16, 8, 0)[g // 4] + 2 * (g % 4)
                a = slice(2 * (g % 4), 2 * (g % 4) + 2)
                dst = (hv[:, a, :], hx1[:], hx0[:, a, :])[g // 4]
                dve.wait_ge(s("hy_drained"), g + 1)
                if 5 <= g <= 7:
                    dve.wait_ge(s("v_ready"), g - 4)
                for m in range(2):
                    ins = ts(dst[:, m, :], zpad[:, g % 2, m, 0:T], pcol("hy_w_short", first + m, 1), pcol("hy_b_short", first + m, 1),
                             ALU.mult, ALU.add)
                chain(ins)
                for tap in (1, 2):
                    for m in range(2):
                        ins = stt(dst[:, m, :], zpad[:, g % 2, m, tap:T + tap], pcol("hy_w_short", 24 * tap + first + m, 1), dst[:, m, :],
                                  ALU.mult, ALU.add)
                    if tap == 1:
                        chain(ins)
                ins.then_inc(s("hy_conved"), 1)
                if g // 4 == 1:
                    dve.wait_ge(s("hy_conved"), g + 1)
                    tt(hv[:, a, :], hv[:, a, :], hx1[:], ALU.mult).then_inc(s("v_ready"), 1)

            def taps_of(half, t0):
                a = slice(half * 512, half * 512 + 512)
                dve.wait_ge(s("filter_taps"), 2 * half + t0 + 1)
                if half == 0 and t0 == 0:
                    dve.wait_ge(s("decay_loaded"), 16)
                if half and t0 == 0:
                    dve.wait_ge(s("filter_spec"), 2)
                b = TAPS_BANK[half, t0]
                tt(tapf[:, t0, :], ps[:, b, :], decay[:, t0, a], ALU.mult)
                if t0 == 0:
                    chain(stt(tapb[:, t0, :], ps[:, b + 1, :], ccol("notfirst"), decay[:, t0, a], ALU.mult, ALU.mult))
                else:
                    chain(tt(tapb[:, t0, :], ps[:, b + 1, :], decay[:, t0, a], ALU.mult))
                chain(tt(taps[:, t0, :], tapf[:, t0, :], tapb[:, t0, :], ALU.add))
                tt(tapf[:, t0, :], tapf[:, t0, :], tapb[:, t0, :], ALU.subtract).then_inc(s("taps_ready"), 1)

            scale_of(5, pcol("mix_pre", 8, 8), 1, 1)
            prenorm("hy_in", h, y, coef[:, 5])
            low("hy_in", y, uhi, ulo, mod_scale(1, 0, 0))
            nc.vector.memset(zpad[:], 0.0).then_inc(s("zpad_clear"), 1)
            for g in range(12):
                split(I_HY + g + RING)
                short_conv(g)
                if g in (2, 3):
                    taps_of(0, g - 2)
                if g in (6, 7):
                    taps_of(1, g - 6)
            gate_of(6, pcol("mix_post", 8, 8), 1, 2)
            scale_of(3, pcol("mlp_pre", 8, 8), 1, 4)
            dve.wait_ge(s("spec_stored"), 4)
            for half in range(2):
                a = slice(half * 512, half * 512 + 512)
                dve.wait_ge(s("vspec"), half + 1)
                c, d = CONV_BANKS[half][0], CONV_BANKS[half][2]
                vc, vs, hc, hs = ps[:, c:c + 2, :], ps[:, d:d + 2, :], spec[:, 0:2, a], spec[:, 2:4, a]
                tt(prod[:, 0], vc, hc, ALU.mult)
                chain(tt(prod[:, 1], vs, hs, ALU.mult))
                chain(tt(yspec[:, half, 0:2, :], prod[:, 0], prod[:, 1], ALU.subtract))
                tt(prod[:, 0], vc, hs, ALU.mult)
                chain(tt(prod[:, 1], vs, hc, ALU.mult))
                chain(tt(yspec[:, half, 2:4, :], prod[:, 0], prod[:, 1], ALU.add))
                dve.sem_inc(s("yspec_ready"), 1)
            for half in range(2):
                for m in range(4):
                    k = 4 * half + m
                    dve.wait_ge(s("conv"), k + 1)
                    ins = stt(hv[:, k, :], hv[:, k, :], pcol("hy_bias", k, 1), ps[:, CONV_BANKS[half][m], 0:T], ALU.mult, ALU.add)
                    ins.then_inc(s("conv_taken"), 1)
                dve.wait_ge(s("conv_taken"), 4 * half + 4)
                a = slice(4 * half, 4 * half + 4)
                tt(hv[:, a, :], hv[:, a, :], hx0[:, a, :], ALU.mult).then_inc(s("normed"), 1)
            low("hy", hv, uhi, ulo)
            for g in range(4):
                split(I_HO + g + RING)
            postnorm("post1", 6)
            mlp(1, "mlp1", I_MLP1)

            def halves(m):
                return m.rearrange("p (m t) -> p m t", m=2)

            def head(u):
                return u // 4, (u // 2) % 2, u % 2

            def low_part(name, b, src):
                dve.wait_ge(s(name + "_hi"), 1)
                tt(ylo[:, b:b + MT, :], src, f32(yhi[:, b:b + MT, :]), ALU.subtract).then_inc(s(name + "_lo"), 1)

            def softplus_of_minus_lambda():
                lam, e, z, z2, acc = pcol("lam"), lru[:, 1, :], lru[:, 2, :], lru[:, 4, :], lru[:, 3, :]
                chain(ts(lru[:, 5, :], lam, -1.0, None, ALU.mult))
                tt(lru[:, 0, :], lam, lru[:, 5, :], ALU.max).then_inc(s("lam_abs"), 1)
                dve.wait_ge(s("lam_exp"), 1)
                chain(ts(z, e, 2.0, None, ALU.add))
                chain(nc.vector.reciprocal(z, z))
                chain(tt(z, z, e, ALU.mult))
                chain(tt(z2, z, z, ALU.mult))
                terms = 9
                chain(ts(acc, z2, 1.0 / (2 * terms + 1), 1.0 / (2 * terms - 1), ALU.mult, ALU.add))
                for k in range(terms - 2, -1, -1):
                    chain(tt(acc, acc, z2, ALU.mult))
                    chain(ts(acc, acc, 1.0 / (2 * k + 1), None, ALU.add))
                chain(stt(acc, acc, 2.0, z, ALU.mult, ALU.mult))
                chain(stt(acc, lru[:, 5, :], 0.0, acc, ALU.max, ALU.add))
                chain(ts(acc, acc, 4.0, None, ALU.mult))
                for w, name in enumerate(("ba", "bx")):
                    chain(ts(lru[:, 8 + w, :], pcol(name), 0.5, None, ALU.mult))

            def blocks_of(c):
                src = ps[:, 0, c * T:(c + 1) * T]
                for half in range(2):
                    a = slice(16 * half, 16 * half + 16)
                    ins = tt(blocks[:, c, a, :].rearrange("p l n -> p n l"),
                             src[:, 16 * half:16 * half + 240].rearrange("p (n l) -> p n l", l=16),
                             over_tiles(cpe[:, c, a], NCMP), ALU.add)
                return ins

            def trailing_sums():
                sa, sb, x = y[:, 0:4, :], y[:, 4:8, :], xd[:, :, 16:16 + T]
                chain(tt(sa, x, xd[:, :, 15:15 + T], ALU.add))
                for g0, w, old, new in ((1, 2, sa, sb), (2, 4, sb, sa), (3, 8, sa, sb)):
                    tt(new[:, g0:4, w:], old[:, g0:4, w:], old[:, g0:4, :-w], ALU.add)
                    chain(nc.vector.tensor_copy(new[:, g0:4, 0:w], old[:, g0:4, 0:w]))
                for g, b in enumerate((sa, sb, sa, sb)):
                    ins = tt(b[:, g, :], b[:, g, :], bcol("recip")[:, g * T:(g + 1) * T], ALU.mult)
                chain(ins)
                for g, b in enumerate((sa, sb, sa, sb)):
                    ins = tt(x[:, g, :], b[:, g, :], x[:, g, :], ALU.subtract)
                ins.then_inc(s("pooled"), 1)
                dve.wait_ge(s("pooled"), 1)

            prenorm("mix_in", h, y, pcol("norm1"))
            low("mix_in", y, uhi, ulo)
            softplus_of_minus_lambda()
            dve.wait_ge(s("mixer_loaded"), 16 * 5)
            dve.wait_ge(s("chunk_used"), I_PROJ + 1)
            blocks_of(0)
            blocks_of(1).then_inc(s("blocks_ready"), 1)
            chain(tt(gmw[:], gmw[:], over_tiles(tril, MT), ALU.mult))
            for g in range(16):
                split(I_PROJ + g + RING)
                if g == 6:
                    dve.wait_ge(s("proj_drained"), 6)
                    chain(ts(gates[:], gates[:], 0.5, 0.5, ALU.mult, ALU.add))
                if g == 8:
                    dve.wait_ge(s("proj_drained"), 8)
                    dve.wait_ge(s("lru_clear"), 1)
                    dve.wait_ge(s("cmp_hidden"), 1)
                    for m in range(MT):
                        ins = ts(sq[:, m, :], rec[:, m, 0:T], pcol("conv_w", m, 1), pcol("conv_b", m, 1), ALU.mult, ALU.add)
                    chain(ins)
                if 9 <= g <= 11:
                    for m in range(MT):
                        ins = stt(sq[:, m, :], rec[:, m, g - 8:g - 8 + T], pcol("conv_w", 4 * (g - 8) + m, 1), sq[:, m, :], ALU.mult, ALU.add)
                    if g < 11:
                        chain(ins)
                    else:
                        ins.then_inc(s("rec_conved"), 1)
                if g == 12:
                    dve.wait_ge(s("proj_drained"), 12)
                    trailing_sums()
            dve.wait_ge(s("v_std"), 1)
            chain(nc.vector.reciprocal(sm[:, 4:6], sm[:, 2:4]))
            for n in range(TT):
                ins = ts(vg[:, n, :], vg[:, n, :], sm[:, 4 + n:5 + n], None, ALU.mult)
            ins.then_inc(s("v_normed"), 1)
            flat = cmp_p.rearrange("p t h n -> p (t h) n")
            top, inv = sm[:, 24:40], sm[:, 40:56]
            rate, inp, pw = mixb[:, 0:4, :], mixb[:, 4:8, :], rec[:, :, 0:T]

            def beside(t):
                if t == 0:
                    dve.wait_ge(s("pool_hi"), 1)
                    for g in range(MT):
                        b = slot_of[3] + g
                        ins = stt(ylo[:, b, :], ps[:, 4 + g // 2, (g % 2) * T:(g % 2 + 1) * T], pcol("pool_scale", g, 1), f32(yhi[:, b, :]),
                                  ALU.mult, ALU.subtract)
                    ins.then_inc(s("pool_lo"), 1)
                if t == 1:
                    dve.wait_ge(s("gm_mixed"), 1)
                    for g in range(MT):
                        ins = stt(y[:, g, :].rearrange("p (n t) -> p n t", n=TT), halves(ps[:, g // 2, (g % 2) * T:(g % 2 + 1) * T]),
                                  pcol("gm_norm", g, 1), over_tiles(gmb[:, g, :], TT), ALU.mult, ALU.add)
                    chain(ins)
                    tt(y[:, 0:MT, :], y[:, 0:MT, :], ug, ALU.mult).then_inc(s("gm_ready"), 1)
                    dve.wait_ge(s("cmp_hidden"), 1)
                if t == 2:
                    low_part("gm", slot_of[0], y[:, 0:MT, :])
                if t == 3:
                    dve.wait_ge(s("rec_tanh"), 1)
                    for m in range(MT):
                        ins = ts(rate[:, m, :], rate[:, m, :], 1.0, lru[:, 3, m:m + 1], ALU.add, ALU.mult)
                    ins.then_inc(s("rec_rate"), 1)
                    dve.wait_ge(s("rec_tanh"), 2)
                    chain(stt(inp, inp, 1.0, sq[:, 0:4, :], ALU.add, ALU.mult))
                if t == 4:
                    dve.wait_ge(s("decay_ready"), 1)
                    chain(tt(sq[:, 4:8, :], rate, rate, ALU.mult))
                    stt(pw, sq[:, 4:8, :], 1.0, pw, ALU.add, ALU.mult).then_inc(s("rec_power"), 1)
                if t == 5:
                    dve.wait_ge(s("rec_root"), 1)
                    chain(stt(inp, inp, 0.5, pw, ALU.mult, ALU.mult))
                    for m in range(MT):
                        ins = nc.vector.tensor_tensor_scan(sq[:, m, :], rate[:, m, :], inp[:, m, :], 0.0, ALU.mult, ALU.add)
                    chain(ins)
                    tt(pw, sq[:, 0:4, :], gate[:], ALU.mult).then_inc(s("lru_ready"), 1)
                if t == 6:
                    low_part("lru", slot_of[1], pw)
                    dve.wait_ge(s("lru_lo"), 1)
                    dve.wait_ge(s("cmp_scores"), 1)
                    for qt in range(2):
                        for g in range(2):
                            ins = tt(cmp_p[:, qt, 4 * g:4 * g + 4], ps[:, 2 * qt + g, 0:64].rearrange("p (h n) -> p h n", n=16)[:, :, 0:NCMP],
                                     over_tiles(bcol("cmask")[:, qt * NCMP:(qt + 1) * NCMP], 4), ALU.add)
                    chain(ins)
                    chain(nc.vector.tensor_reduce(top, flat, AX, ALU.max))
                    tt(flat, flat, over_cols(top, NCMP), ALU.subtract).then_inc(s("cmp_shifted"), 1)
                if t == 7:
                    dve.wait_ge(s("cmp_exp"), 1)
                    chain(nc.vector.tensor_reduce(top, flat, AX, ALU.add))
                    chain(nc.vector.reciprocal(inv, top))
                    for qt in range(2):
                        ins = stt(inv[:, 8 * qt:8 * qt + 8], inv[:, 8 * qt:8 * qt + 8], bcol("cvalid")[:, qt:qt + 1],
                                  gates[:, qt, :].rearrange("p (h b) -> p b h", b=3)[:, 0, :], ALU.mult, ALU.mult)
                    chain(ins)
                    tt(flat, flat, over_cols(inv, NCMP), ALU.mult).then_inc(s("cmp_weights"), 1)


            def nsa_max(u):
                j, g, qt = head(u)
                dve.wait_ge(s("nsa_scores"), u + 1)
                w = 8 + 4 * (u % 2)
                sc = ps[:, u % 2, :].rearrange("p (b k) -> p b k", b=2)
                diag = sc[:, :, qt * P:(qt + 1) * P]
                chain(tt(diag, diag, over_tiles(causal, 2), ALU.add))
                chain(nc.vector.tensor_reduce(sm[:, w + 2:w + 4], sc[:, :, 0:(qt + 1) * P], AX, ALU.max))
                ts(sm[:, w:w + 2], sm[:, w + 2:w + 4], -SCALE, None, ALU.mult).then_inc(s("nsa_max"), 1)

            def nsa_weights(u):
                j, g, qt = head(u)
                dve.wait_ge(s("nsa_exps"), u + 1)
                w = 16 + 4 * (u % 2)
                r = sm[:, w + 2:w + 4]
                hh = g * 4 + j
                chain(nc.vector.reciprocal(r, sm[:, w:w + 2]))
                chain(tt(r, r, gates[:, qt, 3 * hh + 1:3 * hh + 3], ALU.mult))
                for b in range(2):
                    e = nsa_e[:, u % 2, b, 0:(qt + 1) * P]
                    ins = ts(e, e, r[:, b:b + 1], None, ALU.mult)
                ins.then_inc(s("nsa_weights"), 1)

            def attend(u):
                if u == 0:
                    dve.wait_ge(s("cmp_turned"), 1)
                if u < 16:
                    nsa_max(u)
                if 1 <= u <= 16:
                    nsa_weights(u - 1)
                if u >= 7 and (u - 3) % 4 == 0 or u == 19:
                    j = (u - 3) // 4 - 1
                    b = slot_of[2] + j
                    dve.wait_ge(s("nsa_out_hi"), j + 1)
                    tt(ylo[:, b, :], ps[:, 4 + j % 2, 0:T], f32(yhi[:, b, :]), ALU.subtract).then_inc(s("nsa_out_lo"), 1)

            for t in range(24):
                n, g = divmod(t, 6)
                i = I_BR + t
                if t in MID:
                    attend(MID[t])
                if g >= 4:
                    a = slice(4 * (g - 4), 4 * (g - 4) + 4)
                    dve.wait_ge(s("mg_tanh"), 4 * n + 4)
                    dve.wait_ge(s("chunk_used"), i + 1)
                    src = ps[:, 6:8, :].rearrange("p b (m t) -> p (b m) t", m=2)
                    chain(stt(gated[:, a, :] if n else y[:, a, :], gated[:, a, :], 1.0, src, ALU.add, ALU.mult))
                    dve.sem_inc(s("br_free"), 1)
                    if n:
                        chain(tt(y[:, a, :], y[:, a, :], gated[:, a, :], ALU.add))
                    dve.sem_inc(s("gated_free"), 1)
                if t in END:
                    attend(END[t])
                if t:
                    split(i + RING - 1)
                beside(t)
            split(I_WO + RING - 1)
            for c in range(2):
                a = slice(4 * c, 4 * c + 4)
                ts(y[:, a, :], y[:, a, :], 0.5, None, ALU.mult).then_inc(s("normed"), 1)
            low("merged", y, uhi, ulo)
            for g in range(4):
                dve.wait_ge(s("chunk_used"), I_WO + g + 1)
                a = slice(2 * g, 2 * g + 2)
                ins = tt(h[:, a, :], h[:, a, :], halves(ps[:, g, :]), ALU.add)
                ins.then_inc(s("h"), 1)
                split(I_WO + g + RING)

            prenorm("moe_in", h, y, pcol("norm2"))
            dve.wait_ge(s("router_hi"), 1)
            tt(wrlo[:], wr[:], f32(wrhi[:]), ALU.subtract).then_inc(s("router_lo"), 1)
            low("moe_in", y, uhi, ulo)

            def row(k, n=4):
                return ro[:, k, :, 0:n]

            def wide(x, n=4):
                return x.to_broadcast([P, TT, n])

            def first_of(dst, src, top, tmp, tmp_top):
                chain(tt(row(tmp), src, wide(top), ALU.is_equal))
                chain(tt(row(tmp), row(tmp), order4[:].unsqueeze(1).to_broadcast([P, TT, 4]), ALU.mult))
                chain(nc.vector.tensor_reduce(row(tmp_top, 1), row(tmp), AX, ALU.max))
                chain(tt(dst, row(tmp), wide(row(tmp_top, 1)), ALU.is_equal))

            dve.wait_ge(s("router"), 1)
            chain(tt(lg[:], ps[:, 4, 0:64].rearrange("p (t c) -> p t c", t=2)[:, :, 0:20], rb[:].unsqueeze(1).to_broadcast([P, TT, 20]), ALU.add))
            grp = lg[:, :, 0:4]
            chain(nc.vector.tensor_reduce(row(0, 1), grp, AX, ALU.max))
            tt(row(1), grp, wide(row(0, 1)), ALU.subtract).then_inc(s("group_shifted"), 1)
            first_of(row(3), grp, row(0, 1), 4, 5)
            dve.wait_ge(s("group_exp"), 1)
            chain(nc.vector.tensor_reduce(row(6, 1), row(2), AX, ALU.add))
            chain(nc.vector.reciprocal(row(6, 1), row(6, 1)))
            for t0 in range(TT):
                prod4 = ro[:, 14 + 2 * t0:16 + 2 * t0].rearrange("p a b c -> p (a b c)").rearrange("p (g e) -> p g e", g=4)
                chain(tt(prod4, lg[:, t0, 4:20].rearrange("p (g e) -> p g e", g=4), over_cols(ro[:, 3, t0, :], 4), ALU.mult))
                chain(nc.vector.tensor_reduce(ro[:, 7, t0, :], prod4.rearrange("p g e -> p e g"), AX, ALU.add))
            chain(nc.vector.tensor_reduce(row(8, 1), row(7), AX, ALU.max))
            first_of(row(9), row(7), row(8, 1), 4, 5)
            chain(stt(row(7), row(9), MASKED, row(7), ALU.mult, ALU.add))
            chain(nc.vector.tensor_reduce(row(10, 1), row(7), AX, ALU.max))
            tt(row(11, 1), row(10, 1), row(8, 1), ALU.subtract).then_inc(s("top_gap"), 1)
            first_of(row(13), row(7), row(10, 1), 4, 5)
            dve.wait_ge(s("top_exp"), 1)
            chain(ts(row(18, 1), row(12, 1), 1.0, None, ALU.add))
            chain(nc.vector.reciprocal(row(18, 1), row(18, 1)))
            chain(tt(row(18, 1), row(18, 1), row(6, 1), ALU.mult))
            chain(tt(row(19, 1), row(18, 1), row(12, 1), ALU.mult))
            chain(tt(row(9), row(9), wide(row(18, 1)), ALU.mult))
            chain(tt(row(13), row(13), wide(row(19, 1)), ALU.mult))
            chain(tt(row(9), row(9), row(13), ALU.add))
            for t0 in range(TT):
                ins = tt(cb[:, t0, :].rearrange("p (g e) -> p g e", g=4), over_tiles(ro[:, 9, t0, :], 4), over_cols(ro[:, 3, t0, :], 4), ALU.mult)
            ins.then_inc(s("combine_ready"), 1)

            def weighted(i, j, n=None):
                dve.wait_ge(s("chunk_used"), up(i + 1, n, 6))
                dve.wait_ge(s("moe_silu"), j + 1 if n is None else n * 2 + (j + 3))
                a = slice(2 * j, 2 * j + 2)
                tt(hmid[:, a, :], sg[:, a, :], halves(ps[:, 2 + j, :]), ALU.mult).then_inc(s("moe_gated"), 1)
                dve.wait_ge(s("moe_gated"), j + 1 if n is None else n * 2 + (j + 3))
                c = comb[:, 0, :] if n is None else comb[:, bass.ds(n + 1, 1), :].rearrange("p a t -> p (a t)")
                tt(hmid[:, a, :], hmid[:, a, :], over_tiles(c, 2), ALU.mult).then_inc(s("moe_weighted"), 1)

            def expert_low(j, n=None):
                dve.wait_ge(s("moe_hi"), j + 1 if n is None else n * 2 + (j + 3))
                a = slice(2 * j, 2 * j + 2)
                tt(elo[:, a, :], hmid[:, a, :], f32(ehi[:, a, :]), ALU.subtract).then_inc(s("moe_hid"), 1)

            def add_rows(i, j, n=None, last=False):
                dve.wait_ge(s("chunk_used"), up(i + 1, n, 6))
                a = slice(4 * j, 4 * j + 4)
                tt(h[:, a, :], h[:, a, :], ps[:, 4 + 2 * j:6 + 2 * j, :].rearrange("p b (m t) -> p (b m) t", m=2), ALU.add)\
                    .then_inc(s("h" if last else "moe_free"), 1)

            for j in range(4):
                split(I_MOE + j + RING)
            dve.wait_ge(s("comb_stored"), EXPERTS // 2)
            for j in range(2):
                weighted(I_MOE + 2 + j, j)
            for j in range(2):
                expert_low(j)
            dve.drain().then_inc(s("moe_free"), 2)
            with dve.Fori(0, EXPERTS - 1) as n:
                i = I_MOE + 4
                for j in range(2):
                    split(i + j + RING, n, 6)
                for j in range(2):
                    add_rows(i + 2 + j, j, n)
                    split(i + 2 + j + RING, n, 6)
                for j in range(2):
                    weighted(i + 4 + j, j, n)
                    split(i + 4 + j + RING, n, 6)
                for j in range(2):
                    expert_low(j, n)
            dve.wait_ge(s("moe_free"), 2 * EXPERTS)
            for j in range(2):
                add_rows(N_CHUNKS - 2 + j, j, last=True)
            prenorm("final", h, y, pcol("final"))


SPARAMS = ["b_mod", "norm_mix_pre", "norm_mix_post", "norm_mlp_pre", "norm_mlp_post", "attn_subln", "hy_b_in",
           "hy_w_short", "hy_b_short", "hy_bias", "hy_b_out", "norm1_g_2", "gm_norm_g_2", "conv_w_2", "conv_b_2",
           "lru_ba_2", "lru_bx_2", "lru_lambda_2", "pool_scale_2", "norm2_g_2", "final_norm_g_2"]


def laid_out(x):
    ac = np.ascontiguousarray
    a = {k: np.asarray(v) for k, v in x.items()}
    weights = np.zeros((N_CHUNKS + 1, P, CW), np.float32)
    for i, (name, lead, r0, rows, cols) in enumerate(STREAM):
        m = a[name][lead]
        lo, n = cols[0], len(cols)
        m = m[r0:r0 + rows, lo:lo + n] if cols == tuple(range(lo, lo + n)) else m[r0:r0 + rows][:, list(cols)]
        if name == "w_branch_2" and lead[1] == 2:
            order = [g * 256 + j * 64 + d for j in range(4) for g in range(2) for d in range(64)]
            m = m[order]
        k = rows // P
        width = CW // k
        weights[i].reshape(P, k, width)[:, :, :n] = m.reshape(k, P, n).transpose(1, 0, 2)

    def fm(v):
        return ac(v.reshape(T, KT, P).transpose(2, 1, 0))

    params = ac(np.concatenate([a[n].reshape(-1, P) for n in SPARAMS]).T)
    assert params.shape == (P, NPAR)
    out = {
        "weights": weights, 
        "mod_start": ac(a["w_mod"][0][:, 0:START_TILES * P].reshape(KT, P, START_TILES // 2, 2 * P).transpose(1, 2, 0, 3).reshape(P, START_TILES // 2, CW)),
         "params": params, "x": fm(a["x"]), "ctx": fm(a["ctx"]),
        "cvec": ac(np.stack([a["c"].reshape(KT, P).T, a["c_ctx"].reshape(KT, P).T], axis=2)),
        "attn_lambda": ac(a["attn_lambda"].reshape(-1)),
        "hy_filt_w1": ac(a["hy_filt_w1"][0]), "hy_filt_w2": ac(a["hy_filt_w2"][0].transpose(1, 0, 2)),
        "hy_filt_w_out": ac(a["hy_filt_w_out"][0]),
        "fpar": ac(np.stack([a["hy_filt_b1"][0], a["hy_filt_b2"][0, 0], a["hy_filt_b2"][0, 1], a["hy_filt_freq"][0]], axis=1)),
        "cmp_w1": ac(a["cmp_w1_2"][0].reshape(2, 2, CMP_LEN, HD, HD).transpose(1, 3, 0, 2, 4).reshape(P, 2, CMP_LEN * HD)),
        "cmp_w2": ac(a["cmp_w2_2"][0].transpose(1, 2, 0, 3).reshape(P, 2, HD)),
        "cmp_pe": ac(np.concatenate([a["cmp_pe_2"][0].transpose(2, 0, 1)] * 2)),
        "gm_ws": ac(a["gm_ws_2"][0].transpose(2, 0, 1)), "gm_b": ac(a["gm_b_2"][0].reshape(-1)),
        "pool_w": ac(a["pool_w_2"][0].transpose(1, 0, 2)),
        "lru_wa": ac(a["lru_wa_2"][0].reshape(4, 2, HD, HD).transpose(1, 2, 0, 3)),
        "lru_wx": ac(a["lru_wx_2"][0].reshape(4, 2, HD, HD).transpose(1, 2, 0, 3)),
        "router_w": ac(np.concatenate([a["router_w_group_2"][0], a["router_w_expert_2"][0]], axis=1)
                       .reshape(KT, P, 20).transpose(1, 0, 2)),
        "router_b": ac(np.concatenate([a["router_b_group_2"][0], a["router_b_expert_2"][0]])),
        "order4": np.broadcast_to(np.arange(4, 0, -1, dtype=np.float32), (P, 4)).copy(),
        **shape_constants(),
    }
    return out


def kernel(**inputs):
    import concourse.bacc as bacc
    from concourse.bass_utils import run_bass_kernel_spmd

    nc = bacc.Bacc("TRN2", target_bir_lowering=False, num_devices=1)
    arrays = laid_out(inputs)
    aps = {n: nc.dram_tensor(n + "_in", v.shape, mybir.dt.from_np(v.dtype), kind="ExternalInput").ap()
           for n, v in arrays.items()}
    out = nc.dram_tensor("out_0", (P, KT, T), F32, kind="ExternalOutput").ap()
    program(nc, aps, out)
    r = run_bass_kernel_spmd(nc, [{n + "_in": v for n, v in arrays.items()}], core_ids=[0])
    got = r.results[0]["out_0"]
    return np.ascontiguousarray(got.transpose(2, 1, 0)).reshape(1, T, D)
```
